# Optimizing a Trainium2 kernel written in Bass

```python
import math
import jax
import jax.numpy as jnp
from jax import lax
import numpy as np

D_MODEL = 2048
BATCH = 1
SEQ = 256
DEPTH = 1

HEAD_DIM = 128
LRU_BLOCKS = 6
LRU_BD = 128
LRU_W = LRU_BLOCKS * LRU_BD
LRU_C = 8.0
CONV_W = 4
SWA_HEADS = 6
SWA_W = SWA_HEADS * HEAD_DIM
DILATED_PATTERNS = ((128, 1), (512, 4), (2048, 16))
SB_HEADS = 4
SB_W = SB_HEADS * HEAD_DIM
MIX_W = LRU_W + SWA_W + SB_W
IN_W = 2 * LRU_W + 3 * SWA_W + 3 * SB_W
Q_BLOCK = 128
REL_BUCKETS = 32
REL_MAX_DIST = 2048
PEER_HEADS = 8
PEER_NKEYS = 128
PEER_EXPERTS = PEER_NKEYS * PEER_NKEYS
PEER_DQ = 256
PEER_TOPK = 16
TOK_BLOCK = 128
NEG_INF = -1e30
EPS = 1e-6

kernel_name = "hybrid_lru_dilated_stickbreak_peer_block"

def rms_norm(x, g):
    xf = x.astype(jnp.float32)
    y = xf * lax.rsqrt(jnp.mean(xf * xf, axis=-1, keepdims=True) + EPS)
    return (y * g.astype(jnp.float32)).astype(x.dtype)

def t5_bucket(dist):
    dist = np.asarray(dist, np.int32)
    max_exact = REL_BUCKETS // 2
    large = max_exact + (np.log(np.maximum(dist, 1) / max_exact)
                         / np.log(REL_MAX_DIST / max_exact)
                         * (REL_BUCKETS - max_exact)).astype(np.int32)
    large = np.minimum(large, REL_BUCKETS - 1)
    return np.where(dist < max_exact, dist, large).astype(np.int32)

def causal_depthwise_conv(x, w, b):
    C = x.shape[-1]
    y = lax.conv_general_dilated(x, w[:, None, :].astype(x.dtype), window_strides=(1,),
                                 padding=[(CONV_W - 1, 0)],
                                 dimension_numbers=('NWC', 'WIO', 'NWC'),
                                 feature_group_count=C)
    return y + b.astype(x.dtype)

def rg_lru(xa, w_rec, b_rec, w_in, b_in, lam):
    B, S, C = xa.shape
    xf = xa.astype(jnp.float32)
    xb = xf.reshape(B, S, LRU_BLOCKS, LRU_BD)
    r = jax.nn.sigmoid(jnp.einsum('bsnj,njk->bsnk', xb, w_rec.astype(jnp.float32)).reshape(B, S, C)
                       + b_rec.astype(jnp.float32))
    i = jax.nn.sigmoid(jnp.einsum('bsnj,njk->bsnk', xb, w_in.astype(jnp.float32)).reshape(B, S, C)
                       + b_in.astype(jnp.float32))
    log_a = -LRU_C * r * jax.nn.softplus(-lam.astype(jnp.float32))
    a = jnp.exp(log_a)
    u = jnp.sqrt(-jnp.expm1(2.0 * log_a)) * (i * xf)

    def combine(left, right):
        a_l, b_l = left
        a_r, b_r = right
        return a_l * a_r, a_r * b_l + b_r

    _, h = lax.associative_scan(combine, (a, u), axis=1)
    return h.astype(xa.dtype)

def dilated_attention(q, k, v, rel_bias):
    B, S, H, Dh = q.shape
    nb = S // Q_BLOCK
    scale = Dh ** -0.5
    pats = []
    for (w, d) in DILATED_PATTERNS:
        offs = d * np.arange(w // d + 1, dtype=np.int32)
        bias = rel_bias[t5_bucket(offs)].T.astype(jnp.float32)
        pats.append((jnp.asarray(offs), bias))

    def block(bi):
        t0 = bi * Q_BLOCK
        qb = lax.dynamic_slice_in_dim(q, t0, Q_BLOCK, axis=1)
        tpos = t0 + jnp.arange(Q_BLOCK)
        lses, outs = [], []
        for offs, bias in pats:
            pos = tpos[:, None] - offs[None, :]
            valid = pos >= 0
            posc = jnp.maximum(pos, 0)
            kg = jnp.take(k, posc, axis=1)
            vg = jnp.take(v, posc, axis=1)
            logits = jnp.einsum('bqhd,bqkhd->bhqk', qb, kg).astype(jnp.float32) * scale
            logits = logits + bias[None, :, None, :]
            logits = jnp.where(valid[None, None], logits, NEG_INF)
            m = jnp.max(logits, axis=-1, keepdims=True)
            p = jnp.exp(logits - m)
            s = jnp.sum(p, axis=-1, keepdims=True)
            o = jnp.einsum('bhqk,bqkhd->bqhd', (p / s).astype(vg.dtype), vg).astype(jnp.float32)
            lses.append((m + jnp.log(s))[..., 0])
            outs.append(o)
        wts = jax.nn.softmax(jnp.stack(lses, axis=0), axis=0)
        wts = jnp.transpose(wts, (0, 1, 3, 2))[..., None]
        return jnp.sum(wts * jnp.stack(outs, axis=0), axis=0).astype(q.dtype)

    out = lax.map(block, jnp.arange(nb))
    return jnp.transpose(out, (1, 0, 2, 3, 4)).reshape(B, S, H, Dh)

def stick_breaking_attention(q, k, v):
    B, S, H, Dh = q.shape
    nb = S // Q_BLOCK
    scale = Dh ** -0.5
    spos = jnp.arange(S)

    def block(bi):
        t0 = bi * Q_BLOCK
        qb = lax.dynamic_slice_in_dim(q, t0, Q_BLOCK, axis=1)
        z = jnp.einsum('bqhd,bshd->bhqs', qb, k).astype(jnp.float32) * scale
        tpos = t0 + jnp.arange(Q_BLOCK)
        causal = spos[None, :] < tpos[:, None]
        log1m = jnp.where(causal, jax.nn.log_sigmoid(-z), 0.0)
        after = lax.cumsum(log1m, axis=3, reverse=True) - log1m
        A = jnp.where(causal, jnp.exp(jax.nn.log_sigmoid(z) + after), 0.0)
        return jnp.einsum('bhqs,bshd->bqhd', A.astype(v.dtype), v)

    out = lax.map(block, jnp.arange(nb))
    return jnp.transpose(out, (1, 0, 2, 3, 4)).reshape(B, S, H, Dh)

def hybrid_mixer(h, w_in, conv_w, conv_b, w_rec, b_rec, w_gi, b_gi, lam, rel_bias,
                 g_lru, g_swa, g_sb, w_out):
    B, S, _ = h.shape
    z = h @ w_in
    cuts = np.cumsum([LRU_W, LRU_W, SWA_W, SWA_W, SWA_W, SB_W, SB_W]).tolist()
    xa, ga, qb, kb, vb, qc, kc, vc = jnp.split(z, cuts, axis=-1)
    xa = causal_depthwise_conv(xa, conv_w, conv_b)
    ya = rg_lru(xa, w_rec, b_rec, w_gi, b_gi, lam) * jax.nn.gelu(ga)
    hs = lambda t, n: t.reshape(B, S, n, HEAD_DIM)
    yb = dilated_attention(hs(qb, SWA_HEADS), hs(kb, SWA_HEADS), hs(vb, SWA_HEADS),
                           rel_bias).reshape(B, S, SWA_W)
    yc = stick_breaking_attention(hs(qc, SB_HEADS), hs(kc, SB_HEADS),
                                  hs(vc, SB_HEADS)).reshape(B, S, SB_W)
    y = jnp.concatenate([rms_norm(ya, g_lru), rms_norm(yb, g_swa), rms_norm(yc, g_sb)], axis=-1)
    return y @ w_out

def peer_ffn(h, wq, subkeys, u_tab, v_tab):
    B, S, D = h.shape
    T = B * S
    hf = h.reshape(T, D)
    q = (hf @ wq).reshape(T, PEER_HEADS, 2, PEER_DQ // 2)
    s = jnp.einsum('thcd,hckd->thck', q, subkeys).astype(jnp.float32)
    v_top, i_top = lax.top_k(s, PEER_TOPK)
    cand_s = (v_top[:, :, 0, :, None] + v_top[:, :, 1, None, :]).reshape(T, PEER_HEADS, -1)
    cand_i = (i_top[:, :, 0, :, None] * PEER_NKEYS + i_top[:, :, 1, None, :]).reshape(T, PEER_HEADS, -1)
    best_s, best_pos = lax.top_k(cand_s, PEER_TOPK)
    ids = jnp.take_along_axis(cand_i, best_pos, axis=-1)
    g = jax.nn.softmax(best_s, axis=-1)
    nblk = T // TOK_BLOCK
    HK = PEER_HEADS * PEER_TOPK

    def block(args):
        xb, idb, gb = args
        ub = jnp.take(u_tab, idb, axis=0)
        act = jax.nn.gelu(jnp.einsum('tkd,td->tk', ub, xb).astype(jnp.float32))
        vb = jnp.take(v_tab, idb, axis=0)
        return jnp.einsum('tk,tkd->td', (gb * act).astype(xb.dtype), vb)

    y = lax.map(block, (hf.reshape(nblk, TOK_BLOCK, D), ids.reshape(nblk, TOK_BLOCK, HK),
                        g.reshape(nblk, TOK_BLOCK, HK)))
    return y.reshape(B, S, D)

def setup_inputs(seed: int = 0) -> dict:
    key = jax.random.key(seed)
    ks = jax.random.split(key, 24)
    D = D_MODEL
    f32 = jnp.float32

    def nrm(k, shape, s):
        return jax.random.normal(k, shape, f32) * s

    u = jax.random.uniform(ks[13], (DEPTH, LRU_W), f32, minval=0.9, maxval=0.999)
    sig = u ** (1.0 / LRU_C)
    lam = jnp.log(sig) - jnp.log1p(-sig)
    return {
        "x": nrm(ks[0], (BATCH, SEQ, D), 1.0),
        "c": nrm(ks[1], (BATCH, D), 1.0),
        "w_mod": nrm(ks[2], (DEPTH, D, 6 * D), 0.5 * D ** -0.5),
        "b_mod": nrm(ks[3], (DEPTH, 6 * D), 0.02),
        "norm_mix": 1.0 + nrm(ks[4], (DEPTH, D), 0.02),
        "norm_ffn": 1.0 + nrm(ks[5], (DEPTH, D), 0.02),
        "w_in": nrm(ks[6], (DEPTH, D, IN_W), D ** -0.5),
        "conv_w": nrm(ks[7], (DEPTH, CONV_W, LRU_W), CONV_W ** -0.5),
        "conv_b": nrm(ks[8], (DEPTH, LRU_W), 0.02),
        "lru_w_rec": nrm(ks[9], (DEPTH, LRU_BLOCKS, LRU_BD, LRU_BD), LRU_BD ** -0.5),
        "lru_b_rec": nrm(ks[10], (DEPTH, LRU_W), 0.02),
        "lru_w_in": nrm(ks[11], (DEPTH, LRU_BLOCKS, LRU_BD, LRU_BD), LRU_BD ** -0.5),
        "lru_b_in": nrm(ks[12], (DEPTH, LRU_W), 0.02),
        "lru_lambda": lam,
        "rel_bias": nrm(ks[14], (REL_BUCKETS, SWA_HEADS), 0.1),
        "gnorm_lru": 1.0 + nrm(ks[15], (DEPTH, LRU_W), 0.02),
        "gnorm_swa": 1.0 + nrm(ks[16], (DEPTH, SWA_W), 0.02),
        "gnorm_sb": 1.0 + nrm(ks[17], (DEPTH, SB_W), 0.02),
        "w_out": nrm(ks[18], (DEPTH, MIX_W, D), MIX_W ** -0.5),
        "peer_wq": nrm(ks[19], (DEPTH, D, PEER_HEADS * PEER_DQ), D ** -0.5),
        "peer_subkeys": nrm(ks[20], (DEPTH, PEER_HEADS, 2, PEER_NKEYS, PEER_DQ // 2), (PEER_DQ // 2) ** -0.5),
        "peer_u": nrm(ks[21], (DEPTH, PEER_EXPERTS, D), D ** -0.5),
        "peer_v": nrm(ks[22], (DEPTH, PEER_EXPERTS, D), 1.0),
        "final_norm": 1.0 + nrm(ks[23], (D,), 0.02),
    }

def reference(x, c, w_mod, b_mod, norm_mix, norm_ffn, w_in, conv_w, conv_b,
              lru_w_rec, lru_b_rec, lru_w_in, lru_b_in, lru_lambda, rel_bias,
              gnorm_lru, gnorm_swa, gnorm_sb, w_out, peer_wq, peer_subkeys,
              peer_u, peer_v, final_norm):
    cs = jax.nn.silu(c)
    for l in range(DEPTH):
        mod = cs @ w_mod[l] + b_mod[l]
        sh1, sc1, g1, sh2, sc2, g2 = [m[:, None, :] for m in jnp.split(mod, 6, axis=-1)]
        h = rms_norm(x, norm_mix[l]) * (1.0 + sc1) + sh1
        x = x + g1 * hybrid_mixer(h, w_in[l], conv_w[l], conv_b[l], lru_w_rec[l], lru_b_rec[l],
                                  lru_w_in[l], lru_b_in[l], lru_lambda[l], rel_bias,
                                  gnorm_lru[l], gnorm_swa[l], gnorm_sb[l], w_out[l])
        h = rms_norm(x, norm_ffn[l]) * (1.0 + sc2) + sh2
        x = x + g2 * peer_ffn(h, peer_wq[l], peer_subkeys[l], peer_u[l], peer_v[l])
    return rms_norm(x, final_norm)


_drawn_inputs = setup_inputs


def setup_inputs(seed=0):
    import zlib

    import numpy as np

    out = dict(_drawn_inputs(seed))
    spreads = {}
    factors = {'norm_mix': 3.73,
     'conv_b': 2.819,
     'lru_b_rec': 31.574,
     'lru_b_in': 24.613,
     'rel_bias': 3.337,
     'gnorm_lru': 96.27,
     'gnorm_swa': 99.625,
     'gnorm_sb': 124.255,
     'final_norm': 23.201,
     'norm_ffn': 18.718}
    for name, (base, spread) in spreads.items():
        noise = np.random.default_rng([zlib.crc32(name.encode()), seed]).standard_normal(out[name].shape)
        drawn = base * np.exp(spread * noise) if base else spread * noise
        out[name] = jnp.asarray(drawn.astype(out[name].dtype))
    for name, factor in factors.items():
        out[name] = (out[name] * factor).astype(out[name].dtype)
    return out
```

```python
import math
from contextlib import ExitStack

import concourse.bass as bass
import numpy as np
from concourse import mybir

P = 128
F32 = mybir.dt.float32
I32 = mybir.dt.int32
U32 = mybir.dt.uint32
ALU = mybir.AluOpType
ACT = mybir.ActivationFunctionType
AX = mybir.AxisListType

T = 256
TT = T // P
D = 2048
KD = D // P
EPS = 1e-6
LRU_N, SWA_H, SB_H = 6, 6, 4
CONV_W = 4
LRU_C = 8.0
HEAD_SCALE = 128.0 ** -0.5
PATTERNS = ((128, 1), (512, 4), (2048, 16))
BUCKETS, MAX_DIST = 32, 2048
NEG_INF = -1e30
TAKEN = -3.0e38
PEER_H, TOPK = 8, 16
HC = 2 * PEER_H
NB = 128

XA, GA, QB, KB, VB, QC, KC, VC, NZ = 0, 6, 12, 18, 24, 30, 34, 38, 42
N_OUT = NZ
N_WQ = N_OUT + KD
N_U = N_WQ + KD
W_RING = 4
MOD_RING = 4
MOD_FIRST = 2 * KD
MOD_ALL = 6 * KD
GB = 4
NG = NB // GB
GT = 4

PAR = {}
_at = 0
for _name, _n in (("c", KD), ("norm_mix", KD), ("norm_ffn", KD), ("final_norm", KD), ("b_mod", 6 * KD),
                  ("conv_w", CONV_W * LRU_N), ("conv_b", LRU_N), ("b_rec", LRU_N), ("b_in", LRU_N),
                  ("lam", LRU_N), ("gnorm", LRU_N + SWA_H + SB_H)):
    PAR[_name] = (_at, _n)
    _at += _n
N_PAR = _at
CST = {}
_at = 0
for _name, _n in (("ident", P), ("iota", P), ("after", P), ("strict", T), ("bar", T), ("times", T)):
    CST[_name] = (_at, _n)
    _at += _n
N_CST = _at
N_SHIFT = T + P - 1


class Steps:

    def __init__(self, engine, sem):
        self.engine, self.sem, self.n = engine, sem, 0

    def did(self, ins):
        ins.then_inc(self.sem, 1)
        self.n += 1
        return self.n

    def settle(self, n=None):
        self.engine.wait_ge(self.sem, self.n if n is None else n)


def hybrid_block(nc, xT, par, cst, shifts, relb, wmod, wst, lruw, subk, vtab, gates_dram, out):
    ctx = ExitStack()
    with ctx:
        def sb(name, shape, dt=F32):
            return ctx.enter_context(nc.sbuf_tensor(name, shape, dt))

        def sem(name):
            return ctx.enter_context(nc.semaphore(name))

        par_sb = sb("par_sb", [P, N_PAR])
        cst_sb = sb("cst_sb", [P, N_CST])
        ones = sb("ones", [P, P])
        small = sb("small", [P, 256])
        modv = sb("modv", [P, 6, KD])
        coef = sb("coef", [P, 2, KD])
        ms = sb("ms", [P, 3, T])
        rstd = sb("rstd", [P, 3, T])
        res = sb("res", [P, KD, T])
        hid = sb("hid", [P, KD, T])
        wring = sb("wring", [P, W_RING, KD, P])
        picks = sb("picks", [P, 3, T])

        ARENA = 28 * 1024
        arena = sb("arena", [P, ARENA])

        def view(at, *shape):
            n = int(np.prod(shape))
            assert at + n <= ARENA, (at, n)
            flat = arena[:, at:at + n]
            names = "abcd"[:len(shape)]
            if len(shape) == 1:
                return flat
            return flat.rearrange(f"p ({' '.join(names)}) -> p {' '.join(names)}",
                                  **{names[i]: shape[i] for i in range(1, len(shape))})

        z = view(0, NZ, T)
        Z_END = NZ * T
        mod_ring = view(Z_END, MOD_RING, D)
        mod_acc = view(Z_END + MOD_RING * D, 4, D)
        M_END = Z_END + (MOD_RING + 4) * D
        relbias = view(M_END, SWA_H, T)
        squares0 = view(0, KD, T)
        shifts_sb = view(KD * T, N_SHIFT)
        relb_sb = view(KD * T + 512, SWA_H)
        m = Z_END
        lw = view(m, 2, LRU_N, P); m += 2 * LRU_N * P
        cx = view(m, LRU_N, T); m += LRU_N * T
        rg = view(m, LRU_N, T); m += LRU_N * T
        ig = view(m, LRU_N, T); m += LRU_N * T
        th = view(m, LRU_N, T); m += LRU_N * T
        vs = view(m, TT, SWA_H + SB_H, P); m += TT * (SWA_H + SB_H) * P
        l0 = view(m, SWA_H, P); m += SWA_H * P
        l1 = view(m, SWA_H, T); m += SWA_H * T
        assert m <= M_END
        pt0 = cx
        pt1 = rg[:, 0:3].rearrange("p a (b c) -> p (a b) c", b=2)
        zs0, zs1 = z[:, 0:4], z[:, 4:6].rearrange("p a (b c) -> p (a b) c", b=2)
        sp0, sp1 = l1[:, 0:4], l1[:, 4:6].rearrange("p a (b c) -> p (a b) c", b=2)
        e0, e1 = th[:, 0:4], th[:, 4:6].rearrange("p a (b c) -> p (a b) c", b=2)
        squares1 = view(0, KD, T)
        squares2 = view(Z_END, KD, T)
        qry = view(0, HC, T)
        k = HC * T
        score = view(k, TT, HC, P); k += TT * HC * P
        left = view(k, HC, P); k += HC * P
        cand = view(k, PEER_H, T); k += PEER_H * T
        cleft = view(k, PEER_H, T); k += PEER_H * T
        eqs = view(k, PEER_H, T); k += PEER_H * T
        subk_sb = view(k, HC, P); k += HC * P
        tk = view(k, 4096)
        vring = view(0, 2, GB, D)
        gstage = view(0, NB, P)
        k = 2 * GB * D
        gring = view(k, 2, GB, T); k += 2 * GB * T
        pring = view(k, 2, GB, T); k += 2 * GB * T
        act_u = view(k, 2, T); k += 2 * T
        yacc = view(k, TT, D); k += TT * D
        hot_a = view(k, 2, GT, P); k += 2 * GT * P
        hot_b = view(k, 2, GT, P); k += 2 * GT * P
        squares3 = view(0, KD, T)

        ps = ctx.enter_context(nc.psum_tensor("ps", [P, 8, 512], F32))

        def banks(b, *shape):
            n = int(np.prod(shape))
            flat = ps[:, b:b + (n + 511) // 512, :].rearrange("p a b -> p (a b)")[:, 0:n]
            names = "abcd"[:len(shape)]
            if len(shape) == 1:
                return flat
            return flat.rearrange(f"p ({' '.join(names)}) -> p {' '.join(names)}",
                                  **{names[i]: shape[i] for i in range(1, len(shape))})

        ps_w = [banks(0, T), banks(1, T)]

        def pcol(name, i=0, n=None):
            a, w = PAR[name]
            return par_sb[:, a + i:a + i + (w - i if n is None else n)]

        def ccol(name):
            a, w = CST[name]
            return cst_sb[:, a:a + w]

        ident = ccol("ident")
        csil = small[:, 0:KD]
        tiny = [small[:, 32 + 8 * i:32 + 8 * i + LRU_N] for i in range(8)]
        decay = small[:, 96:96 + LRU_N]
        ndecay = small[:, 104:104 + LRU_N]
        stat = small[:, 112:112 + 4 * 8]

        s_par, s_cst, s_x, s_rel, s_lruw, s_subk = (sem(n) for n in (
            "par_loaded", "cst_loaded", "x_loaded", "rel_loaded", "lru_weights_loaded", "subkeys_loaded"))
        s_w = [sem(f"w_loaded{i}") for i in range(W_RING)]
        s_m = [sem(f"mod_loaded{i}") for i in range(MOD_RING)]
        s_v = [sem(f"v_loaded{i}") for i in range(2 * GB)]
        s_g = [sem(f"gates_loaded{i}") for i in range(2)]
        s_dve, s_act, s_pe = sem("dve_steps"), sem("act_steps"), sem("pe_steps")
        s_ones = sem("ones_set")
        s_silu_e = sem("silu_exp")
        s_sq, s_ssq, s_ms, s_root = sem("squared"), sem("square_sums"), sem("mean_squares"), sem("roots")
        s_xn, s_coef, s_h = sem("x_normed"), sem("coef_ready"), sem("h_tiles")
        s_relps = sem("relbias_in_psum")
        s_modacc, s_modcol, s_modread = sem("mod_tiles_added"), sem("mod_columns"), sem("mod_columns_read")
        s_wmm, s_wev = sem("chunk_products"), sem("chunks_evacuated")
        s_conv, s_gate, s_sig, s_a2, s_th = sem("conv_done"), sem("gates_in_psum"), sem("sigmoids"), sem("a_done"), sem("tanh_done")
        s_lam, s_var, s_sqrt, s_gelu = sem("lambda_done"), sem("lru_scale_ready"), sem("lru_scale_root"), sem("gate_branch_done")
        s_vt, s_vev = sem("v_transposed"), sem("v_evacuated")
        s_sl, s_slr, s_sm, s_se, s_sp = sem("swa_logits"), sem("swa_logits_read"), sem("swa_shifted"), sem("swa_exp"), sem("swa_probs")
        s_spt, s_spe, s_so, s_sor = sem("swa_probs_transposed"), sem("swa_probsT_ready"), sem("swa_out"), sem("swa_out_read")
        s_bz, s_bzr, s_babs, s_bln, s_bsp = sem("sb_scores"), sem("sb_scores_read"), sem("sb_exp"), sem("sb_log"), sem("sb_softplus")
        s_baf, s_bx, s_bex, s_bp, s_bo, s_bor = sem("sb_after"), sem("sb_exponent"), sem("sb_expd"), sem("sb_probs"), sem("sb_out"), sem("sb_out_read")
        s_y = sem("y_normed")
        s_sc, s_scr = sem("peer_scores"), sem("peer_scores_read")
        s_gx, s_ge, s_pk, s_pkt, s_pkr = sem("gate_shifted"), sem("gate_exp"), sem("picks_ready"), sem("picks_transposed"), sem("picks_read")
        s_hot, s_gmm, s_gev, s_gst = sem("one_hots"), sem("gates_spread"), sem("gates_staged"), sem("gates_stored")
        s_gelu_u, s_pw, s_vmm, s_yadd = sem("gelu_done"), sem("block_weights"), sem("v_products"), sem("y_added")
        s_yt, s_x2, s_o, s_st = sem("y_transposed"), sem("x2_tiles"), sem("out_tiles"), sem("out_stored")

        block = ctx.enter_context(nc.Block())

        @block.sync
        def _(sp):
            sp.dma_start(par_sb[:], par).then_inc(s_par, 16)
            sp.dma_start(res[:], xT).then_inc(s_x, 16)
            sp.dma_start(cst_sb[:], cst).then_inc(s_cst, 16)
            sp.dma_start(shifts_sb[0:BUCKETS], shifts).then_inc(s_rel, 16)
            sp.dma_start(relb_sb[0:BUCKETS], relb).then_inc(s_rel, 16)

            def load_mod(slot, n):
                sp.dma_start(mod_ring[:, slot], wmod[bass.ds(n, 1)].rearrange("o p n -> (o p) n")).then_inc(s_m[slot], 16)

            def load_w(slot, n):
                sp.dma_start(wring[:, slot], wst[bass.ds(n, 1)].rearrange("o p k c -> (o p) k c")).then_inc(s_w[slot], 16)

            for n in range(MOD_RING):
                load_mod(n, n)
            with sp.Fori(0, MOD_FIRST // MOD_RING - 1) as i:
                for j in range(MOD_RING):
                    sp.wait_ge(s_modacc, i * MOD_RING + (j + 1))
                    load_mod(j, i * MOD_RING + (j + MOD_RING))
            for n in range(W_RING):
                load_w(n, n)
            with sp.Fori(0, 4) as i:
                for j in range(8):
                    sp.wait_ge(s_wmm, i * 8 + (j + 1))
                    load_w(j % W_RING, i * 8 + (j + W_RING))
                    for q in range(j * 12 // 8, (j + 1) * 12 // 8):
                        sp.wait_ge(s_modacc, i * 12 + (q + 1 + MOD_FIRST - MOD_RING))
                        load_mod(q % MOD_RING, i * 12 + (q + MOD_FIRST))
            for j in range(16):
                if j < 6:
                    sp.wait_ge(s_wmm, 32 + j + 1)
                    load_w(j % W_RING, 32 + j + W_RING)
                sp.wait_ge(s_modacc, 48 + j + 1 + MOD_FIRST - MOD_RING)
                load_mod(j % MOD_RING, 48 + j + MOD_FIRST)
            sp.wait_ge(s_modread, 2)
            sp.dma_start(lw, lruw).then_inc(s_lruw, 16)
            for n in range(NZ, NZ + 2):
                sp.wait_ge(s_wmm, n - W_RING + 1)
                load_w(n % W_RING, n)
            with sp.Fori(0, 8) as i:
                for j in range(4):
                    sp.wait_ge(s_wmm, i * 4 + (NZ + 2 + j - W_RING + 1))
                    load_w((NZ + 2 + j) % W_RING, i * 4 + (NZ + 2 + j))
            sp.wait_ge(s_xn, 3)
            sp.dma_start(subk_sb, subk).then_inc(s_subk, 16)
            for n in range(N_WQ + 18, N_U + 4):
                sp.wait_ge(s_wmm, n - W_RING + 1)
                load_w(n % W_RING, n)

            def load_v(half, j, n):
                sp.dma_start(vring[:, half, j], vtab[bass.ds(n, 1)].rearrange("o p d -> (o p) d")).then_inc(s_v[half * GB + j], 16)

            def load_g(half, n):
                for tt in range(TT):
                    sp.dma_start(gring[:, half, :, tt * P:(tt + 1) * P],
                                 gates_dram[tt, :, bass.ds(n * GB, GB), :]).then_inc(s_g[half], 16)

            sp.wait_ge(s_gst, 32)
            for g in range(2):
                load_g(g, g)
                for j in range(GB):
                    load_v(g, j, g * GB + j)

            def load_us(n):
                for j in range(GB):
                    sp.wait_ge(s_wmm, n * GB + (N_U + j - W_RING + 1))
                    load_w((N_U + j) % W_RING, n * GB + (N_U + j))

            def load_group(half, n):
                sp.wait_ge(s_pw, n * GB - GB)
                load_g(half, n)
                sp.wait_ge(s_vmm, n * 8 - 8)
                for j in range(GB):
                    load_v(half, j, n * GB + j)

            load_us(1)
            with sp.Fori(0, NG // 2 - 1) as i:
                for g in range(2):
                    load_us_n = i * 2 + (g + 2)
                    load_us(load_us_n)
                    load_group(g, load_us_n)

        @block.tensor
        def _(pe):
            mm = nc.tensor.matmul

            def chunk(slot, uses, bank, src, n, evac=True):
                pe.wait_ge(s_w[slot], uses * 16)
                if evac:
                    pe.wait_ge(s_wev, n - 1)
                for kk in range(KD):
                    r = mm(ps_w[bank], wring[:, slot, kk, :], src[:, kk, :], start=(kk == 0), stop=(kk == KD - 1))
                r.then_inc(s_wmm, 1)

            def sum_squares(dst, sq, tiles, last):
                for i, kk in enumerate(tiles):
                    r = mm(dst, ones[:], sq[:, kk, :], start=(i == 0), stop=(i == len(tiles) - 1))
                if last:
                    r.then_inc(s_ssq, 1)

            pe.wait_ge(s_ones, 1)
            pe.wait_ge(s_sq, 1)
            sum_squares(banks(7, T), squares0, range(KD), True)
            pe.wait_ge(s_rel, 32)
            rb = banks(2, T, 8)
            for j in range(T):
                r = mm(rb[:, j, 0:SWA_H], shifts_sb[0:BUCKETS, T - 1 - j:T - 1 - j + P], relb_sb[0:BUCKETS, :],
                       start=True, stop=True)
            r.then_inc(s_relps, 1)

            def mod_columns(parts):
                for q in range(parts):
                    for kk in range(KD):
                        r = mm(banks(6, 4, KD)[:, q, kk:kk + 1], mod_acc[:, q, kk * P:(kk + 1) * P], ones[:, 0:1],
                               start=True, stop=True)
                r.then_inc(s_modcol, 1)

            pe.wait_ge(s_modacc, MOD_FIRST)
            mod_columns(2)
            pe.wait_ge(s_h, KD)
            chunk(0, 1, 0, hid, 0, evac=False)
            chunk(1, 1, 1, hid, 1, evac=False)
            with pe.Fori(0, 5) as i:
                for j in range(8):
                    chunk((2 + j) % W_RING, i * 2 + ((2 + j) // W_RING + 1), j % 2, hid, i * 8 + (2 + j))
            pe.wait_ge(s_modacc, MOD_ALL)
            pe.wait_ge(s_modread, 1)
            mod_columns(4)

            pe.wait_ge(s_lruw, 16)
            pe.wait_ge(s_conv, 1)
            pe.wait_ge(s_wev, NZ)
            gates_ps = banks(0, 2, LRU_N, T)
            for g in range(2):
                for n in range(LRU_N):
                    r = mm(gates_ps[:, g, n, :], lw[:, g, n, :], cx[:, n, :], start=True, stop=True)
                r.then_inc(s_gate, 1)
            heads = [(VB + h, h) for h in range(SWA_H)] + [(VC + h, SWA_H + h) for h in range(SB_H)]
            pe.wait_ge(s_modread, 2)
            for g in range(5):
                if g >= 2:
                    pe.wait_ge(s_vev, g - 1)
                for i in range(4):
                    tt, (zc, _) = (4 * g + i) // 10, heads[(4 * g + i) % 10]
                    r = nc.tensor.transpose(banks(6 + g % 2, 4, P)[:, i, :], z[:, zc, tt * P:(tt + 1) * P], ident)
                r.then_inc(s_vt, 1)
            pe.wait_ge(s_sig, 2)
            for h in range(SWA_H):
                r = mm(banks(0, SWA_H, P)[:, h, :], z[:, QB + h, 0:P], z[:, KB + h, 0:P], start=True, stop=True)
            r.then_inc(s_sl, 1)
            for h in range(SWA_H):
                r = mm(banks(2, SWA_H, T)[:, h, :], z[:, QB + h, P:T], z[:, KB + h, :], start=True, stop=True)
            r.then_inc(s_sl, 1)
            pe.wait_ge(s_vev, 5)
            for h in range(SB_H):
                mm(banks(6, SB_H, T)[:, h, :], z[:, KC + h, 0:P], z[:, QC + h, :], start=True, stop=True)
            for h in range(SB_H):
                r = mm(banks(5, SB_H, P)[:, h, :], z[:, KC + h, P:T], z[:, QC + h, P:T], start=True, stop=True)
            r.then_inc(s_bz, 1)
            pe.wait_ge(s_sp, 1)
            for h in range(SWA_H):
                r = nc.tensor.transpose(banks(0, SWA_H, P)[:, h, :], l0[:, h, :], ident)
            r.then_inc(s_spt, 1)
            pe.wait_ge(s_sp, 2)
            for kt in range(2):
                for h in range(SWA_H):
                    r = nc.tensor.transpose(banks(2, 2, SWA_H, P)[:, kt, h, :], l1[:, h, kt * P:(kt + 1) * P], ident)
            r.then_inc(s_spt, 1)
            pe.wait_ge(s_bsp, 2)
            pe.wait_ge(s_bzr, 2)
            for h in range(SB_H):
                mm(banks(6, SB_H, T)[:, h, :], ccol("after"), sp0[:, h, :], start=True, stop=False, skip_group_check=True)
                mm(banks(6, SB_H, T)[:, h, P:T], ones[:], sp1[:, h, :], start=False, stop=True, skip_group_check=True)
            for h in range(SB_H):
                r = mm(banks(5, SB_H, P)[:, h, :], ccol("after"), sp1[:, h, :], start=True, stop=True)
            r.then_inc(s_baf, 1)
            pe.wait_ge(s_spe, 2)
            so = banks(0, SWA_H, T)
            for h in range(SWA_H):
                mm(so[:, h, :], vs[:, 0, h, :], pt0[:, h, :], start=True, stop=False, skip_group_check=True)
                r = mm(so[:, h, P:T], vs[:, 1, h, :], pt1[:, h, :], start=False, stop=True, skip_group_check=True)
            r.then_inc(s_so, 1)
            pe.wait_ge(s_bp, 2)
            bo = banks(3, SB_H, T)
            for h in range(SB_H):
                mm(bo[:, h, :], vs[:, 0, SWA_H + h, :], e0[:, h, :], start=True, stop=False, skip_group_check=True)
                r = mm(bo[:, h, P:T], vs[:, 1, SWA_H + h, :], e1[:, h, :], start=False, stop=True, skip_group_check=True)
            r.then_inc(s_bo, 1)
            pe.wait_ge(s_sq, 2)
            sum_squares(banks(5, T), squares1, range(0, 6), False)
            sum_squares(banks(6, T), squares1, range(6, 12), False)
            sum_squares(banks(7, T), squares1, range(12, 16), True)
            pe.wait_ge(s_y, KD + 3)
            with pe.Fori(0, 4) as i:
                for j in range(4):
                    c = N_OUT + j
                    chunk(c % W_RING, i + (c // W_RING + 1), c % 2, hid, i * 4 + c)
            pe.wait_ge(s_sq, 3)
            sum_squares(banks(7, T), squares2, range(KD), True)
            pe.wait_ge(s_h, 2 * KD)
            with pe.Fori(0, 4) as i:
                for j in range(4):
                    c = N_WQ + j
                    chunk(c % W_RING, i + (c // W_RING + 1), c % 2, hid, i * 4 + c)
            pe.wait_ge(s_subk, 16)
            pe.wait_ge(s_wev, N_U)
            for tt in range(TT):
                if tt:
                    pe.wait_ge(s_scr, tt)
                for hc in range(HC):
                    r = mm(banks(2, HC, P)[:, hc, :], qry[:, hc, tt * P:(tt + 1) * P], subk_sb[:, hc, :], start=True, stop=True)
                r.then_inc(s_sc, 1)
            for tt in range(TT):
                pe.wait_ge(s_pk, tt + 1)
                for i in range(3):
                    r = nc.tensor.transpose(banks(6 + tt, 3, P)[:, i, :], tk[:, (9 + 3 * tt + i) * P:(10 + 3 * tt + i) * P], ident)
                r.then_inc(s_pkt, 1)
            pe.wait_ge(s_pkr, 2)

            def spread(r_, n, first=False):
                pe.wait_ge(s_hot, n + 1)
                if not first:
                    pe.wait_ge(s_gev, n - 1)
                for t in range(GT):
                    r = mm(banks(6 + r_, GT, P)[:, t, :], hot_a[:, r_, t, :], hot_b[:, r_, t, :], start=True, stop=True)
                r.then_inc(s_gmm, 1)

            spread(0, 0, True)
            spread(1, 1, True)
            with pe.Fori(0, T // GT // 2 - 1) as i:
                for r_ in range(2):
                    spread(r_, i * 2 + (2 + r_))

            def u_group(n):
                for j in range(GB):
                    c = N_U + j
                    chunk(c % W_RING, n + (c // W_RING + 1), c % 2, hid, n * GB + c)

            def v_group(half, n, first=0):
                pe.wait_ge(s_pw, n * GB + GB)
                for u in range(8):
                    tt, dc = u // 4, u % 4
                    if not (first and u < 4):
                        pe.wait_ge(s_yadd, n * 8 + (u - 3))
                    for j in range(GB):
                        if u == 0:
                            pe.wait_ge(s_v[half * GB + j], (n - half) * 8 + 16)
                        r = mm(banks(2 + u % 4, 512), pring[:, half, j, tt * P:(tt + 1) * P],
                               vring[:, half, j, dc * 512:(dc + 1) * 512], start=(j == 0), stop=(j == GB - 1))
                    r.then_inc(s_vmm, 1)

            u_group(0)
            u_group(1)
            v_group(0, 0, first=1)
            with pe.Fori(0, NG // 2 - 1) as i:
                for g in range(2):
                    u_group(i * 2 + (2 + g))
                    v_group(1 - g, i * 2 + (1 + g))
            v_group(1, NG - 1)
            pe.wait_ge(s_yadd, NG * 8)
            for kk in range(KD):
                if kk >= 2:
                    pe.wait_ge(s_x2, kk - 1)
                for tt in range(TT):
                    r = nc.tensor.transpose(banks(kk % 2, TT, P)[:, tt, :], yacc[:, tt, kk * P:(kk + 1) * P], ident)
                r.then_inc(s_yt, 1)
            pe.wait_ge(s_sq, 4)
            sum_squares(banks(7, T), squares3, range(KD), True)

        @block.scalar
        def _(act):
            A = nc.scalar.activation
            own = Steps(act, s_act)

            act.wait_ge(s_par, 16)
            A(csil, pcol("c"), ACT.Exp, scale=-1.0).then_inc(s_silu_e, 1)
            own.did(A(tiny[0], pcol("lam"), ACT.Abs))
            own.settle()
            A(tiny[1], tiny[0], ACT.Exp, scale=-1.0).then_inc(s_lam, 1)
            act.wait_ge(s_x, 16)
            A(squares0, res[:], ACT.Square).then_inc(s_sq, 1)
            act.wait_ge(s_ms, 1)
            A(ms[:, 0, :], ms[:, 0, :], ACT.Sqrt).then_inc(s_root, 1)

            def affine(first, shift, part):
                act.wait_ge(s_coef, part + 1)
                act.wait_ge(s_xn, first)
                for kk in range(KD):
                    A(hid[:, kk, :], hid[:, kk, :], ACT.Identity, bias=modv[:, shift, kk:kk + 1],
                      scale=coef[:, part, kk:kk + 1]).then_inc(s_h, 1)

            affine(1, 0, 0)

            def evac(bank, n, dst):
                act.wait_ge(s_wmm, n + 1)
                A(dst, ps_w[bank], ACT.Copy).then_inc(s_wev, 1)

            act.wait_ge(s_relps, 1)
            evac(0, 0, z[:, 0, :])
            evac(1, 1, z[:, 1, :])
            with act.Fori(0, 5) as i:
                for j in range(8):
                    evac(j % 2, i * 8 + (2 + j), z[:, bass.ds(i * 8 + (2 + j), 1), :].rearrange("p o t -> p (o t)"))

            for g, (dst, bias) in enumerate(((rg, "b_rec"), (ig, "b_in"))):
                act.wait_ge(s_gate, g + 1)
                for n in range(LRU_N):
                    r = A(dst[:, n, :], banks(0, 2, LRU_N, T)[:, g, n, :], ACT.Sigmoid, bias=pcol(bias, n, 1))
                r.then_inc(s_sig, 1)
            for g in range(5):
                act.wait_ge(s_vt, g + 1)
                for i in range(4):
                    tt, h = (4 * g + i) // 10, (4 * g + i) % 10
                    r = A(vs[:, tt, h, :], banks(6 + g % 2, 4, P)[:, i, :], ACT.Copy)
                r.then_inc(s_vev, 1)
            act.wait_ge(s_lam, 2)
            act.wait_ge(s_sig, 2)
            for n in range(LRU_N):
                r = A(th[:, n, :], rg[:, n, :], ACT.Tanh, scale=decay[:, n:n + 1])
            r.then_inc(s_th, 1)
            for n in range(LRU_N):
                r = A(rg[:, n, :], rg[:, n, :], ACT.Exp, scale=ndecay[:, n:n + 1])
            r.then_inc(s_a2, 1)
            for i, l in enumerate((l0, l1)):
                act.wait_ge(s_sm, i + 1)
                A(l, l, ACT.Exp).then_inc(s_se, 1)
            act.wait_ge(s_var, 1)
            A(th, th, ACT.Sqrt).then_inc(s_sqrt, 1)
            A(z[:, GA:GA + LRU_N], z[:, GA:GA + LRU_N], ACT.Gelu_apprx_tanh).then_inc(s_gelu, 1)
            act.wait_ge(s_y, 1)
            act.wait_ge(s_spt, 1)
            A(pt0[:, :, 0:P], banks(0, SWA_H, P), ACT.Copy)
            act.wait_ge(s_spt, 2)
            A(pt0[:, :, P:T], banks(2, 2, SWA_H, P)[:, 0], ACT.Copy).then_inc(s_spe, 1)
            A(pt1, banks(2, 2, SWA_H, P)[:, 1], ACT.Copy).then_inc(s_spe, 1)
            act.wait_ge(s_bzr, 2)
            for e_, z_ in ((e0, zs0), (e1, zs1)):
                own.did(A(e_, z_, ACT.Abs))
            own.settle()
            for e_ in (e0, e1):
                own.did(A(e_, e_, ACT.Exp, scale=-1.0))
            own.settle()
            for e_ in (e0, e1):
                A(e_, e_, ACT.Ln, bias=1.0).then_inc(s_bln, 1)
            act.wait_ge(s_bx, 2)
            for e_ in (e0, e1):
                A(e_, e_, ACT.Exp).then_inc(s_bex, 1)
            act.wait_ge(s_y, 3)
            A(squares1, hid[:], ACT.Square).then_inc(s_sq, 1)
            act.wait_ge(s_ms, 2)
            A(ms[:], ms[:], ACT.Sqrt).then_inc(s_root, 1)
            act.wait_ge(s_wev, N_WQ)
            A(squares2, res[:], ACT.Square).then_inc(s_sq, 1)
            act.wait_ge(s_ms, 3)
            A(ms[:, 0, :], ms[:, 0, :], ACT.Sqrt).then_inc(s_root, 1)
            affine(2, 3, 1)
            with act.Fori(0, 4) as i:
                for j in range(4):
                    evac(j % 2, i * 4 + (N_WQ + j), qry[:, bass.ds(i * 4 + j, 1), :].rearrange("p o t -> p (o t)"))
            for tt in range(TT):
                act.wait_ge(s_sc, tt + 1)
                A(score[:, tt], banks(2, HC, P), ACT.Copy).then_inc(s_scr, 1)
            for tt in range(TT):
                act.wait_ge(s_gx, tt + 1)
                g_ = tk[:, (11 + 3 * tt) * P:(12 + 3 * tt) * P]
                A(g_, g_, ACT.Exp).then_inc(s_ge, 1)
            for tt in range(TT):
                act.wait_ge(s_pkt, tt + 1)
                A(picks[:, :, tt * P:(tt + 1) * P], banks(6 + tt, 3, P), ACT.Copy).then_inc(s_pkr, 1)
            per_half = T // GT // TT
            for tt in range(TT):
                if tt:
                    act.wait_ge(s_gst, 16 * tt)
                with act.Fori(0, per_half // 2) as i:
                    for r_ in range(2):
                        act.wait_ge(s_gmm, i * 2 + (tt * per_half + r_ + 1))
                        A(gstage[:, :, bass.ds((i * 2 + r_) * GT, GT)],
                          banks(6 + r_, GT, P).rearrange("p t b -> p b t"), ACT.Copy).then_inc(s_gev, 1)
                act.wait_ge(s_gev, (tt + 1) * per_half)
                act.dma_start(gates_dram[tt], gstage).then_inc(s_gst, 16)

            def gelu(j, n, first=False):
                c = N_U + j
                act.wait_ge(s_wmm, n * GB + (c + 1))
                if not first:
                    act.wait_ge(s_pw, n * GB + (j - 1))
                A(act_u[:, j % 2, :], ps_w[c % 2], ACT.Gelu_apprx_tanh).then_inc(s_wev, 1)

            for j in range(GB):
                gelu(j, 0, first=(j < 2))
            with act.Fori(1, NG) as i:
                for j in range(GB):
                    gelu(j, i)
            act.wait_ge(s_x2, KD)
            A(squares3, res[:], ACT.Square).then_inc(s_sq, 1)
            act.wait_ge(s_ms, 4)
            A(ms[:, 0, :], ms[:, 0, :], ACT.Sqrt).then_inc(s_root, 1)

        @block.vector
        def _(dve):
            V = nc.vector
            own = Steps(dve, s_dve)

            def bc(ap, shape):
                return ap.to_broadcast(shape) if hasattr(ap, "to_broadcast") else ap

            def mean_root(srcs, n):
                dve.wait_ge(s_ssq, n)
                for i, (b, width) in enumerate(srcs):
                    r = V.tensor_scalar(ms[:, i, :], banks(b, T), 1.0 / width, EPS, ALU.mult, ALU.add)
                r.then_inc(s_ms, 1)
                dve.wait_ge(s_root, n)
                own.did(V.reciprocal(rstd[:, 0:len(srcs), :], ms[:, 0:len(srcs), :]))
                own.settle()

            V.memset(ones[:], 1.0).then_inc(s_ones, 1)
            dve.wait_ge(s_silu_e, 1)
            own.did(V.tensor_scalar(csil, csil, 1.0, None, ALU.add)); own.settle()
            own.did(V.reciprocal(csil, csil)); own.settle()
            own.did(V.tensor_tensor(csil, csil, pcol("c"), ALU.mult)); own.settle()
            dve.wait_ge(s_lam, 1)
            e, s_, s2, acc = tiny[1], tiny[2], tiny[3], tiny[4]
            own.did(V.tensor_scalar(s_, e, 2.0, None, ALU.add)); own.settle()
            own.did(V.reciprocal(s_, s_)); own.settle()
            own.did(V.tensor_tensor(s_, s_, e, ALU.mult)); own.settle()
            own.did(V.tensor_tensor(s2, s_, s_, ALU.mult)); own.settle()
            own.did(V.tensor_scalar(acc, s2, 1.0 / 19, 1.0 / 17, ALU.mult, ALU.add)); own.settle()
            for n in (15, 13, 11, 9, 7, 5, 3, 1):
                own.did(V.tensor_tensor(acc, acc, s2, ALU.mult)); own.settle()
                own.did(V.tensor_scalar(acc, acc, 1.0 / n, None, ALU.add)); own.settle()
            own.did(V.tensor_tensor(acc, acc, s_, ALU.mult)); own.settle()
            own.did(V.tensor_scalar(tiny[5], pcol("lam"), -1.0, 0.0, ALU.mult, ALU.max)); own.settle()
            own.did(V.scalar_tensor_tensor(tiny[5], acc, 2.0, tiny[5], ALU.mult, ALU.add)); own.settle()
            V.tensor_scalar(decay, tiny[5], LRU_C, None, ALU.mult)
            V.tensor_scalar(ndecay, tiny[5], -LRU_C, None, ALU.mult).then_inc(s_lam, 1)

            def add_mod(slot, uses, q, kk, n, first=False):
                dve.wait_ge(s_m[slot], uses * 16)
                if not first:
                    dve.wait_ge(s_modacc, n)
                col = csil[:, kk:kk + 1] if isinstance(kk, int) else csil[:, bass.ds(kk, 1)]
                if first:
                    V.tensor_scalar(mod_acc[:, q], mod_ring[:, slot], col, None, ALU.mult).then_inc(s_modacc, 1)
                else:
                    V.scalar_tensor_tensor(mod_acc[:, q], mod_ring[:, slot], col, mod_acc[:, q], ALU.mult,
                                           ALU.add).then_inc(s_modacc, 1)

            add_mod(0, 1, 0, 0, 0, first=True)
            add_mod(1, 1, 1, 0, 0, first=True)
            add_mod(2, 1, 0, 1, 1)
            add_mod(3, 1, 1, 1, 2)
            mean_root([(7, D)], 1)
            V.tensor_tensor(hid[:], res[:], rstd[:, 0:1, :].to_broadcast([P, KD, T]), ALU.mult).then_inc(s_xn, 1)
            dve.wait_ge(s_relps, 1)
            dve.wait_ge(s_cst, 16)
            V.tensor_tensor(relbias, banks(2, T, 8)[:, :, 0:SWA_H].rearrange("p j h -> p h j"),
                            ccol("bar").unsqueeze(1).to_broadcast([P, SWA_H, T]), ALU.add).then_inc(s_dve, 1)
            own.n += 1
            with dve.Fori(1, MOD_FIRST // 4) as i:
                for j in range(4):
                    add_mod(j, i + 1, j % 2, i * 2 + j // 2, i * 4 + (j - 1))
            dve.wait_ge(s_modcol, 1)
            mc = banks(6, 4, KD)
            own.did(V.tensor_tensor(modv[:, 1, :], mc[:, 0, :], pcol("b_mod", KD, KD), ALU.add))
            V.tensor_tensor(modv[:, 0, :], mc[:, 1, :], pcol("b_mod", 0, KD), ALU.add).then_inc(s_modread, 1)
            own.settle()
            dve.wait_ge(s_modread, 1)
            V.scalar_tensor_tensor(coef[:, 0, :], modv[:, 1, :], 1.0, pcol("norm_mix"), ALU.add, ALU.mult).then_inc(s_coef, 1)
            for q in range(4):
                add_mod(q, 9, q, 0, 0, first=True)
            for kk in (1, 2):
                for q in range(4):
                    add_mod(q, 9 + kk, q, kk, MOD_FIRST + kk * 4 + q - 3)
            with dve.Fori(1, 5) as i:
                for j in range(12):
                    add_mod(j % 4, i * 3 + (9 + j // 4), j % 4, i * 3 + j // 4, i * 12 + (MOD_FIRST + j - 3))
            for q in range(4):
                add_mod(q, 24, q, 15, MOD_FIRST + 60 + q - 3)
            dve.wait_ge(s_modcol, 2)
            V.tensor_tensor(modv[:, 2:6, :], mc, pcol("b_mod", 2 * KD).rearrange("p (a b) -> p a b", a=4),
                            ALU.add).then_inc(s_modread, 1)
            dve.wait_ge(s_modread, 2)
            V.scalar_tensor_tensor(coef[:, 1, :], modv[:, 4, :], 1.0, pcol("norm_ffn"), ALU.add, ALU.mult).then_inc(s_coef, 1)

            dve.wait_ge(s_wev, NZ)
            for n in range(LRU_N):
                own.did(V.tensor_scalar(cx[:, n, :], z[:, XA + n, :], pcol("conv_w", 3 * LRU_N + n, 1),
                                        pcol("conv_b", n, 1), ALU.mult, ALU.add))
            for j in (2, 1, 0):
                s = CONV_W - 1 - j
                own.settle()
                for n in range(LRU_N):
                    r = V.scalar_tensor_tensor(cx[:, n, s:T], z[:, XA + n, 0:T - s], pcol("conv_w", j * LRU_N + n, 1),
                                               cx[:, n, s:T], ALU.mult, ALU.add)
                    if j or n < LRU_N - 1:
                        own.did(r)
            r.then_inc(s_conv, 1)

            def swa(i, l, width):
                dve.wait_ge(s_sl, i + 1)
                src = banks((0, 2)[i], SWA_H, width)
                V.scalar_tensor_tensor(l, src, HEAD_SCALE, relbias[:, :, T - width:T], ALU.mult,
                                       ALU.add).then_inc(s_slr, 1)
                dve.wait_ge(s_slr, i + 1)
                top = stat[:, 0:SWA_H]
                own.did(V.tensor_reduce(top, l, AX.X, ALU.max)); own.settle()
                V.tensor_tensor(l, l, top.unsqueeze(2).to_broadcast([P, SWA_H, width]), ALU.subtract).then_inc(s_sm, 1)
                dve.wait_ge(s_se, i + 1)
                times = ccol("times")[:, T - width:T].unsqueeze(1).to_broadcast([P, SWA_H, width])
                own.did(V.tensor_tensor(l, l, times, ALU.mult)); own.settle()
                tot = stat[:, 8:8 + SWA_H]
                own.did(V.tensor_reduce(tot, l, AX.X, ALU.add)); own.settle()
                own.did(V.reciprocal(tot, tot)); own.settle()
                V.tensor_tensor(l, l, tot.unsqueeze(2).to_broadcast([P, SWA_H, width]), ALU.mult).then_inc(s_sp, 1)

            swa(0, l0, P)
            swa(1, l1, T)

            dve.wait_ge(s_a2, 1)
            dve.wait_ge(s_th, 1)
            own.did(V.tensor_tensor(ig, ig, cx, ALU.mult))
            asq = z[:, XA:XA + LRU_N]
            dve.wait_ge(s_conv, 1)
            own.did(V.tensor_tensor(asq, rg, rg, ALU.mult)); own.settle()
            V.scalar_tensor_tensor(th, asq, 1.0, th, ALU.add, ALU.mult).then_inc(s_var, 1)
            dve.wait_ge(s_sqrt, 1)
            own.did(V.tensor_tensor(ig, ig, th, ALU.mult)); own.settle()
            for n in range(LRU_N):
                own.did(V.tensor_tensor_scan(th[:, n, :], rg[:, n, :], ig[:, n, :], 0.0, ALU.mult, ALU.add))
            own.settle()
            dve.wait_ge(s_gelu, 1)
            V.tensor_tensor(hid[:, 0:LRU_N], th, z[:, GA:GA + LRU_N], ALU.mult).then_inc(s_y, 1)

            dve.wait_ge(s_bz, 1)
            V.tensor_scalar(zs0, banks(6, SB_H, T), HEAD_SCALE, None, ALU.mult).then_inc(s_bzr, 1)
            V.tensor_scalar(zs1, banks(5, SB_H, P), HEAD_SCALE, None, ALU.mult).then_inc(s_bzr, 1)
            dve.wait_ge(s_spt, 2)
            for i, (s, z_, e_, w) in enumerate(((sp0, zs0, e0, T), (sp1, zs1, e1, P))):
                mask = ccol("strict")[:, 0:w].unsqueeze(1).to_broadcast([P, SB_H, w])
                dve.wait_ge(s_bln, i + 1)
                own.did(V.scalar_tensor_tensor(s, z_, 0.0, e_, ALU.max, ALU.add)); own.settle()
                own.did(V.tensor_tensor(z_, z_, s, ALU.subtract))
                own.settle()
                V.tensor_tensor(s, s, mask, ALU.mult).then_inc(s_bsp, 1)
            dve.wait_ge(s_baf, 1)
            for e_, z_, ps_ in ((e0, zs0, banks(6, SB_H, T)), (e1, zs1, banks(5, SB_H, P))):
                V.tensor_tensor(e_, z_, ps_, ALU.subtract).then_inc(s_bx, 1)
            for i, (e_, w) in enumerate(((e0, T), (e1, P))):
                mask = ccol("strict")[:, 0:w].unsqueeze(1).to_broadcast([P, SB_H, w])
                dve.wait_ge(s_bex, i + 1)
                V.tensor_tensor(e_, e_, mask, ALU.mult).then_inc(s_bp, 1)
            dve.wait_ge(s_so, 1)
            V.tensor_copy(hid[:, 6:12], banks(0, SWA_H, T)).then_inc(s_y, 1)
            dve.wait_ge(s_bo, 1)
            V.tensor_copy(hid[:, 12:16], banks(3, SB_H, T)).then_inc(s_y, 1)
            mean_root([(5, 768), (6, 768), (7, 512)], 2)
            for kk in range(KD):
                V.scalar_tensor_tensor(hid[:, kk, :], hid[:, kk, :], pcol("gnorm", kk, 1),
                                       rstd[:, 0 if kk < 6 else 1 if kk < 12 else 2, :], ALU.mult,
                                       ALU.mult).then_inc(s_y, 1)
            with dve.Fori(0, 4) as i:
                for j in range(4):
                    dve.wait_ge(s_wmm, i * 4 + (N_OUT + j + 1))
                    x_ = res[:, bass.ds(i * 4 + j, 1), :].rearrange("p o t -> p (o t)")
                    V.scalar_tensor_tensor(x_, ps_w[(N_OUT + j) % 2], modv[:, 2, bass.ds(i * 4 + j, 1)], x_, ALU.mult,
                                           ALU.add).then_inc(s_wev, 1)
            mean_root([(7, D)], 3)
            V.tensor_tensor(hid[:], res[:], rstd[:, 0:1, :].to_broadcast([P, KD, T]), ALU.mult).then_inc(s_xn, 2)

            top_v = tk[:, 0:2 * P].rearrange("p (a b) -> p a b", a=HC)
            top_i = tk[:, 2 * P:4 * P].bitcast(U32).rearrange("p (a b) -> p a b", a=HC)
            top_f = tk[:, 4 * P:6 * P].rearrange("p (a b) -> p a b", a=HC)
            best_i = tk[:, 6 * P:7 * P].bitcast(I32).rearrange("p (a b) -> p a b", a=PEER_H)
            half_i = tk[:, 7 * P:8 * P].bitcast(I32).rearrange("p (a b) -> p a b", a=PEER_H)
            half_f = tk[:, 8 * P:9 * P].rearrange("p (a b) -> p a b", a=PEER_H)
            quad = [P, PEER_H, TOPK, TOPK]

            def top16(vals, idx, src, left_):
                n = src.shape[1]
                for v in range(n):
                    own.did(V.max(vals[:, v, 0:8], src[:, v, :]))
                own.settle()
                for v in range(n):
                    own.did(V.match_replace(left_[:, v, :], vals[:, v, 0:8], src[:, v, :], TAKEN))
                    own.did(V.max_index(idx[:, v, 0:8], vals[:, v, 0:8], src[:, v, :]))
                own.settle()
                for v in range(n):
                    own.did(V.max(vals[:, v, 8:16], left_[:, v, :]))
                own.settle()
                for v in range(n):
                    own.did(V.max_index(idx[:, v, 8:16], vals[:, v, 8:16], left_[:, v, :]))
                own.settle()

            for tt in range(TT):
                dve.wait_ge(s_scr, tt + 1)
                sc = score[:, tt]
                top16(top_v, top_i, sc, left)
                own.did(V.tensor_copy(top_f, top_i))
                tv = top_v.rearrange("p (h c) k -> p h c k", c=2)
                tf = top_f.rearrange("p (h c) k -> p h c k", c=2)
                c4 = cand.rearrange("p h (i j) -> p h i j", i=TOPK)
                own.did(V.tensor_tensor(c4, tv[:, :, 0].unsqueeze(3).to_broadcast(quad),
                                        tv[:, :, 1].unsqueeze(2).to_broadcast(quad), ALU.add))
                own.settle()
                outs = [tk[:, (9 + 3 * tt + i) * P:(10 + 3 * tt + i) * P].rearrange("p (a b) -> p a b", a=PEER_H)
                        for i in range(3)]
                gate = outs[2]
                top16(gate, best_i.bitcast(U32), cand, cleft)
                e4 = eqs.rearrange("p h (i j) -> p h i j", i=TOPK)
                iota4 = ccol("iota")[:, 0:TOPK].unsqueeze(1).unsqueeze(1).to_broadcast(quad)
                for c in range(2):
                    if c == 0:
                        own.did(V.tensor_scalar(half_i, best_i, 4, None, ALU.arith_shift_right))
                    else:
                        own.did(V.tensor_scalar(half_i, best_i, TOPK - 1, None, ALU.bitwise_and))
                    own.settle()
                    own.did(V.tensor_copy(half_f, half_i)); own.settle()
                    own.did(V.tensor_tensor(e4, iota4, half_f.unsqueeze(3).to_broadcast(quad), ALU.is_equal)); own.settle()
                    own.did(V.tensor_tensor(e4, e4, tf[:, :, c].unsqueeze(2).to_broadcast(quad), ALU.mult)); own.settle()
                    own.did(V.tensor_reduce(outs[c], e4, AX.X, ALU.add)); own.settle()
                tri = [P, PEER_H, TOPK]
                own.did(V.tensor_copy(stat[:, 0:PEER_H], gate[:, :, 0])); own.settle()
                V.tensor_tensor(gate, gate, stat[:, 0:PEER_H].unsqueeze(2).to_broadcast(tri), ALU.subtract).then_inc(s_gx, 1)
                dve.wait_ge(s_ge, tt + 1)
                own.did(V.tensor_reduce(stat[:, 8:8 + PEER_H], gate, AX.X, ALU.add)); own.settle()
                own.did(V.reciprocal(stat[:, 8:8 + PEER_H], stat[:, 8:8 + PEER_H])); own.settle()
                V.tensor_tensor(gate, gate, stat[:, 8:8 + PEER_H].unsqueeze(2).to_broadcast(tri), ALU.mult).then_inc(s_pk, 1)

            dve.wait_ge(s_pkr, 2)

            def one_hots(r_, t0, n, first=False):
                if not first:
                    dve.wait_ge(s_gmm, n - 1)
                for t in range(GT):
                    def at(i):
                        return picks[:, i, bass.ds(t0 + t, 1)]
                    V.tensor_scalar(hot_a[:, r_, t, :], ccol("iota"), at(0), None, ALU.is_equal)
                    r = V.tensor_scalar(hot_b[:, r_, t, :], ccol("iota"), at(1), at(2), ALU.is_equal, ALU.mult)
                r.then_inc(s_hot, 1)

            one_hots(0, 0, 0, True)
            one_hots(1, GT, 1, True)
            with dve.Fori(1, T // GT // 2) as i:
                for r_ in range(2):
                    one_hots(r_, i * (2 * GT) + r_ * GT, i * 2 + r_)
            own.did(V.memset(yacc, 0.0)); own.settle()

            def weights(half, n):
                for j in range(GB):
                    if j == 0:
                        dve.wait_ge(s_g[half], (n - half) * 16 + 32)
                    dve.wait_ge(s_wev, n * GB + (N_U + j + 1))
                    V.tensor_tensor(pring[:, half, j, :], act_u[:, j % 2, :], gring[:, half, j, :],
                                    ALU.mult).then_inc(s_pw, 1)

            def add_y(n):
                for u in range(8):
                    dve.wait_ge(s_vmm, n * 8 + (u + 1))
                    y_ = yacc[:, u // 4, (u % 4) * 512:(u % 4 + 1) * 512]
                    if not isinstance(n, int) or n:
                        dve.wait_ge(s_yadd, n * 8 + (u - 7))
                    V.tensor_tensor(y_, y_, banks(2 + u % 4, 512), ALU.add).then_inc(s_yadd, 1)

            weights(0, 0)
            weights(1, 1)
            add_y(0)
            with dve.Fori(0, NG // 2 - 1) as i:
                for g in range(2):
                    weights(g, i * 2 + (2 + g))
                    add_y(i * 2 + (1 + g))
            add_y(NG - 1)
            for kk in range(KD):
                dve.wait_ge(s_yt, kk + 1)
                V.scalar_tensor_tensor(res[:, kk, :], banks(kk % 2, T), modv[:, 5, kk:kk + 1], res[:, kk, :], ALU.mult,
                                       ALU.add).then_inc(s_x2, 1)
            mean_root([(7, D)], 4)
            for kk in range(KD):
                V.scalar_tensor_tensor(res[:, kk, :], res[:, kk, :], pcol("final_norm", kk, 1), rstd[:, 0, :],
                                       ALU.mult, ALU.mult).then_inc(s_o, 1)

        @block.gpsimd
        def _(pool):
            pool.wait_ge(s_o, KD)
            pool.dma_start(out, res[:]).then_inc(s_st, 16)
            pool.wait_ge(s_st, 16)


def t5_bucket(dist):
    exact = BUCKETS // 2
    large = exact + (np.log(np.maximum(dist, 1) / exact) / np.log(MAX_DIST / exact) * (BUCKETS - exact)).astype(np.int32)
    return np.where(dist < exact, dist, np.minimum(large, BUCKETS - 1))


def constants():
    p = np.arange(P)[:, None]
    cst = np.zeros((P, N_CST), np.float32)

    def put(name, value):
        a, w = CST[name]
        cst[:, a:a + w] = value

    put("ident", np.eye(P))
    put("iota", np.arange(P)[None, :])
    put("after", p > np.arange(P)[None, :])
    put("strict", p < np.arange(T)[None, :])
    dist = p + P - np.arange(T)[None, :]
    times = sum(((dist >= 0) & (dist % d == 0) & (dist <= w)).astype(np.float32) for w, d in PATTERNS)
    put("times", times)
    put("bar", np.where(times > 0, 0.0, NEG_INF))
    dist = np.arange(N_SHIFT) - (P - 1)
    shifts = ((t5_bucket(np.maximum(dist, 0))[None, :] == np.arange(BUCKETS)[:, None]) & (dist >= 0)[None, :])
    return cst, shifts.astype(np.float32)


def kernel(x, c, w_mod, b_mod, norm_mix, norm_ffn, w_in, conv_w, conv_b, lru_w_rec, lru_b_rec, lru_w_in, lru_b_in,
           lru_lambda, rel_bias, gnorm_lru, gnorm_swa, gnorm_sb, w_out, peer_wq, peer_subkeys, peer_u, peer_v,
           final_norm):
    import concourse.bacc as bacc
    from concourse.bass_utils import run_bass_kernel_spmd

    A = np.asarray

    def cols(v):
        return A(v).reshape(-1, P).T

    par = np.concatenate([cols(c), cols(norm_mix), cols(norm_ffn), cols(final_norm), cols(b_mod), cols(conv_w),
                          cols(conv_b), cols(lru_b_rec), cols(lru_b_in), cols(lru_lambda), cols(gnorm_lru),
                          cols(gnorm_swa), cols(gnorm_sb)], axis=1)
    cst, shifts = constants()

    def chunks(w):
        return A(w).reshape(KD, P, -1, P).transpose(2, 1, 0, 3)

    u_blocks = A(peer_u)[0].reshape(P, NB, KD, P).transpose(1, 3, 2, 0)
    wst = np.concatenate([chunks(A(w_in)[0]), chunks(A(w_out)[0]), chunks(A(peer_wq)[0]), u_blocks], axis=0)
    wm = A(w_mod)[0].reshape(KD, P, 6, D).transpose(0, 2, 1, 3)
    wmod = np.concatenate([wm[:, [1, 0]].reshape(-1, P, D), wm[:, 2:6].reshape(-1, P, D)], axis=0)
    arrays = {
        "xT": A(x)[0].T.reshape(KD, P, T).transpose(1, 0, 2),
        "par": par,
        "cst": cst,
        "shifts": shifts,
        "relb": A(rel_bias),
        "wmod": wmod,
        "wst": wst,
        "lruw": np.stack([A(lru_w_rec)[0], A(lru_w_in)[0]]).transpose(2, 0, 1, 3),
        "subk": A(peer_subkeys)[0].reshape(HC, P, P).transpose(2, 0, 1),
        "vtab": A(peer_v)[0].reshape(P, NB, D).transpose(1, 0, 2),
    }
    arrays = {k: np.ascontiguousarray(v) for k, v in arrays.items()}
    nc = bacc.Bacc("TRN2", target_bir_lowering=False, num_devices=1)
    aps = {k: nc.dram_tensor(k, v.shape, mybir.dt.from_np(v.dtype), kind="ExternalInput").ap() for k, v in arrays.items()}
    gates = nc.dram_tensor("gates_dram", (TT, P, NB, P), F32, kind="Internal").ap()
    out = nc.dram_tensor("out", (P, KD, T), F32, kind="ExternalOutput").ap()
    hybrid_block(nc, **aps, gates_dram=gates, out=out)
    r = run_bass_kernel_spmd(nc, [arrays], core_ids=[0])
    y = r.results[0]["out"]
    return y.transpose(1, 0, 2).reshape(D, T).T.reshape(1, T, D)
```

```python
import math
from contextlib import ExitStack

import concourse.bass as bass
import numpy as np
from concourse import mybir

P = 128
F32 = mybir.dt.float32
F32R = mybir.dt.float32r
I32 = mybir.dt.int32
U32 = mybir.dt.uint32
ALU = mybir.AluOpType
ACT = mybir.ActivationFunctionType
AX = mybir.AxisListType

T = 256
TT = T // P
D = 2048
KD = D // P
EPS = 1e-6
LRU_N, SWA_H, SB_H = 6, 6, 4
CONV_W = 4
LRU_C = 8.0
HEAD_SCALE = 128.0 ** -0.5
PATTERNS = ((128, 1), (512, 4), (2048, 16))
BUCKETS, MAX_DIST = 32, 2048
NEG_INF = -1e30
TAKEN = -3.0e38
PEER_H, TOPK = 8, 16
HC = 2 * PEER_H
NB = 128

XA, QC, KC, VC, QB, KB, VB, GA, NZ = 0, 6, 10, 14, 18, 24, 30, 36, 42
N_OUT = NZ
N_WQ = N_OUT + KD
N_U = N_WQ + KD
W_RING = 4
M_G1 = 2 * KD
M_H2 = M_G1 + KD
M_G2 = M_H2 + 2 * KD
M_ALL = M_G2 + KD
M_RING = 2
M_RING0 = 4
GB = 2
FIRST = 12
EARLY = 20
LAG = 24
NV = NB // GB
assert LAG % (4 * GB) == 0
TAILS = LAG // GB // 4
V_TAIL = NV - 4 * TAILS + 2
GT = 4
TQ = 4
TW = T // TQ
SPREADS = T // GT
HOT_RING = 4

PAR = {}
_at = 0
for _name, _n in (("c", KD), ("norm_mix", KD), ("norm_ffn", KD), ("final_norm", KD), ("b_mod", 6 * KD),
                  ("conv_w", CONV_W * LRU_N), ("conv_b", LRU_N), ("b_rec", LRU_N), ("b_in", LRU_N),
                  ("lam", LRU_N), ("gnorm", LRU_N + SWA_H + SB_H)):
    PAR[_name] = (_at, _n)
    _at += _n
N_PAR = _at
CST = {"ident": (0, P), "iota": (P, P)}
N_CST = 2 * P
MIX = {"after": (0, P), "strict": (P, T), "bar": (P + T, T), "times": (P + 2 * T, T)}
N_MIX = P + 3 * T
N_SHIFT = T + P - 1


class Steps:

    def __init__(self, engine, sem):
        self.engine, self.sem, self.n = engine, sem, 0

    def did(self, ins):
        ins.then_inc(self.sem, 1)
        self.n += 1
        return self.n

    def settle(self, n=None):
        self.engine.wait_ge(self.sem, self.n if n is None else n)


def hybrid_block(nc, xT, par, cst, mixc, shifts, relb, wmod, wst, lruw, subk, vtab, gates_dram, res_dram, out):
    ctx = ExitStack()
    with ctx:
        def sem(name):
            return ctx.enter_context(nc.semaphore(name))

        base = (nc.sbuf_base + 31) // 32 * 32
        size = (nc.sbuf_usable_end - base) // 4 - 8
        ctx.enter_context(nc.sbuf_tensor("slab", [P, size], F32))

        def at(name, kb, shape, dt=F32):
            assert kb * 256 + int(np.prod(shape)) <= size, name
            return nc.alloc_sbuf_tensor_at(name, [P, *shape], dt, offset=base + int(kb * 1024))

        par_sb = at("par_sb", 0, [N_PAR])
        cst_sb = at("cst_sb", 1, [N_CST])
        ones = at("ones", 2, [P])
        small = at("small", 2.5, [256])
        modv = at("modv", 3.5, [6, KD])
        coef = at("coef", 4, [2, KD])
        ms = at("ms", 4.25, [3, T])
        rstd = at("rstd", 7.25, [3, T])
        picks = at("picks", 10.25, [3, T])
        wraw = at("wraw", 13.5, [W_RING, KD, P])
        wlo = at("wlo", 13.5, [W_RING, KD, P], F32R)
        hid = at("hid", 45.5, [KD, T])
        res = at("res", 157.5, [KD, T])
        squares0 = at("squares0", 61.5, [KD, T])
        mod_ring0 = at("mod_ring0", 77.5, [M_RING0, D])
        shifts_sb = at("shifts_sb", 127.5, [N_SHIFT])
        relb_sb = at("relb_sb", 130, [SWA_H])
        z = at("z", 61.5, [NZ, T])
        cx = at("cx", 103.5, [LRU_N, T])
        rg = at("rg", 109.5, [LRU_N, T])
        ig = at("ig", 115.5, [LRU_N, T])
        th = at("th", 121.5, [LRU_N, T])
        vs = at("vs", 127.5, [TT, SWA_H + SB_H, P])
        l0 = at("l0", 137.5, [SWA_H, P])
        l1 = at("l1", 140.5, [SWA_H, T])
        relbias = at("relbias", 146.5, [SWA_H, T])
        mix_sb = at("mix_sb", 152.5, [N_MIX])
        mod_ring = at("mod_ring", 173.5, [M_RING, D])
        mod_acc = at("mod_acc", 189.5, [3, D])
        lw = at("lw", 213.5, [2, LRU_N, P])
        zs0, zs1 = at("zs0", 103.5, [SB_H, T]), at("zs1", 107.5, [SB_H, P])
        e0, e1 = at("e0", 109.5, [SB_H, T]), at("e1", 113.5, [SB_H, P])
        sp0, sp1 = at("sp0", 115.5, [SB_H, T]), at("sp1", 119.5, [SB_H, P])
        yc = at("yc", 61.5 + QC, [SB_H, T])
        pt0 = at("pt0", 61.5 + QB, [SWA_H, T])
        pt1 = at("pt1", 61.5 + KB, [SWA_H, P])
        squares1 = at("squares1", 103.5, [KD, T])
        sq_ring = at("sq_ring", 61.5, [4, T])
        qry = at("qry", 66.5, [4, T])
        k = 77.5
        score = at("score", k, [TT, HC, P]); k += 16
        left = at("left", k, [TT, HC, P]); k += 16
        cand = at("cand", k, [PEER_H, T]); k += 8
        cleft = at("cleft", k, [PEER_H, T]); k += 8
        eqs = at("eqs", k, [PEER_H, T]); k += 8
        subk_sb = at("subk_sb", k, [HC, P]); k += 8
        top_v = at("top_v", k, [TT, HC, TOPK]); k += 2
        top_i = at("top_i", k, [TT, HC, TOPK], U32); k += 2
        top_f = at("top_f", k, [TT, HC, TOPK]); k += 2
        best_i = at("best_i", k, [PEER_H, TOPK], I32); k += 0.5
        half_i = at("half_i", k, [PEER_H, TOPK], I32); k += 0.5
        half_f = at("half_f", k, [PEER_H, TOPK]); k += 0.5
        pick_t = at("pick_t", k, [TT, 3, PEER_H, TOPK]); k += 3
        assert k <= 157.5
        gstage = at("gstage", 93.5, [2, NB, TW])
        hot_a = at("hot_a", 173.5, [HOT_RING, GT, P])
        hot_b = at("hot_b", 181.5, [HOT_RING, GT, P])
        h_hi = at("h_hi", 61.5, [KD, T], F32R)
        h_lo = at("h_lo", 157.5, [KD, T], F32R)
        whi = at("whi", 77.5, [W_RING, KD, P], F32R)
        vraw = at("vraw", 109.5, [2 * GB, D])
        vlo = at("vlo", 109.5, [2 * GB, D], F32R)
        vhi = [at("vhi01", 141.5, [2, D], F32R)[:, j] for j in range(2)]
        vhi += [at("vhi23", 45.5, [2, D], F32R)[:, j] for j in range(2)]
        yacc = at("yacc", 173.5, [D])
        gring = at("gring", 181.5, [2, TQ, GB, TW])
        praw = at("praw", 185.5, [2, GB, T])
        plo = at("plo", 185.5, [2, GB, T], F32R)
        phi = at("phi", 189.5, [2, GB, T], F32R)
        act_u = at("act_u", 193.5, [LAG, T])
        y0 = at("y0", 141.5, [D])
        res2 = at("res2", 109.5, [KD, T])
        squares3 = at("squares3", 61.5, [KD, T])

        ps = ctx.enter_context(nc.psum_tensor("ps", [P, 8, 512], F32))

        def banks(b, *shape):
            n = int(np.prod(shape))
            flat = ps[:, b:b + (n + 511) // 512, :].rearrange("p a b -> p (a b)")[:, 0:n]
            names = "abcd"[:len(shape)]
            if len(shape) == 1:
                return flat
            return flat.rearrange(f"p ({' '.join(names)}) -> p {' '.join(names)}",
                                  **{names[i]: shape[i] for i in range(1, len(shape))})

        ps_w = [banks(0, T), banks(1, T)]
        ps_modcol = banks(7, 3, KD)
        ps_gates = banks(2, 2, LRU_N, T)
        ps_vt = [banks(2, 4, P), banks(3, 4, P), banks(4, 4, P)]
        ps_bz0, ps_bz1 = banks(4, SB_H, T), banks(6, SB_H, P)
        ps_bo = banks(2, SB_H, T)
        ps_l1, ps_l0 = banks(5, SWA_H, T), banks(3, SWA_H, P)
        ps_pt0, ps_pt1 = banks(3, SWA_H, P), banks(5, 2, SWA_H, P)
        ps_so = banks(2, SWA_H, T)
        ps_ssq = [banks(5, 2, T)[:, 0], banks(5, 2, T)[:, 1], banks(6, T)]
        ps_sc = [banks(2 + i, TT, P) for i in range(4)]
        ps_spread = [banks(4 + i, GT, P) for i in range(HOT_RING)]
        ps_y0 = [banks(2 + i, 512) for i in range(4)]
        ps_y1 = [banks(6, 512), banks(7, 512)]

        def pcol(name, i=0, n=None):
            a, w = PAR[name]
            return par_sb[:, a + i:a + i + (w - i if n is None else n)]

        def mixcol(name, i=0):
            a, w = MIX[name]
            return mix_sb[:, a + i:a + w]

        ident, iota = cst_sb[:, 0:P], cst_sb[:, P:2 * P]
        csil = small[:, 0:KD]
        tiny = [small[:, 32 + 8 * i:32 + 8 * i + LRU_N] for i in range(8)]
        decay = small[:, 96:96 + LRU_N]
        ndecay = small[:, 104:104 + LRU_N]
        stat = small[:, 112:112 + 4 * 8]

        def tile_of(tensor, i):
            return tensor[:, bass.ds(i, 1)].rearrange("p o t -> p (o t)")

        s_par, s_cst, s_x, s_rel, s_lruw, s_subk = (sem(n) for n in (
            "par_loaded", "cst_loaded", "x_loaded", "rel_loaded", "lru_weights_loaded", "subkeys_loaded"))
        s_w = [sem(f"w_loaded{i}") for i in range(W_RING)]
        s_m0 = [sem(f"first_mod_loaded{i}") for i in range(M_RING0)]
        s_m = [sem(f"mod_loaded{i}") for i in range(M_RING)]
        s_v = [sem(f"v_loaded{i}") for i in range(2 * GB)]
        s_g = [sem(f"gates_loaded{i}") for i in range(2)]
        s_spill, s_back = sem("x1_stored"), sem("x1_loaded")
        s_dve, s_act = sem("dve_steps"), sem("act_steps")
        s_ones, s_silu_e, s_lam = sem("ones_set"), sem("silu_exp"), sem("lambda_steps")
        s_sq, s_ssq, s_ms, s_root = sem("squared"), sem("square_sums"), sem("mean_squares"), sem("roots")
        s_xn, s_coef, s_h = sem("x_normed"), sem("coef_ready"), sem("h_tiles")
        s_relps, s_relsb = sem("relbias_in_psum"), sem("relbias_ready")
        s_modacc, s_modcol, s_modread = sem("mod_tiles_added"), sem("mod_columns"), sem("mod_columns_read")
        s_wmm, s_wev = sem("chunk_products"), sem("chunks_evacuated")
        s_conv, s_gate, s_sig, s_a = sem("conv_done"), sem("gates_in_psum"), sem("sigmoids"), sem("a_and_tanh")
        s_var, s_sqrt, s_gelu = sem("lru_scale_squared"), sem("lru_scale"), sem("gate_branch_done")
        s_vt, s_vev = sem("v_transposed"), sem("v_evacuated")
        s_sl, s_slr, s_sm, s_se, s_sp = (sem("swa_logits"), sem("swa_logits_read"), sem("swa_shifted"),
                                         sem("swa_exp"), sem("swa_probs"))
        s_spt, s_spe, s_so = sem("swa_probs_transposed"), sem("swa_probsT_ready"), sem("swa_out")
        s_bz, s_bzr, s_bln, s_bsp = sem("sb_scores"), sem("sb_scores_read"), sem("sb_log"), sem("sb_softplus")
        s_baf, s_bx, s_bex, s_bp, s_bo = (sem("sb_after"), sem("sb_exponent"), sem("sb_expd"), sem("sb_weights"),
                                          sem("sb_out"))
        s_ya, s_yb, s_yc, s_y = sem("ya_ready"), sem("yb_ready"), sem("yc_ready"), sem("y_normed")
        s_sqk = sem("x1_tiles_squared")
        s_sc, s_scr = sem("peer_scores"), sem("peer_scores_read")
        s_gx, s_ge, s_pk, s_pkt, s_pkr = (sem("gate_shifted"), sem("gate_exp"), sem("picks_ready"),
                                          sem("picks_transposed"), sem("picks_read"))
        s_hot, s_gmm, s_gev = sem("one_hots"), sem("gates_spread"), sem("gates_staged")
        s_gst = [sem(f"gates_stored{q}") for q in range(TQ)]
        s_hhi, s_hlo = sem("h_hi_ready"), sem("h_lo_ready")
        s_whi, s_wlo, s_vhi, s_vlo = sem("w_hi_ready"), sem("w_lo_ready"), sem("v_hi_ready"), sem("v_lo_ready")
        s_pm, s_phi, s_plo = sem("weights_ready"), sem("weights_hi_ready"), sem("weights_lo_ready")
        s_y0mm, s_vmm, s_yadd = sem("y0_group_products"), sem("y1_products"), sem("y1_added")
        s_y0e, s_yt, s_x2, s_o, s_st = (sem("y0_evacuated"), sem("y_transposed"), sem("x2_tiles"), sem("out_tiles"),
                                        sem("out_stored"))

        block = ctx.enter_context(nc.Block())

        def stretch(engine, n0, n1, body, per=4):
            if n1 - n0 >= 2 * per:
                assert (n1 - n0) % per == 0
                with engine.Fori(0, (n1 - n0) // per) as i:
                    for j in range(per):
                        body((n0 + j) % per, i * per + (n0 + j), i, n0 + j)
            else:
                for n in range(n0, n1):
                    body(n % per, n, 0, n)

        def turns(i, n, ring, per=4):
            return i * (per // ring) + (n // ring + 1)

        @block.sync
        def _(sp):
            sp.dma_start(par_sb[:], par).then_inc(s_par, 16)
            sp.dma_start(res[:], xT).then_inc(s_x, 16)

            def load_mod0(slot, n):
                sp.dma_start(mod_ring0[:, slot], wmod[bass.ds(n, 1)].rearrange("o p n -> (o p) n")).then_inc(s_m0[slot], 16)

            def load_w(slot, n):
                sp.dma_start(wraw[:, slot], wst[bass.ds(n, 1)].rearrange("o p k c -> (o p) k c")).then_inc(s_w[slot], 16)

            for n in range(M_RING0):
                load_mod0(n, n)
            sp.dma_start(shifts_sb[0:BUCKETS], shifts).then_inc(s_rel, 16)
            sp.dma_start(relb_sb[0:BUCKETS], relb).then_inc(s_rel, 16)
            sp.dma_start(cst_sb[:], cst).then_inc(s_cst, 16)
            sp.dma_start(mix_sb[:], mixc).then_inc(s_cst, 16)

            def next_mod0(j, n, i, k):
                sp.wait_ge(s_modacc, n - M_RING0 + 1)
                load_mod0(j, n)

            stretch(sp, M_RING0, M_G1, next_mod0)
            for n in range(W_RING):
                load_w(n, n)
            sp.dma_start(lw[:], lruw).then_inc(s_lruw, 16)

            def next_w(j, n, i, k):
                sp.wait_ge(s_wmm, n - W_RING + 1)
                load_w(j, n)

            stretch(sp, W_RING, N_WQ - 2, next_w)
            stretch(sp, N_WQ - 2, N_WQ, next_w)
            sp.wait_ge(s_y, KD)
            sp.dma_start(subk_sb[:], subk).then_inc(s_subk, 16)
            stretch(sp, N_WQ, N_U + LAG, next_w)

            def load_v(j, n):
                sp.dma_start(vraw[:, j], vtab[bass.ds(n, 1)].rearrange("o p d -> (o p) d")).then_inc(s_v[j], 16)

            def load_g(half, n):
                sp.dma_start(gring[:, half].rearrange("p q b t -> p q (b t)"),
                             gates_dram[:, :, bass.ds(n * GB, GB), :].rearrange("q a b t -> a q (b t)")).then_inc(s_g[half], 16)

            for q in range(TQ):
                sp.wait_ge(s_gst[q], 16)
            for g in range(2):
                load_g(g, g)
                for j in range(GB):
                    load_v(g * GB + j, g * GB + j)

            def next_group(half, n):
                sp.wait_ge(s_pm, n - 1)
                load_g(half, n)
                sp.wait_ge(s_vmm, n * 4 - 4)
                for j in range(GB):
                    load_v(half * GB + j, n * GB + j)

            lead = LAG + W_RING
            stretch(sp, N_U + LAG, N_U + lead, next_w)
            with sp.Fori(0, (NB - lead) // 4) as i:
                for g in range(2):
                    for j in range(GB):
                        n = N_U + lead + g * GB + j
                        sp.wait_ge(s_wmm, i * 4 + (n - W_RING + 1))
                        load_w(n % W_RING, i * 4 + n)
                    next_group(g, i * 2 + (2 + g))
            def load_tail(slot, n):
                sp.dma_start(wraw[:, slot].rearrange("p k c -> p (k c)"),
                             vtab[bass.ds(n, 1)].rearrange("o p d -> (o p) d")).then_inc(s_w[slot], 16)

            for g in range(2):
                for j in range(GB):
                    m = N_U + NB + g * GB + j
                    sp.wait_ge(s_wmm, m - W_RING + 1)
                    load_tail(m % W_RING, (V_TAIL + g) * GB + j)
                next_group(g, V_TAIL - 2 + g)
            with sp.Fori(0, TAILS - 1) as i:
                for g in range(2):
                    n = V_TAIL - 2 + g
                    sp.wait_ge(s_pm, i * 4 + (n + 1))
                    load_g(g, i * 4 + (n + 2))
                    sp.wait_ge(s_vmm, i * 16 + (n + 1) * 4)
                    for j in range(GB):
                        load_v(g * GB + j, i * (4 * GB) + ((n + 4) * GB + j))
                for g in range(2):
                    n = V_TAIL + g
                    sp.wait_ge(s_pm, i * 4 + (n + 1))
                    load_g(g, i * 4 + (n + 2))
                    sp.wait_ge(s_vmm, i * 16 + (n + 1) * 4)
                    for j in range(GB):
                        load_tail((N_U + NB + g * GB + j) % W_RING, i * (4 * GB) + ((n + 4) * GB + j))
            for g in range(2):
                sp.wait_ge(s_pm, NV - 3 + g)
                load_g(g, NV - 2 + g)

        @block.tensor
        def _(pe):
            mm = nc.tensor.matmul
            flip = nc.tensor.transpose

            def chunk(j, n, i, k, evac=True, between=None):
                pe.wait_ge(s_w[j], turns(i, k, W_RING) * 16)
                if evac:
                    pe.wait_ge(s_wev, n - 1)
                for kk in range(KD):
                    r = mm(ps_w[k % 2], wraw[:, j, kk, :], hid[:, kk, :], start=(kk == 0), stop=(kk == KD - 1))
                    if kk == KD - 1:
                        r.then_inc(s_wmm, 1)
                    if between:
                        between(kk)

            def sum_squares(dst, sq, tiles):
                for i, kk in enumerate(tiles):
                    r = mm(dst, ones[:], sq[:, kk, :], start=(i == 0), stop=(i == len(tiles) - 1))
                r.then_inc(s_ssq, 1)

            pe.wait_ge(s_ones, 1)
            pe.wait_ge(s_sq, 1)
            sum_squares(banks(7, T), squares0, range(KD))
            pe.wait_ge(s_rel, 32)
            rb = banks(2, T, 8)
            for j in range(T):
                r = mm(rb[:, j, 0:SWA_H], shifts_sb[0:BUCKETS, T - 1 - j:T - 1 - j + P], relb_sb[0:BUCKETS, :],
                       start=True, stop=True)
            r.then_inc(s_relps, 1)

            def mod_columns(accs):
                for q in accs:
                    for kk in range(KD):
                        r = mm(ps_modcol[:, q, kk:kk + 1], mod_acc[:, q, kk * P:(kk + 1) * P], ones[:, 0:1],
                               start=True, stop=True)
                r.then_inc(s_modcol, 1)

            pe.wait_ge(s_ms, 1)
            pe.wait_ge(s_modacc, M_G1)
            mod_columns((0, 1))
            pe.wait_ge(s_h, KD)
            chunk(0, 0, 0, 0, evac=False)
            chunk(1, 1, 0, 1, evac=False)
            stretch(pe, 2, 10, chunk)
            pe.wait_ge(s_lruw, 16)
            pe.wait_ge(s_conv, 1)
            pe.wait_ge(s_relsb, 1)
            pe.wait_ge(s_modread, 1)
            for g in range(2):
                for n in range(LRU_N):
                    r = mm(ps_gates[:, g, n, :], lw[:, g, n, :], cx[:, n, :], start=True, stop=True)
                r.then_inc(s_gate, 1)
            stretch(pe, 10, 18, chunk)

            def turn_values(first, rounds):
                for g, (z0, h0) in enumerate(rounds):
                    for i in range(4):
                        tt, h = first[g][i]
                        r = flip(ps_vt[g][:, i, :], z[:, z0 + h, tt * P:(tt + 1) * P], ident)
                    r.then_inc(s_vt, 1)

            pe.wait_ge(s_sig, 2)
            pe.wait_ge(s_wev, 18)
            for h in range(SB_H):
                mm(ps_bz0[:, h, :], z[:, KC + h, 0:P], z[:, QC + h, :], start=True, stop=True)
            for h in range(SB_H):
                r = mm(ps_bz1[:, h, :], z[:, KC + h, P:T], z[:, QC + h, P:T], start=True, stop=True)
            r.then_inc(s_bz, 1)
            turn_values([[(0, h) for h in range(4)], [(1, h) for h in range(4)]], [(VC, SWA_H)] * 2)
            stretch(pe, 18, 26, chunk)
            pe.wait_ge(s_bsp, 2)
            for h in range(SB_H):
                mm(ps_bz0[:, h, :], mixcol("after"), sp0[:, h, :], start=True, stop=False, skip_group_check=True)
                mm(ps_bz0[:, h, P:T], ones[:], sp1[:, h, :], start=False, stop=True, skip_group_check=True)
            for h in range(SB_H):
                r = mm(ps_bz1[:, h, :], mixcol("after"), sp1[:, h, :], start=True, stop=True)
            r.then_inc(s_baf, 1)
            stretch(pe, 26, 30, chunk)
            pe.wait_ge(s_bp, 2)
            pe.wait_ge(s_vev, 2)
            for h in range(SB_H):
                mm(ps_bo[:, h, :], vs[:, 0, SWA_H + h, :], e0[:, h, :], start=True, stop=False, skip_group_check=True)
                r = mm(ps_bo[:, h, P:T], vs[:, 1, SWA_H + h, :], e1[:, h, :], start=False, stop=True,
                       skip_group_check=True)
            r.then_inc(s_bo, 1)
            pe.wait_ge(s_wev, 30)
            pe.wait_ge(s_bx, 2)
            for h in range(SWA_H):
                r = mm(ps_l1[:, h, :], z[:, QB + h, P:T], z[:, KB + h, :], start=True, stop=True)
            r.then_inc(s_sl, 1)
            pe.wait_ge(s_yc, 1)
            for h in range(SWA_H):
                r = mm(ps_l0[:, h, :], z[:, QB + h, 0:P], z[:, KB + h, 0:P], start=True, stop=True)
            r.then_inc(s_sl, 1)
            stretch(pe, 30, 36, chunk)
            pe.wait_ge(s_wev, 36)
            pe.wait_ge(s_slr, 2)
            turn_values([[(0, h) for h in range(4)], [(0, 4), (0, 5), (1, 0), (1, 1)], [(1, h) for h in range(2, 6)]],
                        [(VB, 0)] * 3)
            stretch(pe, 36, 40, chunk)
            pe.wait_ge(s_vev, 5)
            pe.wait_ge(s_sp, 2)
            for h in range(SWA_H):
                r = flip(ps_pt0[:, h, :], l0[:, h, :], ident)
            r.then_inc(s_spt, 1)
            for kt in range(2):
                for h in range(SWA_H):
                    r = flip(ps_pt1[:, kt, h, :], l1[:, h, kt * P:(kt + 1) * P], ident)
            r.then_inc(s_spt, 1)
            stretch(pe, 40, 42, chunk)
            pe.wait_ge(s_spe, 2)
            for h in range(SWA_H):
                mm(ps_so[:, h, :], vs[:, 0, h, :], pt0[:, h, :], start=True, stop=False, skip_group_check=True)
                r = mm(ps_so[:, h, P:T], vs[:, 1, h, :], pt1[:, h, :], start=False, stop=True, skip_group_check=True)
            r.then_inc(s_so, 1)
            pe.wait_ge(s_modacc, M_G2)
            mod_columns((0, 1, 2))
            pe.wait_ge(s_sq, 2)
            sum_squares(ps_ssq[2], squares1, range(12, 16))
            pe.wait_ge(s_sq, 3)
            sum_squares(ps_ssq[0], squares1, range(0, 6))
            pe.wait_ge(s_sq, 4)
            sum_squares(ps_ssq[1], squares1, range(6, 12))
            pe.wait_ge(s_y, KD)

            def x1_square(tile, n, first=False, last=False):
                pe.wait_ge(s_sqk, n)
                r = mm(banks(7, T), ones[:], sq_ring[:, tile % 4, :], start=first, stop=last, skip_group_check=True)
                return r

            def out_chunk(j, n, i, k):
                chunk(j, n, i, k)
                if k > N_OUT:
                    r = x1_square((k - N_OUT - 1) % 4, n - N_OUT, first=(k == N_OUT + 1 and isinstance(n, int)))
                    r.then_inc(s_ssq, 1)

            pe.wait_ge(s_modread, 2)
            for n in range(N_OUT, N_OUT + 4):
                out_chunk(n % 4, n, 0, n)
            stretch(pe, N_OUT + 4, N_WQ, out_chunk)
            x1_square(3, KD, last=True).then_inc(s_ssq, 1)
            pe.wait_ge(s_modacc, M_ALL)
            pe.wait_ge(s_ms, 3)
            mod_columns((2,))
            pe.wait_ge(s_h, 2 * KD)
            pe.wait_ge(s_subk, 16)

            def scores(hc):
                pe.wait_ge(s_wev, N_WQ + hc + 1)
                if hc >= 4:
                    pe.wait_ge(s_scr, hc - 3)
                for tt in range(TT):
                    r = mm(ps_sc[hc % 4][:, tt, :], qry[:, hc % 4, tt * P:(tt + 1) * P], subk_sb[:, hc, :],
                           start=True, stop=True)
                r.then_inc(s_sc, 1)

            for hc in range(HC):
                chunk((N_WQ + hc) % 4, N_WQ + hc, 0, N_WQ + hc)
                if hc:
                    scores(hc - 1)
            chunk(N_U % 4, N_U, 0, N_U)
            scores(HC - 1)
            chunk((N_U + 1) % 4, N_U + 1, 0, N_U + 1)
            for n in (N_U + 2, N_U + 3):
                chunk(n % 4, n, 0, n)
            stretch(pe, N_U + 4, N_U + FIRST, chunk)
            for tt in range(TT):
                pe.wait_ge(s_pk, tt + 1)
                for i in range(3):
                    r = flip(ps_spread[tt][:, i, :], pick_t[:, tt, i].rearrange("p h k -> p (h k)"), ident)
                r.then_inc(s_pkt, 1)
            pe.wait_ge(s_pkr, 2)

            def spread(r_, n, first=False):
                pe.wait_ge(s_hot, n + 1)
                if not first:
                    pe.wait_ge(s_gev, n - (HOT_RING - 1))
                for t in range(GT):
                    r = mm(ps_spread[r_][:, t, :], hot_a[:, r_, t, :], hot_b[:, r_, t, :], start=True, stop=True)
                r.then_inc(s_gmm, 1)

            per = SPREADS // (EARLY - FIRST)

            def chunk_and_spreads(j, n, i, k):
                def between(kk):
                    if (kk + 1) % (KD // per) == 0:
                        m = (k - N_U - FIRST) * per + kk // (KD // per)
                        spread(m % HOT_RING, i * (4 * per) + m, first=(m < HOT_RING and isinstance(n, int)))

                chunk(j, n, i, k, between=between)

            for n in range(N_U + FIRST, N_U + FIRST + 4):
                chunk_and_spreads(n % 4, n, 0, n)
            stretch(pe, N_U + FIRST + 4, N_U + EARLY, chunk_and_spreads)

            def u_block(j, n, i, k):
                pe.wait_ge(s_wlo, n - (N_U + EARLY - 1))
                pe.wait_ge(s_wev, n - 1)
                for kk in range(KD):
                    hi, lo = whi[:, j, kk, :], wlo[:, j, kk, :]
                    mm(ps_w[k % 2], hi, h_hi[:, kk, :], start=(kk == 0), stop=False)
                    mm(ps_w[k % 2], hi, h_lo[:, kk, :], start=False, stop=False)
                    r = mm(ps_w[k % 2], lo, h_hi[:, kk, :], start=False, stop=(kk == KD - 1))
                r.then_inc(s_wmm, 1)

            pe.wait_ge(s_hlo, 1)
            for n in range(N_U + EARLY, N_U + LAG):
                u_block(n % 4, n, 0, n)

            v_ring = [(vhi[b], vlo[:, b]) for b in range(2 * GB)]
            w_ring = [tuple(w[:, (N_U + NB + b) % W_RING].rearrange("p k c -> p (k c)") for w in (whi, wlo))
                      for b in range(W_RING)]

            def v_group(half_, n, split, blocks, first=False, last=False):
                pe.wait_ge(s_plo, n + 1)
                for j in range(GB):
                    pe.wait_ge(split[0], split[1] + (j + 1))
                    wh, wl = phi[:, half_, j, 0:P], plo[:, half_, j, 0:P]
                    for u in range(4):
                        vh, vl = (v[:, u * 512:(u + 1) * 512] for v in blocks[j])
                        mm(ps_y0[u], wh, vh, start=(first and j == 0), stop=False, skip_group_check=True)
                        mm(ps_y0[u], wh, vl, start=False, stop=False, skip_group_check=True)
                        r = mm(ps_y0[u], wl, vh, start=False, stop=(last and j == GB - 1), skip_group_check=True)
                if last:
                    r.then_inc(s_y0mm, 1)
                for u in range(4):
                    if not (first and u < 2):
                        pe.wait_ge(s_yadd, n * 4 + (u - 1))
                    for j in range(GB):
                        wh, wl = phi[:, half_, j, P:T], plo[:, half_, j, P:T]
                        vh, vl = (v[:, u * 512:(u + 1) * 512] for v in blocks[j])
                        mm(ps_y1[u % 2], wh, vh, start=(j == 0), stop=False)
                        mm(ps_y1[u % 2], wh, vl, start=False, stop=False)
                        r = mm(ps_y1[u % 2], wl, vh, start=False, stop=(j == GB - 1))
                    r.then_inc(s_vmm, 1)

            def from_v(g, n, m, **kw):
                v_group(g, n, (s_vlo, m * GB), v_ring[g * GB:g * GB + GB], **kw)

            def from_w(g, n, m, **kw):
                v_group(g, n, (s_wlo, m - (N_U + EARLY)), w_ring[g * GB:g * GB + GB], **kw)

            loops = (NB - LAG) // (2 * GB)
            for g in range(2):
                for j in range(GB):
                    n = N_U + LAG + g * GB + j
                    u_block(n % 4, n, 0, n)
                from_v(g, g, g, first=(g == 0))
            with pe.Fori(1, loops) as i:
                for g in range(2):
                    for j in range(GB):
                        n = N_U + LAG + g * GB + j
                        u_block(n % 4, i * (2 * GB) + n, i, n)
                    from_v(g, i * 2 + g, i * 2 + g)

            def turn(i, last=False):
                for g in range(2):
                    from_v(g, i * 4 + (V_TAIL - 2 + g), i * 2 + (V_TAIL - 2 + g))
                for g in range(2):
                    from_w(g, i * 4 + (V_TAIL + g), i * (2 * GB) + (N_U + NB + g * GB), last=(last and g == 1))

            with pe.Fori(0, TAILS - 1) as i:
                turn(i)
            turn(TAILS - 1, last=True)
            pe.wait_ge(s_y0e, 4)
            pe.wait_ge(s_yadd, NV * 4)
            for kk in range(KD):
                if kk >= 4:
                    pe.wait_ge(s_x2, kk - 3)
                flip(banks(kk % 4, TT, P)[:, 0, :], y0[:, kk * P:(kk + 1) * P], ident)
                flip(banks(kk % 4, TT, P)[:, 1, :], yacc[:, kk * P:(kk + 1) * P], ident).then_inc(s_yt, 1)
            for kk in range(KD):
                pe.wait_ge(s_sqk, KD + kk + 1)
                r = mm(banks(7, T), ones[:], squares3[:, kk, :], start=(kk == 0), stop=(kk == KD - 1))
                r.then_inc(s_ssq, 1)

        @block.scalar
        def _(act):
            A = nc.scalar.activation
            own = Steps(act, s_act)

            act.wait_ge(s_par, 16)
            A(csil, pcol("c"), ACT.Exp, scale=-1.0).then_inc(s_silu_e, 1)
            own.did(A(tiny[0], pcol("lam"), ACT.Abs))
            own.settle()
            A(tiny[1], tiny[0], ACT.Exp, scale=-1.0).then_inc(s_lam, 1)
            act.wait_ge(s_x, 16)
            A(squares0[:], res[:], ACT.Square).then_inc(s_sq, 1)

            def root(n, m):
                act.wait_ge(s_ms, n)
                A(ms[:, 0:m, :], ms[:, 0:m, :], ACT.Sqrt).then_inc(s_root, 1)

            root(1, 1)

            act.wait_ge(s_coef, 1)
            act.wait_ge(s_xn, 1)
            for kk in range(KD):
                A(hid[:, kk, :], hid[:, kk, :], ACT.Identity, bias=modv[:, 0, kk:kk + 1],
                  scale=coef[:, 0, kk:kk + 1]).then_inc(s_h, 1)

            def evac(j, n, i, k):
                act.wait_ge(s_wmm, n + 1)
                A(tile_of(z, n), ps_w[k % 2], ACT.Copy).then_inc(s_wev, 1)

            stretch(act, 0, 12, evac)
            for g, (dst, bias) in enumerate(((rg, "b_rec"), (ig, "b_in"))):
                act.wait_ge(s_gate, g + 1)
                for n in range(LRU_N):
                    r = A(dst[:, n, :], ps_gates[:, g, n, :], ACT.Sigmoid, bias=pcol(bias, n, 1))
                r.then_inc(s_sig, 1)
            stretch(act, 12, 14, evac)
            act.wait_ge(s_lam, 2)
            act.wait_ge(s_sig, 2)
            for n in range(LRU_N):
                own.did(A(th[:, n, :], rg[:, n, :], ACT.Tanh, scale=decay[:, n:n + 1]))
            own.settle()
            for n in range(LRU_N):
                r = A(rg[:, n, :], rg[:, n, :], ACT.Exp, scale=ndecay[:, n:n + 1])
            r.then_inc(s_a, 1)
            stretch(act, 14, 16, evac)
            act.wait_ge(s_var, 1)
            A(th[:], th[:], ACT.Sqrt).then_inc(s_sqrt, 1)
            stretch(act, 16, 19, evac)

            def values(first, m):
                for g in range(m):
                    act.wait_ge(s_vt, first + g + 1)
                    if first == 0:
                        A(vs[:, g, SWA_H:], ps_vt[g], ACT.Copy).then_inc(s_vev, 1)
                    elif g == 0:
                        A(vs[:, 0, 0:4], ps_vt[0], ACT.Copy).then_inc(s_vev, 1)
                    elif g == 1:
                        own.did(A(vs[:, 0, 4:6], ps_vt[1][:, 0:2], ACT.Copy))
                        A(vs[:, 1, 0:2], ps_vt[1][:, 2:4], ACT.Copy).then_inc(s_vev, 1)
                    else:
                        A(vs[:, 1, 2:6], ps_vt[2], ACT.Copy).then_inc(s_vev, 1)

            values(0, 2)
            stretch(act, 19, 21, evac)
            act.wait_ge(s_bzr, 2)
            own.did(A(e0[:], zs0[:], ACT.Abs))
            own.did(A(e1[:], zs1[:], ACT.Abs))
            own.settle()
            own.did(A(e0[:], e0[:], ACT.Exp, scale=-1.0))
            own.did(A(e1[:], e1[:], ACT.Exp, scale=-1.0))
            own.settle()
            for e_ in (e0, e1):
                A(e_[:], e_[:], ACT.Ln, bias=1.0).then_inc(s_bln, 1)
            stretch(act, 21, 27, evac)
            act.wait_ge(s_bx, 2)
            for e_ in (e0, e1):
                A(e_[:], e_[:], ACT.Exp).then_inc(s_bex, 1)
            stretch(act, 27, 32, evac)
            act.wait_ge(s_sm, 1)
            A(l1[:], l1[:], ACT.Exp).then_inc(s_se, 1)
            stretch(act, 32, 34, evac)
            act.wait_ge(s_sm, 2)
            A(l0[:], l0[:], ACT.Exp).then_inc(s_se, 1)
            act.wait_ge(s_yc, 1)
            act.wait_ge(s_bo, 1)
            A(squares1[:, 12:16], yc[:], ACT.Square).then_inc(s_sq, 1)
            stretch(act, 34, 37, evac)
            values(2, 3)
            stretch(act, 37, 41, evac)
            act.wait_ge(s_spt, 1)
            act.wait_ge(s_sl, 2)
            own.did(A(pt0[:, :, 0:P], ps_pt0, ACT.Copy))
            act.wait_ge(s_spt, 2)
            A(pt0[:, :, P:T], ps_pt1[:, 0], ACT.Copy).then_inc(s_spe, 1)
            A(pt1[:], ps_pt1[:, 1], ACT.Copy).then_inc(s_spe, 1)
            stretch(act, 41, 42, evac)
            act.wait_ge(s_wev, NZ)
            A(z[:, GA:GA + LRU_N], z[:, GA:GA + LRU_N], ACT.Gelu_apprx_tanh).then_inc(s_gelu, 1)
            act.wait_ge(s_ya, 1)
            A(squares1[:, 0:6], hid[:, 0:6], ACT.Square).then_inc(s_sq, 1)
            act.wait_ge(s_yb, 1)
            A(squares1[:, 6:12], hid[:, 6:12], ACT.Square).then_inc(s_sq, 1)
            root(2, 3)

            def square_tile(j, n, i, k):
                act.wait_ge(s_wev, n + 1)
                if not (isinstance(n, int) and n < N_OUT + 4):
                    act.wait_ge(s_ssq, n - (N_OUT + 4) + 1 + 4)
                A(sq_ring[:, (k - N_OUT) % 4, :], tile_of(res, n - N_OUT), ACT.Square).then_inc(s_sqk, 1)

            for n in range(N_OUT, N_OUT + 4):
                square_tile(n % 4, n, 0, n)
            stretch(act, N_OUT + 4, N_WQ, square_tile)
            root(3, 1)
            for kk in range(KD):
                act.wait_ge(s_xn, kk + 2)
                A(hid[:, kk, :], hid[:, kk, :], ACT.Identity, bias=modv[:, 3, kk:kk + 1]).then_inc(s_h, 1)

            def score_out(hc):
                act.wait_ge(s_sc, hc + 1)
                A(score[:, :, hc, :], ps_sc[hc % 4], ACT.Copy).then_inc(s_scr, 1)

            for hc in range(HC):
                act.wait_ge(s_wmm, N_WQ + hc + 1)
                if hc >= 4:
                    act.wait_ge(s_sc, hc - 3)
                A(qry[:, hc % 4, :], ps_w[hc % 2], ACT.Copy).then_inc(s_wev, 1)
                if hc:
                    score_out(hc - 1)

            def gelu(n, k, b):
                act.wait_ge(s_wmm, n + 1)
                A(tile_of(act_u, b % LAG), ps_w[k % 2], ACT.Gelu_apprx_tanh).then_inc(s_wev, 1)

            act.wait_ge(s_modread, 3)
            gelu(N_U, N_U, 0)
            score_out(HC - 1)
            for b in range(1, FIRST):
                gelu(N_U + b, N_U + b, b)
                if b == FIRST // 2:
                    act.wait_ge(s_h, 2 * KD)
                    act.wait_ge(s_sc, HC)
                    A(h_hi[:], hid[:], ACT.Copy).then_inc(s_hhi, 1)
                if b in (FIRST // 2 - 1, FIRST - 1):
                    tt = b // (FIRST // 2)
                    act.wait_ge(s_gx, tt + 1)
                    A(pick_t[:, tt, 2], pick_t[:, tt, 2], ACT.Exp).then_inc(s_ge, 1)
            for tt in range(TT):
                act.wait_ge(s_pkt, tt + 1)
                A(picks[:, :, tt * P:(tt + 1) * P], ps_spread[tt][:, 0:3], ACT.Copy).then_inc(s_pkr, 1)

            per = SPREADS // (EARLY - FIRST)
            for q in range(TQ):
                if q >= 2:
                    act.wait_ge(s_gst[q - 2], 16)
                for b in range(FIRST + 2 * q, FIRST + 2 * q + 2):
                    m0 = (b - FIRST) * per
                    with act.Fori(0, per // HOT_RING) as i:
                        for r_ in range(HOT_RING):
                            act.wait_ge(s_gmm, i * HOT_RING + (m0 + r_ + 1))
                            A(gstage[:, q % 2, :, bass.ds((i * HOT_RING + (m0 - q * 2 * per + r_)) * GT, GT)],
                              ps_spread[r_].rearrange("p t b -> p b t"), ACT.Copy).then_inc(s_gev, 1)
                    gelu(N_U + b, N_U + b, b)
                act.wait_ge(s_gev, (q + 1) * 2 * per)
                act.dma_start(gates_dram[q], gstage[:, q % 2]).then_inc(s_gst[q], 16)

            def w_hi(j, n, i, k):
                act.wait_ge(s_w[j], turns(i, k, W_RING) * 16)
                A(whi[:, j], wraw[:, j], ACT.Copy).then_inc(s_whi, 1)

            def v_hi(b, i, m):
                act.wait_ge(s_v[b], i * 16 + (m + 1) * 16)
                A(vhi[b], vraw[:, b], ACT.Copy).then_inc(s_vhi, 1)

            def p_hi(half_, n):
                act.wait_ge(s_pm, n + 1)
                A(phi[:, half_], praw[:, half_], ACT.Copy).then_inc(s_phi, 1)

            act.wait_ge(s_gst[2], 16)
            for n in range(N_U + EARLY, N_U + LAG):
                w_hi(n % 4, n, 0, n)
            for b in range(EARLY, LAG):
                gelu(N_U + b, b, b)
                if b < EARLY + GB:
                    n = N_U + b + 4
                    w_hi(n % 4, n, 0, n)
            v_hi(0, 0, 0)
            v_hi(1, 0, 0)
            p_hi(0, 0)

            def ahead(g, i, u_next=True):
                n = i * 2 + g
                if u_next:
                    for j in range(GB):
                        k = N_U + LAG + GB + g * GB + j
                        w_hi(k % 4, 0, i, k)
                k = LAG + g * GB
                gelu(i * (2 * GB) + (N_U + k), k, i * (2 * GB) + k)
                for j in range(GB):
                    k = (g + 1) * GB + j
                    v_hi(k % 4, i, k // 4)
                p_hi(1 - g, n + 1)
                k = LAG + g * GB + 1
                gelu(i * (2 * GB) + (N_U + k), k, i * (2 * GB) + k)

            loops = (NB - LAG) // (2 * GB)
            with act.Fori(0, loops - 1) as i:
                for g in range(2):
                    ahead(g, i)
            ahead(0, loops - 1)
            ahead(1, loops - 1, u_next=False)
            def v_next(g, i, n, m):
                for j in range(GB):
                    v_hi(g * GB + j, i, m)
                p_hi(g, n)

            def w_next(g, i):
                for j in range(GB):
                    k = N_U + NB + g * GB + j
                    w_hi(k % 4, 0, i, k)
                p_hi(g, i * 4 + (V_TAIL + g))

            turn = V_TAIL // 2 - 1
            with act.Fori(0, TAILS - 1) as i:
                v_next(1, i, i * 4 + (V_TAIL - 1), turn)
                w_next(0, i)
                w_next(1, i)
                v_next(0, i, i * 4 + (V_TAIL + 2), turn + 1)
            v_next(1, 0, NV - 3, turn + TAILS - 1)
            w_next(0, TAILS - 1)
            w_next(1, TAILS - 1)
            act.wait_ge(s_y0mm, 1)
            for u in range(4):
                A(y0[:, u * 512:(u + 1) * 512], ps_y0[u], ACT.Copy).then_inc(s_y0e, 1)
            act.wait_ge(s_vmm, NV * 4)
            for kk in range(KD):
                act.wait_ge(s_x2, kk + 1)
                A(squares3[:, kk, :], res2[:, kk, :], ACT.Square).then_inc(s_sqk, 1)
            root(4, 1)

        @block.vector
        def _(dve):
            V = nc.vector
            own = Steps(dve, s_dve)

            def mean_root(srcs, sums, n):
                dve.wait_ge(s_ssq, sums)
                for i, (src, width) in enumerate(srcs):
                    r = V.tensor_scalar(ms[:, i, :], src, 1.0 / width, EPS, ALU.mult, ALU.add)
                    if i < len(srcs) - 1:
                        own.did(r)
                own.settle()
                r.then_inc(s_ms, 1)
                dve.wait_ge(s_root, n)
                own.did(V.reciprocal(rstd[:, 0:len(srcs), :], ms[:, 0:len(srcs), :]))
                own.settle()

            V.memset(ones[:], 1.0).then_inc(s_ones, 1)
            dve.wait_ge(s_silu_e, 1)
            own.did(V.tensor_scalar(csil, csil, 1.0, None, ALU.add)); own.settle()
            own.did(V.reciprocal(csil, csil)); own.settle()
            own.did(V.tensor_tensor(csil, csil, pcol("c"), ALU.mult)); own.settle()

            def add_mod(q, kk, tile, loaded, done, first):
                dve.wait_ge(*loaded)
                col = csil[:, kk:kk + 1] if isinstance(kk, int) else csil[:, bass.ds(kk, 1)]
                if first:
                    V.tensor_scalar(mod_acc[:, q], tile, col, None, ALU.mult).then_inc(s_modacc, 1)
                else:
                    dve.wait_ge(s_modacc, done)
                    V.scalar_tensor_tensor(mod_acc[:, q], tile, col, mod_acc[:, q], ALU.mult,
                                           ALU.add).then_inc(s_modacc, 1)

            def mod0(j, n, i, k):
                add_mod(k % 2, i * 2 + k // 2, mod_ring0[:, j], (s_m0[j], turns(i, k, M_RING0) * 16), n - 1, k < 2)

            def mod_one(j, n, i, k):
                k0 = M_G2 if k >= M_G2 else M_G1
                add_mod(2, i * 4 + (k - k0), mod_ring[:, k % 2], (s_m[k % 2], i * 32 + ((k - M_G1) // 2 + 1) * 16), n,
                        k == k0)

            def mod_two(j, n, i, k):
                add_mod(k % 2, i * 2 + (k - M_H2) // 2, mod_ring[:, k % 2],
                        (s_m[k % 2], i * 32 + ((k - M_G1) // 2 + 1) * 16), n - 1, k < M_H2 + 2)

            for n in range(4):
                mod0(n, n, 0, n)
            mean_root([(banks(7, T), D)], 1, 1)
            V.tensor_tensor(hid[:], res[:], rstd[:, 0:1, :].to_broadcast([P, KD, T]), ALU.mult).then_inc(s_xn, 1)
            stretch(dve, 4, M_G1, mod0)
            dve.wait_ge(s_modcol, 1)
            own.did(V.tensor_tensor(modv[:, 1, :], ps_modcol[:, 0, :], pcol("b_mod", KD, KD), ALU.add))
            V.tensor_tensor(modv[:, 0, :], ps_modcol[:, 1, :], pcol("b_mod", 0, KD), ALU.add).then_inc(s_modread, 1)
            own.settle()
            dve.wait_ge(s_modread, 1)
            V.scalar_tensor_tensor(coef[:, 0, :], modv[:, 1, :], 1.0, pcol("norm_mix"), ALU.add,
                                   ALU.mult).then_inc(s_coef, 1)
            dve.wait_ge(s_relps, 1)
            dve.wait_ge(s_cst, 32)
            V.tensor_tensor(relbias[:], banks(2, T, 8)[:, :, 0:SWA_H].rearrange("p j h -> p h j"),
                            mixcol("bar").unsqueeze(1).to_broadcast([P, SWA_H, T]), ALU.add).then_inc(s_relsb, 1)
            dve.wait_ge(s_lam, 1)
            e, s_, s2, acc = tiny[1], tiny[2], tiny[3], tiny[4]
            own.did(V.tensor_scalar(s_, e, 2.0, None, ALU.add)); own.settle()
            own.did(V.reciprocal(s_, s_)); own.settle()
            own.did(V.tensor_tensor(s_, s_, e, ALU.mult)); own.settle()
            own.did(V.tensor_tensor(s2, s_, s_, ALU.mult)); own.settle()
            own.did(V.tensor_scalar(acc, s2, 1.0 / 19, 1.0 / 17, ALU.mult, ALU.add)); own.settle()
            for n in (15, 13, 11, 9, 7, 5, 3, 1):
                own.did(V.tensor_tensor(acc, acc, s2, ALU.mult)); own.settle()
                own.did(V.tensor_scalar(acc, acc, 1.0 / n, None, ALU.add)); own.settle()
            own.did(V.tensor_tensor(acc, acc, s_, ALU.mult)); own.settle()
            own.did(V.tensor_scalar(tiny[5], pcol("lam"), -1.0, 0.0, ALU.mult, ALU.max)); own.settle()
            own.did(V.scalar_tensor_tensor(tiny[5], acc, 2.0, tiny[5], ALU.mult, ALU.add)); own.settle()
            own.did(V.tensor_scalar(decay, tiny[5], LRU_C, None, ALU.mult)); own.settle()
            V.tensor_scalar(ndecay, tiny[5], -LRU_C, None, ALU.mult).then_inc(s_lam, 1)
            for n in range(M_G1, M_G1 + 4):
                mod_one(n % 4, n, 0, n)
            stretch(dve, M_G1 + 4, M_H2, mod_one)
            dve.wait_ge(s_wev, LRU_N)
            for n in range(LRU_N):
                own.did(V.tensor_scalar(cx[:, n, :], z[:, XA + n, :], pcol("conv_w", 3 * LRU_N + n, 1),
                                        pcol("conv_b", n, 1), ALU.mult, ALU.add))
            for j in (2, 1, 0):
                s = CONV_W - 1 - j
                own.settle()
                for n in range(LRU_N):
                    r = V.scalar_tensor_tensor(cx[:, n, s:T], z[:, XA + n, 0:T - s], pcol("conv_w", j * LRU_N + n, 1),
                                               cx[:, n, s:T], ALU.mult, ALU.add)
                    if j or n < LRU_N - 1:
                        own.did(r)
            own.settle()
            r.then_inc(s_conv, 1)
            for n in range(M_H2, M_H2 + 4):
                mod_two(n % 4, n, 0, n)
            stretch(dve, M_H2 + 4, M_H2 + 8, mod_two)
            dve.wait_ge(s_a, 1)
            dve.wait_ge(s_conv, 1)
            own.did(V.tensor_tensor(ig[:], ig[:], cx[:], ALU.mult))
            asq = z[:, XA:XA + LRU_N]
            own.did(V.tensor_tensor(asq, rg[:], rg[:], ALU.mult)); own.settle()
            V.scalar_tensor_tensor(th[:], asq, 1.0, th[:], ALU.add, ALU.mult).then_inc(s_var, 1)
            stretch(dve, M_H2 + 8, M_H2 + 12, mod_two)
            dve.wait_ge(s_sqrt, 1)
            own.did(V.tensor_tensor(ig[:], ig[:], th[:], ALU.mult)); own.settle()
            for n in range(LRU_N):
                own.did(V.tensor_tensor_scan(th[:, n, :], rg[:, n, :], ig[:, n, :], 0.0, ALU.mult, ALU.add))
            own.settle()
            dve.wait_ge(s_bz, 1)
            V.tensor_scalar(zs0[:], ps_bz0, HEAD_SCALE, None, ALU.mult).then_inc(s_bzr, 1)
            V.tensor_scalar(zs1[:], ps_bz1, HEAD_SCALE, None, ALU.mult).then_inc(s_bzr, 1)
            stretch(dve, M_H2 + 12, M_H2 + 16, mod_two)

            def strict(w):
                return mixcol("strict")[:, 0:w].unsqueeze(1).to_broadcast([P, SB_H, w])

            for i, (s, z_, e_, w) in enumerate(((sp0, zs0, e0, T), (sp1, zs1, e1, P))):
                dve.wait_ge(s_bln, i + 1)
                own.did(V.scalar_tensor_tensor(s[:], z_[:], 0.0, e_[:], ALU.max, ALU.add)); own.settle()
                own.did(V.tensor_tensor(z_[:], z_[:], s[:], ALU.subtract)); own.settle()
                V.tensor_tensor(s[:], s[:], strict(w), ALU.mult).then_inc(s_bsp, 1)
            stretch(dve, M_H2 + 16, M_H2 + 24, mod_two)
            dve.wait_ge(s_baf, 1)
            for e_, z_, ps_ in ((e0, zs0, ps_bz0), (e1, zs1, ps_bz1)):
                V.tensor_tensor(e_[:], z_[:], ps_, ALU.subtract).then_inc(s_bx, 1)
            stretch(dve, M_H2 + 24, M_H2 + 28, mod_two)
            for i, (e_, w) in enumerate(((e0, T), (e1, P))):
                dve.wait_ge(s_bex, i + 1)
                V.tensor_tensor(e_[:], e_[:], strict(w), ALU.mult).then_inc(s_bp, 1)
            dve.wait_ge(s_bo, 1)
            V.tensor_copy(yc[:], ps_bo).then_inc(s_yc, 1)

            def swa_shift(i, l, src, width):
                dve.wait_ge(s_sl, i + 1)
                V.scalar_tensor_tensor(l[:], src, HEAD_SCALE, relbias[:, :, T - width:T], ALU.mult,
                                       ALU.add).then_inc(s_slr, 1)
                dve.wait_ge(s_slr, i + 1)
                top = stat[:, 8 * i:8 * i + SWA_H]
                own.did(V.tensor_reduce(top, l[:], AX.X, ALU.max)); own.settle()
                V.tensor_tensor(l[:], l[:], top.unsqueeze(2).to_broadcast([P, SWA_H, width]),
                                ALU.subtract).then_inc(s_sm, 1)

            def swa_probs(i, l, width):
                dve.wait_ge(s_se, i + 1)
                times = mixcol("times", T - width).unsqueeze(1).to_broadcast([P, SWA_H, width])
                own.did(V.tensor_tensor(l[:], l[:], times, ALU.mult)); own.settle()
                tot = stat[:, 16 + 8 * i:16 + 8 * i + SWA_H]
                own.did(V.tensor_reduce(tot, l[:], AX.X, ALU.add)); own.settle()
                own.did(V.reciprocal(tot, tot)); own.settle()
                V.tensor_tensor(l[:], l[:], tot.unsqueeze(2).to_broadcast([P, SWA_H, width]), ALU.mult).then_inc(s_sp, 1)

            swa_shift(0, l1, ps_l1, T)
            swa_shift(1, l0, ps_l0, P)
            swa_probs(0, l1, T)
            swa_probs(1, l0, P)
            stretch(dve, M_H2 + 28, M_G2, mod_two)
            dve.wait_ge(s_gelu, 1)
            dve.wait_ge(s_wmm, NZ)
            V.tensor_tensor(hid[:, 0:LRU_N], th[:], z[:, GA:GA + LRU_N], ALU.mult).then_inc(s_ya, 1)
            dve.wait_ge(s_so, 1)
            V.tensor_copy(hid[:, 6:12], ps_so).then_inc(s_yb, 1)
            dve.wait_ge(s_modcol, 2)
            own.did(V.tensor_tensor(modv[:, 2, :], ps_modcol[:, 2, :], pcol("b_mod", 2 * KD, KD), ALU.add))
            V.tensor_tensor(modv[:, 3:5, :], ps_modcol[:, 0:2, :],
                            pcol("b_mod", 3 * KD, 2 * KD).rearrange("p (a b) -> p a b", a=2), ALU.add).then_inc(s_modread, 1)
            own.settle()
            dve.wait_ge(s_modread, 2)
            V.scalar_tensor_tensor(coef[:, 1, :], modv[:, 4, :], 1.0, pcol("norm_ffn"), ALU.add,
                                   ALU.mult).then_inc(s_coef, 1)
            mean_root([(ps_ssq[0], 768), (ps_ssq[1], 768), (ps_ssq[2], 512)], 4, 2)
            for kk in range(KD):
                src = hid[:, kk, :] if kk < 12 else yc[:, kk - 12, :]
                V.scalar_tensor_tensor(hid[:, kk, :], src, pcol("gnorm", kk, 1),
                                       rstd[:, 0 if kk < 6 else 1 if kk < 12 else 2, :], ALU.mult,
                                       ALU.mult).then_inc(s_y, 1)

            def x1_tile(j, n, i, k):
                dve.wait_ge(s_wmm, n + 1)
                x_ = tile_of(res, n - N_OUT)
                V.scalar_tensor_tensor(x_, ps_w[k % 2], modv[:, 2, bass.ds(n - N_OUT, 1)], x_, ALU.mult,
                                       ALU.add).then_inc(s_wev, 1)
                m = k - N_OUT + M_G2
                mod_one(m % 4, n - N_OUT + M_G2, i, m)

            for n in range(N_OUT, N_OUT + 4):
                x1_tile(n % 4, n, 0, n)
            stretch(dve, N_OUT + 4, N_WQ, x1_tile)
            mean_root([(banks(7, T), D)], 4 + KD, 3)
            for kk in range(KD):
                V.scalar_tensor_tensor(hid[:, kk, :], res[:, kk, :], coef[:, 1, kk:kk + 1], rstd[:, 0, :], ALU.mult,
                                       ALU.mult).then_inc(s_xn, 1)
            dve.wait_ge(s_modcol, 3)
            V.tensor_tensor(modv[:, 5, :], ps_modcol[:, 2, :], pcol("b_mod", 5 * KD, KD), ALU.add).then_inc(s_modread, 1)

            def top16(rows):
                for vals, idx, src, rest in rows:
                    own.did(V.max(vals[:, 0:8], src))
                own.settle()
                for vals, idx, src, rest in rows:
                    own.did(V.match_replace(rest, vals[:, 0:8], src, TAKEN))
                    own.did(V.max_index(idx[:, 0:8], vals[:, 0:8], src))
                own.settle()
                for vals, idx, src, rest in rows:
                    own.did(V.max(vals[:, 8:16], rest))
                own.settle()
                for vals, idx, src, rest in rows:
                    own.did(V.max_index(idx[:, 8:16], vals[:, 8:16], rest))

            for hc in range(HC):
                dve.wait_ge(s_scr, hc + 1)
                top16([(top_v[:, tt, hc], top_i[:, tt, hc], score[:, tt, hc], left[:, tt, hc]) for tt in range(TT)])
            own.settle()
            own.did(V.tensor_copy(top_f[:], top_i[:]))
            quad = [P, PEER_H, TOPK, TOPK]
            tri = [P, PEER_H, TOPK]
            c4 = cand[:].rearrange("p h (i j) -> p h i j", i=TOPK)
            e4 = eqs[:].rearrange("p h (i j) -> p h i j", i=TOPK)
            iota4 = iota[:, 0:TOPK].unsqueeze(1).unsqueeze(1).to_broadcast(quad)
            for tt in range(TT):
                tv = top_v[:, tt].rearrange("p (h c) k -> p h c k", c=2)
                tf = top_f[:, tt].rearrange("p (h c) k -> p h c k", c=2)
                gate = pick_t[:, tt, 2]
                own.did(V.tensor_tensor(c4, tv[:, :, 0].unsqueeze(3).to_broadcast(quad),
                                        tv[:, :, 1].unsqueeze(2).to_broadcast(quad), ALU.add))
                own.settle()
                top16([(gate[:, h], best_i[:, h].bitcast(U32), cand[:, h], cleft[:, h]) for h in range(PEER_H)])
                own.settle()
                own.did(V.tensor_copy(stat[:, 0:PEER_H], gate[:, :, 0])); own.settle()
                V.tensor_tensor(gate, gate, stat[:, 0:PEER_H].unsqueeze(2).to_broadcast(tri),
                                ALU.subtract).then_inc(s_gx, 1)
                for c in range(2):
                    if c == 0:
                        own.did(V.tensor_scalar(half_i[:], best_i[:], 4, None, ALU.arith_shift_right))
                    else:
                        own.did(V.tensor_scalar(half_i[:], best_i[:], TOPK - 1, None, ALU.bitwise_and))
                    own.settle()
                    own.did(V.tensor_copy(half_f[:], half_i[:])); own.settle()
                    own.did(V.tensor_tensor(e4, iota4, half_f[:].unsqueeze(3).to_broadcast(quad), ALU.is_equal)); own.settle()
                    own.did(V.tensor_tensor(e4, e4, tf[:, :, c].unsqueeze(2).to_broadcast(quad), ALU.mult)); own.settle()
                    own.did(V.tensor_reduce(pick_t[:, tt, c], e4, AX.X, ALU.add)); own.settle()
                dve.wait_ge(s_ge, tt + 1)
                tot = stat[:, 8:8 + PEER_H]
                own.did(V.tensor_reduce(tot, gate, AX.X, ALU.add)); own.settle()
                own.did(V.reciprocal(tot, tot)); own.settle()
                V.tensor_tensor(gate, gate, tot.unsqueeze(2).to_broadcast(tri), ALU.mult).then_inc(s_pk, 1)

            dve.wait_ge(s_hhi, 1)
            dve.wait_ge(s_spill, 16)
            V.tensor_tensor(h_lo[:], hid[:], h_hi[:].bitcast(F32), ALU.subtract).then_inc(s_hlo, 1)
            dve.wait_ge(s_pkr, 2)

            def one_hots(r_, n, first=False):
                if not first:
                    dve.wait_ge(s_gmm, n - (HOT_RING - 1))
                V.tensor_tensor(hot_a[:, r_], iota.unsqueeze(1).to_broadcast([P, GT, P]),
                                picks[:, 0, bass.ds(n * GT, GT)].unsqueeze(2).to_broadcast([P, GT, P]), ALU.is_equal)
                for t in range(GT):
                    b, g = (picks[:, i, bass.ds(n * GT + t, 1)] for i in (1, 2))
                    r = V.tensor_scalar(hot_b[:, r_, t, :], iota, b, g, ALU.is_equal, ALU.mult)
                r.then_inc(s_hot, 1)

            for n in range(HOT_RING):
                one_hots(n, n, True)
            with dve.Fori(1, SPREADS // HOT_RING) as i:
                for r_ in range(HOT_RING):
                    one_hots(r_, i * HOT_RING + r_)
            def w_lo(j, n):
                dve.wait_ge(s_whi, n - (N_U + EARLY - 1))
                V.tensor_tensor(wlo[:, j], wraw[:, j], whi[:, j].bitcast(F32), ALU.subtract).then_inc(s_wlo, 1)

            def v_lo(b, n):
                dve.wait_ge(s_vhi, n + 1)
                V.tensor_tensor(vlo[:, b], vraw[:, b], vhi[b].bitcast(F32), ALU.subtract).then_inc(s_vlo, 1)

            def p_mul(half_, n, first=False):
                dve.wait_ge(s_g[half_], (n - half_) * 8 + 16)
                for j in range(GB):
                    b = n * GB + j
                    r = V.tensor_tensor(praw[:, half_, j].rearrange("p (q t) -> p q t", q=TQ),
                                        tile_of(act_u, b % LAG).rearrange("p (q t) -> p q t", q=TQ),
                                        gring[:, half_, :, j, :], ALU.mult)
                r.then_inc(s_pm, 1)

            def p_lo(half_, n):
                dve.wait_ge(s_phi, n + 1)
                V.tensor_tensor(plo[:, half_], praw[:, half_], phi[:, half_].bitcast(F32),
                                ALU.subtract).then_inc(s_plo, 1)

            for n in range(N_U + EARLY, N_U + LAG):
                w_lo(n % 4, n)
            own.did(V.memset(yacc[:], 0.0)); own.settle()
            for n in range(N_U + LAG, N_U + LAG + GB):
                w_lo(n % 4, n)
            v_lo(0, 0)
            v_lo(1, 1)
            dve.wait_ge(s_wev, N_U + GB)
            p_mul(0, 0)
            p_lo(0, 0)

            def add_y(n):
                for u in range(4):
                    dve.wait_ge(s_vmm, n * 4 + (u + 1))
                    y_ = yacc[:, u * 512:(u + 1) * 512]
                    if not isinstance(n, int) or n:
                        dve.wait_ge(s_yadd, n * 4 + (u - 3))
                    V.tensor_tensor(y_, y_, ps_y1[u % 2], ALU.add).then_inc(s_yadd, 1)

            def ahead(g, i, u_next=True, v_next=True):
                n = i * 2 + g
                if u_next:
                    for j in range(GB):
                        k = N_U + LAG + GB + g * GB + j
                        w_lo(k % 4, i * (2 * GB) + k)
                if v_next:
                    p_mul(1 - g, n + 1)
                    for j in range(GB):
                        k = (g + 1) * GB + j
                        v_lo(k % 4, i * (2 * GB) + k)
                    p_lo(1 - g, n + 1)
                add_y(n)

            loops = (NB - LAG) // (2 * GB)
            ahead(0, 0)
            ahead(1, 0)
            with dve.Fori(1, loops - 1) as i:
                for g in range(2):
                    ahead(g, i)
            ahead(0, loops - 1)
            ahead(1, loops - 1, u_next=False)
            def v_next(g, n, m):
                p_mul(g, n)
                for j in range(GB):
                    v_lo(g * GB + j, m * GB + j)
                p_lo(g, n)
                add_y(n - 1)

            def w_next(g, n, m):
                p_mul(g, n)
                for j in range(GB):
                    w_lo((N_U + NB + g * GB + j) % 4, m + j)
                p_lo(g, n)
                add_y(n - 1)

            with dve.Fori(0, TAILS - 1) as i:
                v_next(1, i * 4 + (V_TAIL - 1), i * 2 + (V_TAIL - 1))
                for g in range(2):
                    w_next(g, i * 4 + (V_TAIL + g), i * 4 + (N_U + NB + g * GB))
                v_next(0, i * 4 + (V_TAIL + 2), i * 2 + V_TAIL)
            v_next(1, NV - 3, V_TAIL - 1 + 2 * (TAILS - 1))
            for g in range(2):
                w_next(g, NV - 2 + g, N_U + NB + 4 * (TAILS - 1) + g * GB)
            add_y(NV - 1)
            dve.wait_ge(s_back, 16)
            for kk in range(KD):
                dve.wait_ge(s_yt, kk + 1)
                V.scalar_tensor_tensor(res2[:, kk, :], banks(kk % 4, T), modv[:, 5, kk:kk + 1], res2[:, kk, :], ALU.mult,
                                       ALU.add).then_inc(s_x2, 1)
            mean_root([(banks(7, T), D)], 4 + 2 * KD, 4)
            for kk in range(KD):
                V.scalar_tensor_tensor(res2[:, kk, :], res2[:, kk, :], pcol("final_norm", kk, 1), rstd[:, 0, :],
                                       ALU.mult, ALU.mult).then_inc(s_o, 1)

        @block.gpsimd
        def _(pool):
            def load_mod(j, n, i, k):
                if not (isinstance(n, int) and n < M_G1 + M_RING):
                    pool.wait_ge(s_modacc, n - M_RING + 1)
                pool.dma_start(mod_ring[:, k % 2], wmod[bass.ds(n, 1)].rearrange("o p n -> (o p) n")).then_inc(s_m[k % 2], 16)

            pool.wait_ge(s_modacc, M_G1 - 4)
            for n in range(M_G1, M_G1 + 4):
                load_mod(0, n, 0, n)
            stretch(pool, M_G1 + 4, M_ALL, load_mod)
            pool.wait_ge(s_wev, N_WQ)
            pool.dma_start(res_dram, res[:]).then_inc(s_spill, 16)
            pool.wait_ge(s_spill, 16)
            pool.wait_ge(s_vmm, (NV - 2) * 4)
            pool.dma_start(res2[:], res_dram).then_inc(s_back, 16)
            for q in range(4):
                pool.wait_ge(s_o, 4 * q + 4)
                pool.dma_start(out[:, 4 * q:4 * q + 4], res2[:, 4 * q:4 * q + 4]).then_inc(s_st, 16)
            pool.wait_ge(s_st, 64)


def t5_bucket(dist):
    exact = BUCKETS // 2
    large = exact + (np.log(np.maximum(dist, 1) / exact) / np.log(MAX_DIST / exact) * (BUCKETS - exact)).astype(np.int32)
    return np.where(dist < exact, dist, np.minimum(large, BUCKETS - 1))


def constants():
    p = np.arange(P)[:, None]
    cst = np.zeros((P, N_CST + N_MIX), np.float32)

    def put(name, value):
        a, w = CST[name] if name in CST else (N_CST + MIX[name][0], MIX[name][1])
        cst[:, a:a + w] = value

    put("ident", np.eye(P))
    put("iota", np.arange(P)[None, :])
    put("after", p > np.arange(P)[None, :])
    put("strict", p < np.arange(T)[None, :])
    dist = p + P - np.arange(T)[None, :]
    times = sum(((dist >= 0) & (dist % d == 0) & (dist <= w)).astype(np.float32) for w, d in PATTERNS)
    put("times", times)
    put("bar", np.where(times > 0, 0.0, NEG_INF))
    dist = np.arange(N_SHIFT) - (P - 1)
    shifts = ((t5_bucket(np.maximum(dist, 0))[None, :] == np.arange(BUCKETS)[:, None]) & (dist >= 0)[None, :])
    return cst[:, :N_CST], cst[:, N_CST:], shifts.astype(np.float32)


def kernel(x, c, w_mod, b_mod, norm_mix, norm_ffn, w_in, conv_w, conv_b, lru_w_rec, lru_b_rec, lru_w_in, lru_b_in,
           lru_lambda, rel_bias, gnorm_lru, gnorm_swa, gnorm_sb, w_out, peer_wq, peer_subkeys, peer_u, peer_v,
           final_norm):
    import concourse.bacc as bacc
    from concourse.bass_utils import run_bass_kernel_spmd

    A = np.asarray

    def cols(v):
        return A(v).reshape(-1, P).T

    par = np.concatenate([cols(c), cols(norm_mix), cols(norm_ffn), cols(final_norm), cols(b_mod), cols(conv_w),
                          cols(conv_b), cols(lru_b_rec), cols(lru_b_in), cols(lru_lambda), cols(gnorm_lru),
                          cols(gnorm_swa), cols(gnorm_sb)], axis=1)
    cst, mixc, shifts = constants()

    def chunks(w):
        return A(w).reshape(KD, P, -1, P).transpose(2, 1, 0, 3)

    u_blocks = A(peer_u)[0].reshape(P, NB, KD, P).transpose(1, 3, 2, 0)
    order = [*range(0, 6), *range(30, 42), *range(12, 30), *range(6, 12)]
    wst = np.concatenate([chunks(A(w_in)[0])[order], chunks(A(w_out)[0]), chunks(A(peer_wq)[0]), u_blocks], axis=0)
    wm = A(w_mod)[0].reshape(KD, P, 6, D).transpose(0, 2, 1, 3)
    wmod = np.concatenate([wm[:, parts].reshape(-1, P, D) for parts in ([1, 0], [2], [3, 4], [5])], axis=0)
    arrays = {
        "xT": A(x)[0].T.reshape(KD, P, T).transpose(1, 0, 2),
        "par": par,
        "cst": cst,
        "mixc": mixc,
        "shifts": shifts,
        "relb": A(rel_bias),
        "wmod": wmod,
        "wst": wst,
        "lruw": np.stack([A(lru_w_rec)[0], A(lru_w_in)[0]]).transpose(2, 0, 1, 3),
        "subk": A(peer_subkeys)[0].reshape(HC, P, P).transpose(2, 0, 1),
        "vtab": A(peer_v)[0].reshape(P, NB, D).transpose(1, 0, 2),
    }
    arrays = {k: np.ascontiguousarray(v) for k, v in arrays.items()}
    nc = bacc.Bacc("TRN2", target_bir_lowering=False, num_devices=1, dynamic_dma_scratch_size=4096)
    aps = {k: nc.dram_tensor(k, v.shape, mybir.dt.from_np(v.dtype), kind="ExternalInput").ap() for k, v in arrays.items()}
    gates = nc.dram_tensor("gates_dram", (TQ, P, NB, TW), F32, kind="Internal").ap()
    kept = nc.dram_tensor("x1_dram", (P, KD, T), F32, kind="Internal").ap()
    out = nc.dram_tensor("out", (P, KD, T), F32, kind="ExternalOutput").ap()
    hybrid_block(nc, **aps, gates_dram=gates, res_dram=kept, out=out)
    r = run_bass_kernel_spmd(nc, [arrays], core_ids=[0])
    y = r.results[0]["out"]
    return y.transpose(1, 0, 2).reshape(D, T).T.reshape(1, T, D)
```

```python
import math
from contextlib import ExitStack

import concourse.bass as bass
import numpy as np
from concourse import mybir

P = 128
F32 = mybir.dt.float32
F32R = mybir.dt.float32r
I32 = mybir.dt.int32
U32 = mybir.dt.uint32
ALU = mybir.AluOpType
ACT = mybir.ActivationFunctionType
AX = mybir.AxisListType

T = 256
TT = T // P
D = 2048
KD = D // P
EPS = 1e-6
LRU_N, SWA_H, SB_H = 6, 6, 4
CONV_W = 4
LRU_C = 8.0
HEAD_SCALE = 128.0 ** -0.5
PATTERNS = ((128, 1), (512, 4), (2048, 16))
BUCKETS, MAX_DIST = 32, 2048
NEG_INF = -1e30
TAKEN = -3.0e38
PEER_H, TOPK = 8, 16
HC = 2 * PEER_H
NB = 128

XA, QC, KC, VC, QB, KB, VB, GA, NZ = 0, 6, 10, 14, 18, 24, 30, 36, 42
N_OUT = NZ
N_WQ = N_OUT + KD
N_U = N_WQ + KD
W_RING = 4
M_G1 = 2 * KD
M_H2 = M_G1 + KD
M_G2 = M_H2 + 2 * KD
M_ALL = M_G2 + KD
M_RING = 2
M_RING0 = 4
GB = 2
FIRST = 12
EARLY = 20
LAG = 24
NV = NB // GB
assert LAG % (4 * GB) == 0
TAILS = LAG // GB // 4
V_TAIL = NV - 4 * TAILS + 2
GT = 4
TQ = 4
TW = T // TQ
SPREADS = T // GT
HOT_RING = 4

PAR = {}
_at = 0
for _name, _n in (("c", KD), ("norm_mix", KD), ("norm_ffn", KD), ("final_norm", KD), ("b_mod", 6 * KD),
                  ("conv_w", CONV_W * LRU_N), ("conv_b", LRU_N), ("b_rec", LRU_N), ("b_in", LRU_N),
                  ("lam", LRU_N), ("gnorm", LRU_N + SWA_H + SB_H)):
    PAR[_name] = (_at, _n)
    _at += _n
N_PAR = _at
CST = {"ident": (0, P), "iota": (P, P)}
N_CST = 2 * P
MIX = {"after": (0, P), "strict": (P, T), "bar": (P + T, T), "times": (P + 2 * T, T)}
N_MIX = P + 3 * T
N_SHIFT = T + P


class Steps:

    def __init__(self, engine, sem):
        self.engine, self.sem, self.n = engine, sem, 0

    def did(self, ins):
        ins.then_inc(self.sem, 1)
        self.n += 1
        return self.n

    def settle(self, n=None):
        self.engine.wait_ge(self.sem, self.n if n is None else n)


def hybrid_block(nc, xT, par, cst, mixc, shifts, relb, wmod, wst, lruw, subk, vtab, rel_dram, gates_dram, res_dram, out):
    ctx = ExitStack()
    with ctx:
        def sem(name):
            return ctx.enter_context(nc.semaphore(name))

        base = (nc.sbuf_base + 31) // 32 * 32
        size = (nc.sbuf_usable_end - base) // 4 - 8
        ctx.enter_context(nc.sbuf_tensor("slab", [P, size], F32))

        def at(name, kb, shape, dt=F32):
            assert kb * 256 + int(np.prod(shape)) <= size, name
            return nc.alloc_sbuf_tensor_at(name, [P, *shape], dt, offset=base + int(kb * 1024))

        par_sb = at("par_sb", 0, [N_PAR])
        cst_sb = at("cst_sb", 1, [N_CST])
        ones = at("ones", 2, [P])
        small = at("small", 2.5, [256])
        modv = at("modv", 3.5, [6, KD])
        coef = at("coef", 4, [2, KD])
        ms = at("ms", 4.25, [3, T])
        rstd = at("rstd", 7.25, [3, T])
        picks = at("picks", 10.25, [3, T])
        wraw = at("wraw", 13.5, [W_RING, KD, P])
        wlo = at("wlo", 13.5, [W_RING, KD, P], F32R)
        hid = at("hid", 45.5, [KD, T])
        h_lo = at("h_lo", 45.5, [KD, T], F32R)
        chi = at("chi", 157.5, [2, KD, P], F32R)
        x0 = at("x0", 157.5, [KD, T])
        squares0 = at("squares0", 61.5, [KD, T])
        mod_ring0 = at("mod_ring0", 77.5, [M_RING0, D])
        relw = at("relw", 109.5, [SWA_H, P])
        rel_rows = at("rel_rows", 112.5, [SWA_H, N_SHIFT])
        shifts_sb = at("shifts_sb", 127.5, [N_SHIFT])
        relb_sb = at("relb_sb", 130, [SWA_H])
        z = at("z", 61.5, [GA, T])
        cx = at("cx", 97.5, [LRU_N, T])
        rg = at("rg", 103.5, [LRU_N, T])
        ig = at("ig", 109.5, [LRU_N, T])
        th = at("th", 115.5, [LRU_N, T])
        vs = at("vs", 121.5, [TT, SWA_H + SB_H, P])
        relbias = at("relbias", 131.5, [SWA_H, T])
        mix_sb = at("mix_sb", 145.5, [N_MIX])
        mod_ring = at("mod_ring", 173.5, [M_RING, D])
        mod_acc = [at("mod_acc0", 137.5, [D]), at("mod_acc1", 205.5, [D])]
        h1_hi = at("h1_hi", 189.5, [KD, T], F32R)
        lw = at("lw", 213.5, [2, LRU_N, P])
        zs0, zs1 = at("zs0", 97.5, [SB_H, T]), at("zs1", 101.5, [SB_H, P])
        e0, e1 = at("e0", 103.5, [SB_H, T]), at("e1", 107.5, [SB_H, P])
        sp0, sp1 = at("sp0", 109.5, [SB_H, T]), at("sp1", 113.5, [SB_H, P])
        yc = at("yc", 61.5 + QC, [SB_H, T])
        l1 = at("l1", 97.5, [SWA_H, T])
        l0 = at("l0", 109.5, [SWA_H, P])
        pt0 = at("pt0", 61.5 + QB, [SWA_H, T])
        pt1 = at("pt1", 61.5 + KB, [SWA_H, P])
        squares1 = at("squares1", 97.5, [KD, T])
        sq_ring = at("sq_ring", 61.5, [4, T])
        y_hi = at("y_hi", 77.5, [KD, T], F32R)
        res = at("res", 189.5, [KD, T])
        h_hi = at("h_hi", 61.5, [KD, T], F32R)
        qry = at("qry", 213.5, [4, T])
        eqs = at("eqs", 205.5, [PEER_H, T])
        k = 77.5
        score = at("score", k, [TT, HC, P]); k += 16
        left = at("left", k, [TT, HC, P]); k += 16
        cand = at("cand", k, [PEER_H, T]); k += 8
        cleft = at("cleft", k, [PEER_H, T]); k += 8
        subk_sb = at("subk_sb", k, [HC, P]); k += 8
        top_v = at("top_v", k, [TT, HC, TOPK]); k += 2
        top_i = at("top_i", k, [TT, HC, TOPK], U32); k += 2
        top_f = at("top_f", k, [TT, HC, TOPK]); k += 2
        best_i = at("best_i", k, [PEER_H, TOPK], I32); k += 0.5
        half_i = at("half_i", k, [PEER_H, TOPK], I32); k += 0.5
        half_f = at("half_f", k, [PEER_H, TOPK]); k += 0.5
        pick_t = at("pick_t", k, [TT, 3, PEER_H, TOPK]); k += 3
        assert k <= 157.5
        gstage = at("gstage", 85.5, [2, NB, TW])
        hot_a = at("hot_a", 173.5, [HOT_RING, GT, P])
        hot_b = at("hot_b", 181.5, [HOT_RING, GT, P])
        whi = at("whi", 77.5, [W_RING, KD, P], F32R)
        vraw = at("vraw", 109.5, [2 * GB, D])
        vlo = at("vlo", 109.5, [2 * GB, D], F32R)
        vhi = [at("vhi01", 141.5, [2, D], F32R)[:, j] for j in range(2)]
        vhi += [at("vhi23", 157.5, [2, D], F32R)[:, j] for j in range(2)]
        yacc = at("yacc", 173.5, [D])
        gring = at("gring", 181.5, [2, TQ, GB, TW])
        praw = at("praw", 185.5, [2, GB, T])
        plo = at("plo", 185.5, [2, GB, T], F32R)
        phi = at("phi", 189.5, [2, GB, T], F32R)
        act_u = at("act_u", 193.5, [LAG, T])
        y0 = at("y0", 141.5, [D])
        res2 = at("res2", 109.5, [KD, T])
        squares3 = at("squares3", 61.5, [KD, T])

        ps = ctx.enter_context(nc.psum_tensor("ps", [P, 8, 512], F32))

        def banks(b, *shape):
            n = int(np.prod(shape))
            flat = ps[:, b:b + (n + 511) // 512, :].rearrange("p a b -> p (a b)")[:, 0:n]
            names = "abcd"[:len(shape)]
            if len(shape) == 1:
                return flat
            return flat.rearrange(f"p ({' '.join(names)}) -> p {' '.join(names)}",
                                  **{names[i]: shape[i] for i in range(1, len(shape))})

        ps_w = [banks(0, T), banks(1, T)]
        ps_modcol = banks(7, 3, KD)
        ps_gates = banks(2, 2, LRU_N, T)
        ps_vt = [banks(2, 4, P), banks(3, 4, P), banks(4, 4, P)]
        ps_bz0, ps_bz1 = banks(4, SB_H, T), banks(6, SB_H, P)
        ps_bo = banks(2, SB_H, T)
        ps_l1, ps_l0 = banks(5, SWA_H, T), banks(3, SWA_H, P)
        ps_pt0, ps_pt1 = banks(3, SWA_H, P), banks(5, 2, SWA_H, P)
        ps_so = banks(2, SWA_H, T)
        ps_ssq = [banks(5, 2, T)[:, 0], banks(5, 2, T)[:, 1], banks(6, T)]
        ps_sc = [banks(2 + i, TT, P) for i in range(4)]
        ps_spread = [banks(4 + i, GT, P) for i in range(HOT_RING)]
        ps_y0 = [banks(2 + i, 512) for i in range(4)]
        ps_y1 = [banks(6, 512), banks(7, 512)]

        def pcol(name, i=0, n=None):
            a, w = PAR[name]
            return par_sb[:, a + i:a + i + (w - i if n is None else n)]

        def mixcol(name, i=0):
            a, w = MIX[name]
            return mix_sb[:, a + i:a + w]

        ident, iota = cst_sb[:, 0:P], cst_sb[:, P:2 * P]
        csil = small[:, 0:KD]
        tiny = [small[:, 32 + 8 * i:32 + 8 * i + LRU_N] for i in range(8)]
        decay = small[:, 96:96 + LRU_N]
        ndecay = small[:, 104:104 + LRU_N]
        stat = small[:, 112:112 + 4 * 8]

        def tile_of(tensor, i):
            return tensor[:, bass.ds(i, 1)].rearrange("p o t -> p (o t)")

        s_par, s_cst, s_x, s_rel, s_lruw, s_subk = (sem(n) for n in (
            "par_loaded", "cst_loaded", "x_loaded", "rel_loaded", "lru_weights_loaded", "subkeys_loaded"))
        s_w = [sem(f"w_loaded{i}") for i in range(W_RING)]
        s_m0 = [sem(f"first_mod_loaded{i}") for i in range(M_RING0)]
        s_m = [sem(f"mod_loaded{i}") for i in range(M_RING)]
        s_v = [sem(f"v_loaded{i}") for i in range(2 * GB)]
        s_g = [sem(f"gates_loaded{i}") for i in range(2)]
        s_spill, s_back = sem("x1_stored"), sem("x1_loaded")
        s_dve, s_act = sem("dve_steps"), sem("act_steps")
        s_ones, s_silu_e, s_lam = sem("ones_set"), sem("silu_exp"), sem("lambda_steps")
        s_sq, s_ssq, s_ms, s_root = sem("squared"), sem("square_sums"), sem("mean_squares"), sem("roots")
        s_xn, s_coef, s_h = sem("x_normed"), sem("coef_ready"), sem("h_lo_tiles")
        s_relw, s_relps, s_relrow, s_reld, s_relt = (sem("relbias_spread"), sem("relbias_in_psum"), sem("relbias_rows"),
                                                     sem("relbias_rows_stored"), sem("relbias_by_place"))
        s_h0 = sem("x_times_root")
        s_modlast = sem("last_shift1_quarters")
        s_modacc, s_modcol, s_modread = sem("mod_tiles_added"), sem("mod_columns"), sem("mod_columns_read")
        s_wmm, s_wev = sem("chunk_products"), sem("chunks_evacuated")
        s_conv, s_gate, s_sig, s_a = sem("conv_done"), sem("gates_in_psum"), sem("sigmoids"), sem("a_and_tanh")
        s_var, s_sqrt, s_gelu = sem("lru_scale_squared"), sem("lru_scale"), sem("gate_branch_done")
        s_vt, s_vev = sem("v_transposed"), sem("v_evacuated")
        s_sl, s_slr, s_sm, s_se, s_sp = (sem("swa_logits"), sem("swa_logits_read"), sem("swa_shifted"),
                                         sem("swa_exp"), sem("swa_probs"))
        s_spt, s_spe, s_so = sem("swa_probs_transposed"), sem("swa_probsT_ready"), sem("swa_out")
        s_bz, s_bzr, s_bln, s_bsp = sem("sb_scores"), sem("sb_scores_read"), sem("sb_log"), sem("sb_softplus")
        s_baf, s_bx, s_bex, s_bp, s_bo = (sem("sb_after"), sem("sb_exponent"), sem("sb_expd"), sem("sb_weights"),
                                          sem("sb_out"))
        s_ya, s_yb, s_yc, s_y = sem("ya_ready"), sem("yb_ready"), sem("yc_ready"), sem("y_normed")
        s_sqk = sem("x1_tiles_squared")
        s_sc, s_scr = sem("peer_scores"), sem("peer_scores_read")
        s_gx, s_ge, s_pk, s_pkt, s_pkr = (sem("gate_shifted"), sem("gate_exp"), sem("picks_ready"),
                                          sem("picks_transposed"), sem("picks_read"))
        s_hot, s_gmm, s_gev = sem("one_hots"), sem("gates_spread"), sem("gates_staged")
        s_gst = [sem(f"gates_stored{q}") for q in range(TQ)]
        s_hhi, s_yhi, s_ylo = sem("h_hi_tiles"), sem("y_hi_tiles"), sem("y_lo_tiles")
        s_chi, s_clo = sem("chunk_hi_halves"), sem("chunk_lo_halves")
        s_whi, s_wlo, s_vhi, s_vlo = sem("w_hi_ready"), sem("w_lo_ready"), sem("v_hi_ready"), sem("v_lo_ready")
        s_pm, s_phi, s_plo = sem("weights_ready"), sem("weights_hi_ready"), sem("weights_lo_ready")
        s_y0mm, s_vmm, s_yadd = sem("y0_group_products"), sem("y1_products"), sem("y1_added")
        s_y0e, s_yt, s_x2, s_o, s_st = (sem("y0_evacuated"), sem("y_transposed"), sem("x2_tiles"), sem("out_tiles"),
                                        sem("out_stored"))

        block = ctx.enter_context(nc.Block())

        def stretch(engine, n0, n1, body, per=4):
            if n1 - n0 >= 2 * per:
                assert (n1 - n0) % per == 0
                with engine.Fori(0, (n1 - n0) // per) as i:
                    for j in range(per):
                        body((n0 + j) % per, i * per + (n0 + j), i, n0 + j)
            else:
                for n in range(n0, n1):
                    body(n % per, n, 0, n)

        def turns(i, n, ring, per=4):
            return i * (per // ring) + (n // ring + 1)

        @block.sync
        def _(sp):
            sp.dma_start(par_sb[:], par).then_inc(s_par, 16)
            sp.dma_start(x0[:], xT).then_inc(s_x, 16)

            def load_mod0(slot, n):
                sp.dma_start(mod_ring0[:, slot], wmod[bass.ds(n, 1)].rearrange("o p n -> (o p) n")).then_inc(s_m0[slot], 16)

            def load_w(slot, n):
                sp.dma_start(wraw[:, slot], wst[bass.ds(n, 1)].rearrange("o p k c -> (o p) k c")).then_inc(s_w[slot], 16)

            for n in range(M_RING0):
                load_mod0(n, n)
            sp.dma_start(shifts_sb[0:BUCKETS], shifts).then_inc(s_rel, 16)
            sp.dma_start(relb_sb[0:BUCKETS], relb).then_inc(s_rel, 16)
            sp.dma_start(cst_sb[:], cst).then_inc(s_cst, 16)
            sp.dma_start(mix_sb[:], mixc).then_inc(s_cst, 16)

            def next_mod0(j, n, i, k):
                sp.wait_ge(s_modacc, n - M_RING0 + 1)
                load_mod0(j, n)

            stretch(sp, M_RING0, M_G1, next_mod0)
            sp.dma_start(lw[:], lruw).then_inc(s_lruw, 16)
            sp.wait_ge(s_w[W_RING - 1], 16)

            def load_mod(j, n, i, k):
                if not (isinstance(n, int) and n < M_G1 + M_RING):
                    sp.wait_ge(s_modacc, n - M_RING + 1)
                sp.dma_start(mod_ring[:, k % 2], wmod[bass.ds(n, 1)].rearrange("o p n -> (o p) n")).then_inc(s_m[k % 2], 16)

            for n in range(M_G1, M_G1 + 4):
                load_mod(0, n, 0, n)
            stretch(sp, M_G1 + 4, M_G2, load_mod)
            sp.wait_ge(s_wmm, NZ)
            sp.dma_start(res[:], xT).then_inc(s_x, 16)
            stretch(sp, M_G2, M_ALL, load_mod)
            sp.dma_start(subk_sb[:], subk).then_inc(s_subk, 16)
            sp.wait_ge(s_wev, N_WQ)
            sp.dma_start(res_dram, res[:]).then_inc(s_spill, 16)

            def load_v(j, n):
                sp.dma_start(vraw[:, j], vtab[bass.ds(n, 1)].rearrange("o p d -> (o p) d")).then_inc(s_v[j], 16)

            def load_g(half, n):
                sp.dma_start(gring[:, half].rearrange("p q b t -> p q (b t)"),
                             gates_dram[:, :, bass.ds(n * GB, GB), :].rearrange("q a b t -> a q (b t)")).then_inc(s_g[half], 16)

            for q in range(TQ):
                sp.wait_ge(s_gst[q], 16)
            for g in range(2):
                load_g(g, g)
                for j in range(GB):
                    load_v(g * GB + j, g * GB + j)

            def next_group(half, n):
                sp.wait_ge(s_pm, n - 1)
                load_g(half, n)
                sp.wait_ge(s_vmm, n * 4 - 4)
                for j in range(GB):
                    load_v(half * GB + j, n * GB + j)

            lead = LAG + W_RING
            for n in range(N_U + LAG, N_U + lead):
                sp.wait_ge(s_wmm, n - W_RING + 1)
                load_w(n % W_RING, n)
            with sp.Fori(0, (NB - lead) // 4) as i:
                for g in range(2):
                    for j in range(GB):
                        n = N_U + lead + g * GB + j
                        sp.wait_ge(s_wmm, i * 4 + (n - W_RING + 1))
                        load_w(n % W_RING, i * 4 + n)
                    next_group(g, i * 2 + (2 + g))
            def load_tail(slot, n):
                sp.dma_start(wraw[:, slot].rearrange("p k c -> p (k c)"),
                             vtab[bass.ds(n, 1)].rearrange("o p d -> (o p) d")).then_inc(s_w[slot], 16)

            for g in range(2):
                for j in range(GB):
                    m = N_U + NB + g * GB + j
                    sp.wait_ge(s_wmm, m - W_RING + 1)
                    load_tail(m % W_RING, (V_TAIL + g) * GB + j)
                next_group(g, V_TAIL - 2 + g)
            with sp.Fori(0, TAILS - 1) as i:
                for g in range(2):
                    n = V_TAIL - 2 + g
                    sp.wait_ge(s_pm, i * 4 + (n + 1))
                    load_g(g, i * 4 + (n + 2))
                    sp.wait_ge(s_vmm, i * 16 + (n + 1) * 4)
                    for j in range(GB):
                        load_v(g * GB + j, i * (4 * GB) + ((n + 4) * GB + j))
                for g in range(2):
                    n = V_TAIL + g
                    sp.wait_ge(s_pm, i * 4 + (n + 1))
                    load_g(g, i * 4 + (n + 2))
                    sp.wait_ge(s_vmm, i * 16 + (n + 1) * 4)
                    for j in range(GB):
                        load_tail((N_U + NB + g * GB + j) % W_RING, i * (4 * GB) + ((n + 4) * GB + j))
            for g in range(2):
                sp.wait_ge(s_pm, NV - 3 + g)
                load_g(g, NV - 2 + g)

        @block.tensor
        def _(pe):
            mm = nc.tensor.matmul
            flip = nc.tensor.transpose

            def three(dst, hi, lo, src_hi, src_lo, first, last):
                mm(dst, hi, src_hi, start=first, stop=False)
                mm(dst, hi, src_lo, start=False, stop=False)
                return mm(dst, lo, src_hi, start=False, stop=last)

            def chunk(j, n, i, k, src=h1_hi, evac=True, between=None, tiles=None):
                if evac:
                    pe.wait_ge(s_wev, n - 1)
                for kk in range(KD):
                    if kk % (KD // 2) == 0:
                        pe.wait_ge(s_clo, n * 2 + (1 + kk // (KD // 2)))
                    if tiles:
                        pe.wait_ge(tiles[0], tiles[1] + (kk + 1))
                    r = three(ps_w[k % 2], chi[:, k % 2, kk, :], wlo[:, j, kk, :], src[:, kk, :], h_lo[:, kk, :],
                              kk == 0, kk == KD - 1)
                    if kk == KD - 1:
                        r.then_inc(s_wmm, 1)
                    if between:
                        between(kk)

            def sum_squares(dst, sq, tiles):
                for i, kk in enumerate(tiles):
                    r = mm(dst, ones[:], sq[:, kk, :], start=(i == 0), stop=(i == len(tiles) - 1))
                r.then_inc(s_ssq, 1)

            pe.wait_ge(s_ones, 1)
            pe.wait_ge(s_sq, 1)
            sum_squares(banks(7, T), squares0, range(KD))
            pe.wait_ge(s_relw, 1)
            for h in range(SWA_H):
                r = mm(ps[:, h, 0:N_SHIFT], relw[0:BUCKETS, h, :], shifts_sb[0:BUCKETS, :], start=True, stop=True)
            r.then_inc(s_relps, 1)

            def mod_columns(col, acc, by_quarters=False):
                for kk in range(KD):
                    if by_quarters and kk % 4 == 0:
                        pe.wait_ge(*((s_modlast, kk // 4 + 1) if kk // 4 < 3 else (s_modacc, M_G1)))
                    r = mm(ps_modcol[:, col, kk:kk + 1], mod_acc[acc][:, kk * P:(kk + 1) * P], ones[:, 0:1],
                           start=True, stop=True)
                r.then_inc(s_modcol, 1)

            pe.wait_ge(s_ms, 1)
            pe.wait_ge(s_modacc, KD)
            mod_columns(0, 0)
            pe.wait_ge(s_coef, 1)
            mod_columns(1, 1, by_quarters=True)
            pe.wait_ge(s_relrow, 1)
            chunk(0, 0, 0, 0, evac=False, tiles=(s_h, 0))
            chunk(1, 1, 0, 1, evac=False)
            stretch(pe, 2, 10, chunk)
            pe.wait_ge(s_lruw, 16)
            pe.wait_ge(s_conv, 1)
            pe.wait_ge(s_modread, 1)
            for g in range(2):
                for n in range(LRU_N):
                    r = mm(ps_gates[:, g, n, :], lw[:, g, n, :], cx[:, n, :], start=True, stop=True)
                r.then_inc(s_gate, 1)
            stretch(pe, 10, 18, chunk)

            def turn_values(first, rounds):
                for g, (z0, h0) in enumerate(rounds):
                    for i in range(4):
                        tt, h = first[g][i]
                        r = flip(ps_vt[g][:, i, :], z[:, z0 + h, tt * P:(tt + 1) * P], ident)
                    r.then_inc(s_vt, 1)

            pe.wait_ge(s_sig, 2)
            pe.wait_ge(s_wev, 18)
            for h in range(SB_H):
                mm(ps_bz0[:, h, :], z[:, KC + h, 0:P], z[:, QC + h, :], start=True, stop=True)
            for h in range(SB_H):
                r = mm(ps_bz1[:, h, :], z[:, KC + h, P:T], z[:, QC + h, P:T], start=True, stop=True)
            r.then_inc(s_bz, 1)
            turn_values([[(0, h) for h in range(4)], [(1, h) for h in range(4)]], [(VC, SWA_H)] * 2)
            pe.wait_ge(s_modacc, M_H2)
            mod_columns(2, 0)
            stretch(pe, 18, 26, chunk)
            pe.wait_ge(s_bsp, 2)
            for h in range(SB_H):
                mm(ps_bz0[:, h, :], mixcol("after"), sp0[:, h, :], start=True, stop=False, skip_group_check=True)
                mm(ps_bz0[:, h, P:T], ones[:], sp1[:, h, :], start=False, stop=True, skip_group_check=True)
            for h in range(SB_H):
                r = mm(ps_bz1[:, h, :], mixcol("after"), sp1[:, h, :], start=True, stop=True)
            r.then_inc(s_baf, 1)
            stretch(pe, 26, 30, chunk)
            pe.wait_ge(s_bp, 2)
            pe.wait_ge(s_vev, 2)
            for h in range(SB_H):
                mm(ps_bo[:, h, :], vs[:, 0, SWA_H + h, :], e0[:, h, :], start=True, stop=False, skip_group_check=True)
                r = mm(ps_bo[:, h, P:T], vs[:, 1, SWA_H + h, :], e1[:, h, :], start=False, stop=True,
                       skip_group_check=True)
            r.then_inc(s_bo, 1)
            pe.wait_ge(s_wev, 30)
            pe.wait_ge(s_bx, 2)
            pe.wait_ge(s_modread, 2)
            for h in range(SWA_H):
                r = mm(ps_l1[:, h, :], z[:, QB + h, P:T], z[:, KB + h, :], start=True, stop=True)
            r.then_inc(s_sl, 1)
            pe.wait_ge(s_yc, 1)
            for h in range(SWA_H):
                r = mm(ps_l0[:, h, :], z[:, QB + h, 0:P], z[:, KB + h, 0:P], start=True, stop=True)
            r.then_inc(s_sl, 1)
            stretch(pe, 30, 36, chunk)
            pe.wait_ge(s_wev, 36)
            pe.wait_ge(s_slr, 2)
            turn_values([[(0, h) for h in range(4)], [(0, 4), (0, 5), (1, 0), (1, 1)], [(1, h) for h in range(2, 6)]],
                        [(VB, 0)] * 3)
            stretch(pe, 36, 40, chunk)
            pe.wait_ge(s_vev, 5)
            pe.wait_ge(s_sp, 2)
            for h in range(SWA_H):
                r = flip(ps_pt0[:, h, :], l0[:, h, :], ident)
            r.then_inc(s_spt, 1)
            for kt in range(2):
                for h in range(SWA_H):
                    r = flip(ps_pt1[:, kt, h, :], l1[:, h, kt * P:(kt + 1) * P], ident)
            r.then_inc(s_spt, 1)
            stretch(pe, 40, 42, chunk)
            pe.wait_ge(s_spe, 2)
            for h in range(SWA_H):
                mm(ps_so[:, h, :], vs[:, 0, h, :], pt0[:, h, :], start=True, stop=False, skip_group_check=True)
                r = mm(ps_so[:, h, P:T], vs[:, 1, h, :], pt1[:, h, :], start=False, stop=True, skip_group_check=True)
            r.then_inc(s_so, 1)
            mod_columns(0, 1)
            pe.wait_ge(s_modacc, M_G2)
            mod_columns(1, 0)
            pe.wait_ge(s_sq, 2)
            sum_squares(ps_ssq[2], squares1, range(12, 16))
            pe.wait_ge(s_sq, 3)
            sum_squares(ps_ssq[0], squares1, range(0, 6))
            pe.wait_ge(s_sq, 4)
            sum_squares(ps_ssq[1], squares1, range(6, 12))
            def x1_square(tile, n, first=False, last=False):
                pe.wait_ge(s_sqk, n)
                r = mm(banks(7, T), ones[:], sq_ring[:, tile % 4, :], start=first, stop=last, skip_group_check=True)
                return r

            def out_chunk(j, n, i, k):
                chunk(j, n, i, k, src=y_hi, tiles=(s_ylo, 0) if k == N_OUT else None)
                if k > N_OUT:
                    r = x1_square((k - N_OUT - 1) % 4, n - N_OUT, first=(k == N_OUT + 1 and isinstance(n, int)))
                    r.then_inc(s_ssq, 1)

            pe.wait_ge(s_modread, 3)
            for n in range(N_OUT, N_OUT + 4):
                out_chunk(n % 4, n, 0, n)
            stretch(pe, N_OUT + 4, N_WQ, out_chunk)
            x1_square(3, KD, last=True).then_inc(s_ssq, 1)
            pe.wait_ge(s_modacc, M_ALL)
            pe.wait_ge(s_ms, 3)
            mod_columns(2, 1)
            pe.wait_ge(s_subk, 16)

            def scores(hc):
                pe.wait_ge(s_wev, N_WQ + hc + 1)
                if hc >= 4:
                    pe.wait_ge(s_scr, hc - 3)
                for tt in range(TT):
                    r = mm(ps_sc[hc % 4][:, tt, :], qry[:, hc % 4, tt * P:(tt + 1) * P], subk_sb[:, hc, :],
                           start=True, stop=True)
                r.then_inc(s_sc, 1)

            for hc in range(HC):
                chunk((N_WQ + hc) % 4, N_WQ + hc, 0, N_WQ + hc, src=h_hi, tiles=None if hc else (s_h, KD))
                if hc:
                    scores(hc - 1)
            def h2_chunk(j, n, i, k):
                chunk(j, n, i, k, src=h_hi)

            h2_chunk(N_U % 4, N_U, 0, N_U)
            scores(HC - 1)
            for n in range(N_U + 1, N_U + 4):
                h2_chunk(n % 4, n, 0, n)
            stretch(pe, N_U + 4, N_U + FIRST, h2_chunk)
            for tt in range(TT):
                pe.wait_ge(s_pk, tt + 1)
                for i in range(3):
                    r = flip(ps_spread[tt][:, i, :], pick_t[:, tt, i].rearrange("p h k -> p (h k)"), ident)
                r.then_inc(s_pkt, 1)
            pe.wait_ge(s_pkr, 2)

            def spread(r_, n, first=False):
                pe.wait_ge(s_hot, n + 1)
                if not first:
                    pe.wait_ge(s_gev, n - (HOT_RING - 1))
                for t in range(GT):
                    r = mm(ps_spread[r_][:, t, :], hot_a[:, r_, t, :], hot_b[:, r_, t, :], start=True, stop=True)
                r.then_inc(s_gmm, 1)

            per = SPREADS // (EARLY - FIRST)

            def chunk_and_spreads(j, n, i, k):
                def between(kk):
                    if (kk + 1) % (KD // per) == 0:
                        m = (k - N_U - FIRST) * per + kk // (KD // per)
                        spread(m % HOT_RING, i * (4 * per) + m, first=(m < HOT_RING and isinstance(n, int)))

                chunk(j, n, i, k, src=h_hi, between=between)

            for n in range(N_U + FIRST, N_U + FIRST + 4):
                chunk_and_spreads(n % 4, n, 0, n)
            stretch(pe, N_U + FIRST + 4, N_U + EARLY, chunk_and_spreads)

            def u_block(j, n, i, k):
                pe.wait_ge(s_wlo, n - (N_U + EARLY - 1))
                pe.wait_ge(s_wev, n - 1)
                for kk in range(KD):
                    r = three(ps_w[k % 2], whi[:, j, kk, :], wlo[:, j, kk, :], h_hi[:, kk, :], h_lo[:, kk, :],
                              kk == 0, kk == KD - 1)
                r.then_inc(s_wmm, 1)

            for n in range(N_U + EARLY, N_U + LAG):
                u_block(n % 4, n, 0, n)

            v_ring = [(vhi[b], vlo[:, b]) for b in range(2 * GB)]
            w_ring = [tuple(w[:, (N_U + NB + b) % W_RING].rearrange("p k c -> p (k c)") for w in (whi, wlo))
                      for b in range(W_RING)]

            def v_group(half_, n, split, blocks, first=False, last=False):
                pe.wait_ge(s_plo, n + 1)
                for j in range(GB):
                    pe.wait_ge(split[0], split[1] + (j + 1))
                    wh, wl = phi[:, half_, j, 0:P], plo[:, half_, j, 0:P]
                    for u in range(4):
                        vh, vl = (v[:, u * 512:(u + 1) * 512] for v in blocks[j])
                        mm(ps_y0[u], wh, vh, start=(first and j == 0), stop=False, skip_group_check=True)
                        mm(ps_y0[u], wh, vl, start=False, stop=False, skip_group_check=True)
                        r = mm(ps_y0[u], wl, vh, start=False, stop=(last and j == GB - 1), skip_group_check=True)
                if last:
                    r.then_inc(s_y0mm, 1)
                for u in range(4):
                    if not (first and u < 2):
                        pe.wait_ge(s_yadd, n * 4 + (u - 1))
                    for j in range(GB):
                        wh, wl = phi[:, half_, j, P:T], plo[:, half_, j, P:T]
                        vh, vl = (v[:, u * 512:(u + 1) * 512] for v in blocks[j])
                        mm(ps_y1[u % 2], wh, vh, start=(j == 0), stop=False)
                        mm(ps_y1[u % 2], wh, vl, start=False, stop=False)
                        r = mm(ps_y1[u % 2], wl, vh, start=False, stop=(j == GB - 1))
                    r.then_inc(s_vmm, 1)

            def from_v(g, n, m, **kw):
                v_group(g, n, (s_vlo, m * GB), v_ring[g * GB:g * GB + GB], **kw)

            def from_w(g, n, m, **kw):
                v_group(g, n, (s_wlo, m - (N_U + EARLY)), w_ring[g * GB:g * GB + GB], **kw)

            loops = (NB - LAG) // (2 * GB)
            for g in range(2):
                for j in range(GB):
                    n = N_U + LAG + g * GB + j
                    u_block(n % 4, n, 0, n)
                from_v(g, g, g, first=(g == 0))
            with pe.Fori(1, loops) as i:
                for g in range(2):
                    for j in range(GB):
                        n = N_U + LAG + g * GB + j
                        u_block(n % 4, i * (2 * GB) + n, i, n)
                    from_v(g, i * 2 + g, i * 2 + g)

            def turn(i, last=False):
                for g in range(2):
                    from_v(g, i * 4 + (V_TAIL - 2 + g), i * 2 + (V_TAIL - 2 + g))
                for g in range(2):
                    from_w(g, i * 4 + (V_TAIL + g), i * (2 * GB) + (N_U + NB + g * GB), last=(last and g == 1))

            with pe.Fori(0, TAILS - 1) as i:
                turn(i)
            turn(TAILS - 1, last=True)
            pe.wait_ge(s_y0e, 4)
            pe.wait_ge(s_yadd, NV * 4)
            for kk in range(KD):
                if kk >= 4:
                    pe.wait_ge(s_x2, kk - 3)
                flip(banks(kk % 4, TT, P)[:, 0, :], y0[:, kk * P:(kk + 1) * P], ident)
                flip(banks(kk % 4, TT, P)[:, 1, :], yacc[:, kk * P:(kk + 1) * P], ident).then_inc(s_yt, 1)
            for kk in range(KD):
                pe.wait_ge(s_sqk, KD + kk + 1)
                r = mm(banks(7, T), ones[:], squares3[:, kk, :], start=(kk == 0), stop=(kk == KD - 1))
                r.then_inc(s_ssq, 1)

        @block.scalar
        def _(act):
            A = nc.scalar.activation
            own = Steps(act, s_act)

            act.wait_ge(s_par, 16)
            A(csil, pcol("c"), ACT.Exp, scale=-1.0).then_inc(s_silu_e, 1)
            own.did(A(tiny[0], pcol("lam"), ACT.Abs))
            own.settle()
            A(tiny[1], tiny[0], ACT.Exp, scale=-1.0).then_inc(s_lam, 1)
            act.wait_ge(s_x, 16)
            A(squares0[:], x0[:], ACT.Square).then_inc(s_sq, 1)

            def root(n, m):
                act.wait_ge(s_ms, n)
                A(ms[:, 0:m, :], ms[:, 0:m, :], ACT.Sqrt).then_inc(s_root, 1)

            root(1, 1)
            act.wait_ge(s_relps, 1)
            A(rel_rows[:], ps[:, 0:SWA_H, 0:N_SHIFT], ACT.Copy).then_inc(s_relrow, 1)

            def load_w(slot, n):
                act.dma_start(wraw[:, slot], wst[bass.ds(n, 1)].rearrange("o p k c -> (o p) k c")).then_inc(s_w[slot], 16)

            def chunk_hi(i, k):
                act.wait_ge(s_w[k % 4], turns(i, k, W_RING) * 16)
                for half in range(2):
                    kk = slice(half * (KD // 2), (half + 1) * (KD // 2))
                    A(chi[:, k % 2, kk], wraw[:, k % 4, kk], ACT.Copy).then_inc(s_chi, 1)

            def multiplied(j, n, i, k):
                act.wait_ge(s_wmm, n + 1)
                load_w(j, n + 4)
                if k < N_U + EARLY - 2:
                    chunk_hi(i, k + 2)

            act.wait_ge(s_modacc, M_G1 - 3)
            for n in range(W_RING):
                load_w(n, n)
            act.wait_ge(s_h0, 1)
            chunk_hi(0, 0)

            def h_upper(dst, shift, base):
                for kk in range(KD):
                    act.wait_ge(s_xn, base + kk + 1)
                    A(dst[:, kk, :], hid[:, kk, :], ACT.Identity, bias=modv[:, shift, kk:kk + 1]).then_inc(s_hhi, 1)

            act.wait_ge(s_modread, 1)
            h_upper(h1_hi, 0, 0)
            chunk_hi(0, 1)

            def evac(j, n, i, k):
                multiplied(j, n, i, k)
                A(tile_of(z, n if k < GA else n - GA), ps_w[k % 2], ACT.Copy).then_inc(s_wev, 1)

            stretch(act, 0, 12, evac)
            for g, (dst, bias) in enumerate(((rg, "b_rec"), (ig, "b_in"))):
                act.wait_ge(s_gate, g + 1)
                for n in range(LRU_N):
                    r = A(dst[:, n, :], ps_gates[:, g, n, :], ACT.Sigmoid, bias=pcol(bias, n, 1))
                r.then_inc(s_sig, 1)
            stretch(act, 12, 14, evac)
            act.wait_ge(s_lam, 2)
            act.wait_ge(s_sig, 2)
            for n in range(LRU_N):
                own.did(A(th[:, n, :], rg[:, n, :], ACT.Tanh, scale=decay[:, n:n + 1]))
            own.settle()
            for n in range(LRU_N):
                r = A(rg[:, n, :], rg[:, n, :], ACT.Exp, scale=ndecay[:, n:n + 1])
            r.then_inc(s_a, 1)
            stretch(act, 14, 16, evac)
            act.wait_ge(s_var, 1)
            A(th[:], th[:], ACT.Sqrt).then_inc(s_sqrt, 1)
            stretch(act, 16, 19, evac)

            def values(first, m):
                for g in range(m):
                    act.wait_ge(s_vt, first + g + 1)
                    if first == 0:
                        A(vs[:, g, SWA_H:], ps_vt[g], ACT.Copy).then_inc(s_vev, 1)
                    elif g == 0:
                        A(vs[:, 0, 0:4], ps_vt[0], ACT.Copy).then_inc(s_vev, 1)
                    elif g == 1:
                        own.did(A(vs[:, 0, 4:6], ps_vt[1][:, 0:2], ACT.Copy))
                        A(vs[:, 1, 0:2], ps_vt[1][:, 2:4], ACT.Copy).then_inc(s_vev, 1)
                    else:
                        A(vs[:, 1, 2:6], ps_vt[2], ACT.Copy).then_inc(s_vev, 1)

            values(0, 2)
            stretch(act, 19, 21, evac)
            act.wait_ge(s_bzr, 2)
            own.did(A(e0[:], zs0[:], ACT.Abs))
            own.did(A(e1[:], zs1[:], ACT.Abs))
            own.settle()
            own.did(A(e0[:], e0[:], ACT.Exp, scale=-1.0))
            own.did(A(e1[:], e1[:], ACT.Exp, scale=-1.0))
            own.settle()
            for e_ in (e0, e1):
                A(e_[:], e_[:], ACT.Ln, bias=1.0).then_inc(s_bln, 1)
            stretch(act, 21, 27, evac)
            act.wait_ge(s_bx, 2)
            for e_ in (e0, e1):
                A(e_[:], e_[:], ACT.Exp).then_inc(s_bex, 1)
            stretch(act, 27, 32, evac)
            act.wait_ge(s_sm, 1)
            A(l1[:], l1[:], ACT.Exp).then_inc(s_se, 1)
            stretch(act, 32, 34, evac)
            act.wait_ge(s_sm, 2)
            A(l0[:], l0[:], ACT.Exp).then_inc(s_se, 1)
            stretch(act, 34, 37, evac)
            values(2, 3)
            stretch(act, 37, 41, evac)
            act.wait_ge(s_spt, 1)
            act.wait_ge(s_sl, 2)
            own.did(A(pt0[:, :, 0:P], ps_pt0, ACT.Copy))
            act.wait_ge(s_spt, 2)
            A(pt0[:, :, P:T], ps_pt1[:, 0], ACT.Copy).then_inc(s_spe, 1)
            A(pt1[:], ps_pt1[:, 1], ACT.Copy).then_inc(s_spe, 1)
            stretch(act, 41, 42, evac)
            act.wait_ge(s_wev, NZ)
            A(z[:, 0:LRU_N], z[:, 0:LRU_N], ACT.Gelu_apprx_tanh).then_inc(s_gelu, 1)
            act.wait_ge(s_yc, 1)
            A(squares1[:, 12:16], yc[:], ACT.Square).then_inc(s_sq, 1)
            act.wait_ge(s_ya, 1)
            A(squares1[:, 0:6], hid[:, 0:6], ACT.Square).then_inc(s_sq, 1)
            act.wait_ge(s_yb, 1)
            A(squares1[:, 6:12], hid[:, 6:12], ACT.Square).then_inc(s_sq, 1)
            root(2, 3)
            for kk in range(KD):
                act.wait_ge(s_y, kk + 1)
                A(y_hi[:, kk, :], hid[:, kk, :], ACT.Copy).then_inc(s_yhi, 1)

            def square_tile(j, n, i, k):
                multiplied(j, n, i, k)
                act.wait_ge(s_wev, n + 1)
                if not (isinstance(n, int) and n < N_OUT + 4):
                    act.wait_ge(s_ssq, n - (N_OUT + 4) + 1 + 4)
                A(sq_ring[:, (k - N_OUT) % 4, :], tile_of(res, n - N_OUT), ACT.Square).then_inc(s_sqk, 1)

            for n in range(N_OUT, N_OUT + 4):
                square_tile(n % 4, n, 0, n)
            stretch(act, N_OUT + 4, N_WQ, square_tile)
            root(3, 1)
            h_upper(h_hi, 3, KD)

            def score_out(hc):
                act.wait_ge(s_sc, hc + 1)
                A(score[:, :, hc, :], ps_sc[hc % 4], ACT.Copy).then_inc(s_scr, 1)

            for hc in range(HC):
                multiplied((N_WQ + hc) % 4, N_WQ + hc, 0, N_WQ + hc)
                if hc >= 4:
                    act.wait_ge(s_sc, hc - 3)
                A(qry[:, hc % 4, :], ps_w[hc % 2], ACT.Copy).then_inc(s_wev, 1)
                if hc:
                    score_out(hc - 1)

            def gelu(n, k, b):
                act.wait_ge(s_wmm, n + 1)
                A(tile_of(act_u, b % LAG), ps_w[k % 2], ACT.Gelu_apprx_tanh).then_inc(s_wev, 1)

            def early_gelu(b):
                n = N_U + b
                multiplied(n % 4, n, 0, n)
                gelu(n, n, b)

            act.wait_ge(s_spill, 16)
            early_gelu(0)
            score_out(HC - 1)
            for b in range(1, FIRST):
                early_gelu(b)
                if b in (FIRST // 2 - 1, FIRST - 1):
                    tt = b // (FIRST // 2)
                    act.wait_ge(s_gx, tt + 1)
                    A(pick_t[:, tt, 2], pick_t[:, tt, 2], ACT.Exp).then_inc(s_ge, 1)
            for tt in range(TT):
                act.wait_ge(s_pkt, tt + 1)
                A(picks[:, :, tt * P:(tt + 1) * P], ps_spread[tt][:, 0:3], ACT.Copy).then_inc(s_pkr, 1)

            per = SPREADS // (EARLY - FIRST)
            for q in range(TQ):
                if q >= 2:
                    act.wait_ge(s_gst[q - 2], 16)
                for b in range(FIRST + 2 * q, FIRST + 2 * q + 2):
                    m0 = (b - FIRST) * per
                    with act.Fori(0, per // HOT_RING) as i:
                        for r_ in range(HOT_RING):
                            act.wait_ge(s_gmm, i * HOT_RING + (m0 + r_ + 1))
                            A(gstage[:, q % 2, :, bass.ds((i * HOT_RING + (m0 - q * 2 * per + r_)) * GT, GT)],
                              ps_spread[r_].rearrange("p t b -> p b t"), ACT.Copy).then_inc(s_gev, 1)
                    early_gelu(b)
                act.wait_ge(s_gev, (q + 1) * 2 * per)
                act.dma_start(gates_dram[q], gstage[:, q % 2]).then_inc(s_gst[q], 16)

            def w_hi(j, n, i, k):
                act.wait_ge(s_w[j], turns(i, k, W_RING) * 16)
                A(whi[:, j], wraw[:, j], ACT.Copy).then_inc(s_whi, 1)

            def v_hi(b, i, m):
                act.wait_ge(s_v[b], i * 16 + (m + 1) * 16)
                A(vhi[b], vraw[:, b], ACT.Copy).then_inc(s_vhi, 1)

            def p_hi(half_, n):
                act.wait_ge(s_pm, n + 1)
                A(phi[:, half_], praw[:, half_], ACT.Copy).then_inc(s_phi, 1)

            act.wait_ge(s_gst[2], 16)
            for n in range(N_U + EARLY, N_U + LAG):
                w_hi(n % 4, n, 0, n)
            for b in range(EARLY, LAG):
                gelu(N_U + b, b, b)
                if b < EARLY + GB:
                    n = N_U + b + 4
                    w_hi(n % 4, n, 0, n)
            v_hi(0, 0, 0)
            v_hi(1, 0, 0)
            p_hi(0, 0)

            def ahead(g, i, u_next=True):
                n = i * 2 + g
                if u_next:
                    for j in range(GB):
                        k = N_U + LAG + GB + g * GB + j
                        w_hi(k % 4, 0, i, k)
                k = LAG + g * GB
                gelu(i * (2 * GB) + (N_U + k), k, i * (2 * GB) + k)
                for j in range(GB):
                    k = (g + 1) * GB + j
                    v_hi(k % 4, i, k // 4)
                p_hi(1 - g, n + 1)
                k = LAG + g * GB + 1
                gelu(i * (2 * GB) + (N_U + k), k, i * (2 * GB) + k)

            loops = (NB - LAG) // (2 * GB)
            with act.Fori(0, loops - 1) as i:
                for g in range(2):
                    ahead(g, i)
            ahead(0, loops - 1)
            ahead(1, loops - 1, u_next=False)
            def v_next(g, i, n, m):
                for j in range(GB):
                    v_hi(g * GB + j, i, m)
                p_hi(g, n)

            def w_next(g, i):
                for j in range(GB):
                    k = N_U + NB + g * GB + j
                    w_hi(k % 4, 0, i, k)
                p_hi(g, i * 4 + (V_TAIL + g))

            turn = V_TAIL // 2 - 1
            with act.Fori(0, TAILS - 1) as i:
                v_next(1, i, i * 4 + (V_TAIL - 1), turn)
                w_next(0, i)
                w_next(1, i)
                v_next(0, i, i * 4 + (V_TAIL + 2), turn + 1)
            v_next(1, 0, NV - 3, turn + TAILS - 1)
            w_next(0, TAILS - 1)
            w_next(1, TAILS - 1)
            act.wait_ge(s_y0mm, 1)
            for u in range(4):
                A(y0[:, u * 512:(u + 1) * 512], ps_y0[u], ACT.Copy).then_inc(s_y0e, 1)
            act.wait_ge(s_vmm, NV * 4)
            for kk in range(KD):
                act.wait_ge(s_x2, kk + 1)
                A(squares3[:, kk, :], res2[:, kk, :], ACT.Square).then_inc(s_sqk, 1)
            root(4, 1)

        @block.vector
        def _(dve):
            V = nc.vector
            own = Steps(dve, s_dve)

            def mean_root(srcs, sums, n):
                dve.wait_ge(s_ssq, sums)
                for i, (src, width) in enumerate(srcs):
                    r = V.tensor_scalar(ms[:, i, :], src, 1.0 / width, EPS, ALU.mult, ALU.add)
                    if i < len(srcs) - 1:
                        own.did(r)
                own.settle()
                r.then_inc(s_ms, 1)
                dve.wait_ge(s_root, n)
                own.did(V.reciprocal(rstd[:, 0:len(srcs), :], ms[:, 0:len(srcs), :]))
                own.settle()

            V.memset(ones[:], 1.0).then_inc(s_ones, 1)
            dve.wait_ge(s_silu_e, 1)
            own.did(V.tensor_scalar(csil, csil, 1.0, None, ALU.add)); own.settle()
            own.did(V.reciprocal(csil, csil)); own.settle()
            own.did(V.tensor_tensor(csil, csil, pcol("c"), ALU.mult)); own.settle()

            def add_mod(q, kk, tile, loaded, done, first):
                dve.wait_ge(*loaded)
                col = csil[:, kk:kk + 1] if isinstance(kk, int) else csil[:, bass.ds(kk, 1)]
                if first:
                    V.tensor_scalar(mod_acc[q][:], tile, col, None, ALU.mult).then_inc(s_modacc, 1)
                else:
                    dve.wait_ge(s_modacc, done)
                    V.scalar_tensor_tensor(mod_acc[q][:], tile, col, mod_acc[q][:], ALU.mult,
                                           ALU.add).then_inc(s_modacc, 1)

            def mod0(j, n, i, k):
                add_mod(k // KD, i * 4 + k % KD, mod_ring0[:, j], (s_m0[j], turns(i, k, M_RING0) * 16), n, k % KD == 0)

            def mod_one(j, n, i, k):
                part, kk = (k - M_G1) // KD, (k - M_G1) % KD
                add_mod(part % 2, i * 4 + kk, mod_ring[:, k % 2], (s_m[k % 2], i * 32 + ((k - M_G1) // 2 + 1) * 16), n,
                        kk == 0)

            for n in range(4):
                mod0(n, n, 0, n)
            mean_root([(banks(7, T), D)], 1, 1)
            V.tensor_tensor(hid[:], x0[:], rstd[:, 0:1, :].to_broadcast([P, KD, T]), ALU.mult).then_inc(s_h0, 1)
            dve.wait_ge(s_rel, 32)
            V.tensor_copy(relw[0:BUCKETS], relb_sb[0:BUCKETS].unsqueeze(2).to_broadcast([BUCKETS, SWA_H, P])).then_inc(s_relw, 1)
            stretch(dve, 4, KD, mod0)
            for n in range(KD, KD + 4):
                mod0(n % 4, n, 0, n)
            dve.wait_ge(s_modcol, 1)
            own.did(V.tensor_tensor(modv[:, 1, :], ps_modcol[:, 0, :], pcol("b_mod", KD, KD), ALU.add))
            own.settle()
            V.scalar_tensor_tensor(coef[:, 0, :], modv[:, 1, :], 1.0, pcol("norm_mix"), ALU.add,
                                   ALU.mult).then_inc(s_coef, 1)
            dve.wait_ge(s_coef, 1)
            for kk in range(KD):
                V.tensor_scalar(hid[:, kk, :], hid[:, kk, :], coef[:, 0, kk:kk + 1], None, ALU.mult).then_inc(s_xn, 1)
            stretch(dve, KD + 4, 2 * KD - 4, mod0)
            for n in range(2 * KD - 4, 2 * KD - 1):
                mod0(n % 4, n, 0, n)
            n = 2 * KD - 1
            dve.wait_ge(s_m0[n % 4], turns(0, n, M_RING0) * 16)
            dve.wait_ge(s_modacc, n)
            for u in range(4):
                sl = slice(u * 512, (u + 1) * 512)
                r = V.scalar_tensor_tensor(mod_acc[1][:, sl], mod_ring0[:, n % 4, sl], csil[:, KD - 1:KD],
                                           mod_acc[1][:, sl], ALU.mult, ALU.add)
                r.then_inc(s_modlast if u < 3 else s_modacc, 1)
            dve.wait_ge(s_modcol, 2)
            V.tensor_tensor(modv[:, 0, :], ps_modcol[:, 1, :], pcol("b_mod", 0, KD), ALU.add).then_inc(s_modread, 1)

            def h_lower(hi, shift, base):
                for kk in range(KD):
                    dve.wait_ge(s_hhi, base + kk + 1)
                    V.scalar_tensor_tensor(h_lo[:, kk, :], hid[:, kk, :], modv[:, shift, kk:kk + 1],
                                           hi[:, kk, :].bitcast(F32), ALU.add, ALU.subtract).then_inc(s_h, 1)

            dve.wait_ge(s_modread, 1)
            h_lower(h1_hi, 0, 0)
            dve.wait_ge(s_relt, 16)
            dve.wait_ge(s_cst, 32)
            own.did(V.tensor_tensor(relbias[:], relbias[:], mixcol("bar").unsqueeze(1).to_broadcast([P, SWA_H, T]),
                                    ALU.add))
            dve.wait_ge(s_lam, 1)
            e, s_, s2, acc = tiny[1], tiny[2], tiny[3], tiny[4]
            own.did(V.tensor_scalar(s_, e, 2.0, None, ALU.add)); own.settle()
            own.did(V.reciprocal(s_, s_)); own.settle()
            own.did(V.tensor_tensor(s_, s_, e, ALU.mult)); own.settle()
            own.did(V.tensor_tensor(s2, s_, s_, ALU.mult)); own.settle()
            own.did(V.tensor_scalar(acc, s2, 1.0 / 19, 1.0 / 17, ALU.mult, ALU.add)); own.settle()
            for n in (15, 13, 11, 9, 7, 5, 3, 1):
                own.did(V.tensor_tensor(acc, acc, s2, ALU.mult)); own.settle()
                own.did(V.tensor_scalar(acc, acc, 1.0 / n, None, ALU.add)); own.settle()
            own.did(V.tensor_tensor(acc, acc, s_, ALU.mult)); own.settle()
            own.did(V.tensor_scalar(tiny[5], pcol("lam"), -1.0, 0.0, ALU.mult, ALU.max)); own.settle()
            own.did(V.scalar_tensor_tensor(tiny[5], acc, 2.0, tiny[5], ALU.mult, ALU.add)); own.settle()
            own.did(V.tensor_scalar(decay, tiny[5], LRU_C, None, ALU.mult)); own.settle()
            V.tensor_scalar(ndecay, tiny[5], -LRU_C, None, ALU.mult).then_inc(s_lam, 1)
            for n in range(M_G1, M_G1 + 4):
                mod_one(n % 4, n, 0, n)
            for n in range(M_G1 + 4, M_G1 + 8):
                mod_one(n % 4, n, 0, n)
            dve.wait_ge(s_wev, LRU_N)
            for n in range(LRU_N):
                own.did(V.tensor_scalar(cx[:, n, :], z[:, XA + n, :], pcol("conv_w", 3 * LRU_N + n, 1),
                                        pcol("conv_b", n, 1), ALU.mult, ALU.add))
            for j in (2, 1, 0):
                s = CONV_W - 1 - j
                own.settle()
                for n in range(LRU_N):
                    r = V.scalar_tensor_tensor(cx[:, n, s:T], z[:, XA + n, 0:T - s], pcol("conv_w", j * LRU_N + n, 1),
                                               cx[:, n, s:T], ALU.mult, ALU.add)
                    if j or n < LRU_N - 1:
                        own.did(r)
            own.settle()
            r.then_inc(s_conv, 1)
            stretch(dve, M_G1 + 8, M_H2, mod_one)
            for n in range(M_H2, M_H2 + 4):
                mod_one(n % 4, n, 0, n)
            stretch(dve, M_H2 + 4, M_H2 + 8, mod_one)
            dve.wait_ge(s_a, 1)
            dve.wait_ge(s_conv, 1)
            own.did(V.tensor_tensor(ig[:], ig[:], cx[:], ALU.mult))
            asq = z[:, XA:XA + LRU_N]
            own.did(V.tensor_tensor(asq, rg[:], rg[:], ALU.mult)); own.settle()
            V.scalar_tensor_tensor(th[:], asq, 1.0, th[:], ALU.add, ALU.mult).then_inc(s_var, 1)
            stretch(dve, M_H2 + 8, M_H2 + 12, mod_one)
            dve.wait_ge(s_sqrt, 1)
            own.did(V.tensor_tensor(ig[:], ig[:], th[:], ALU.mult)); own.settle()
            for n in range(LRU_N):
                own.did(V.tensor_tensor_scan(th[:, n, :], rg[:, n, :], ig[:, n, :], 0.0, ALU.mult, ALU.add))
            own.settle()
            dve.wait_ge(s_bz, 1)
            V.tensor_scalar(zs0[:], ps_bz0, HEAD_SCALE, None, ALU.mult).then_inc(s_bzr, 1)
            V.tensor_scalar(zs1[:], ps_bz1, HEAD_SCALE, None, ALU.mult).then_inc(s_bzr, 1)
            stretch(dve, M_H2 + 12, M_H2 + 16, mod_one)

            def strict(w):
                return mixcol("strict")[:, 0:w].unsqueeze(1).to_broadcast([P, SB_H, w])

            for i, (s, z_, e_, w) in enumerate(((sp0, zs0, e0, T), (sp1, zs1, e1, P))):
                dve.wait_ge(s_bln, i + 1)
                own.did(V.scalar_tensor_tensor(s[:], z_[:], 0.0, e_[:], ALU.max, ALU.add)); own.settle()
                own.did(V.tensor_tensor(z_[:], z_[:], s[:], ALU.subtract)); own.settle()
                V.tensor_tensor(s[:], s[:], strict(w), ALU.mult).then_inc(s_bsp, 1)
            dve.wait_ge(s_modcol, 3)
            V.tensor_tensor(modv[:, 2, :], ps_modcol[:, 2, :], pcol("b_mod", 2 * KD, KD), ALU.add).then_inc(s_modread, 1)
            for n in range(M_H2 + KD, M_H2 + KD + 8):
                mod_one(n % 4, n, 0, n)
            dve.wait_ge(s_baf, 1)
            for e_, z_, ps_ in ((e0, zs0, ps_bz0), (e1, zs1, ps_bz1)):
                V.tensor_tensor(e_[:], z_[:], ps_, ALU.subtract).then_inc(s_bx, 1)
            stretch(dve, M_H2 + 24, M_H2 + 28, mod_one)
            for i, (e_, w) in enumerate(((e0, T), (e1, P))):
                dve.wait_ge(s_bex, i + 1)
                V.tensor_tensor(e_[:], e_[:], strict(w), ALU.mult).then_inc(s_bp, 1)
            dve.wait_ge(s_bo, 1)
            V.tensor_copy(yc[:], ps_bo).then_inc(s_yc, 1)

            def swa_shift(i, l, src, width):
                dve.wait_ge(s_sl, i + 1)
                V.scalar_tensor_tensor(l[:], src, HEAD_SCALE, relbias[:, :, T - width:T], ALU.mult,
                                       ALU.add).then_inc(s_slr, 1)
                dve.wait_ge(s_slr, i + 1)
                top = stat[:, 8 * i:8 * i + SWA_H]
                own.did(V.tensor_reduce(top, l[:], AX.X, ALU.max)); own.settle()
                V.tensor_tensor(l[:], l[:], top.unsqueeze(2).to_broadcast([P, SWA_H, width]),
                                ALU.subtract).then_inc(s_sm, 1)

            def swa_probs(i, l, width):
                dve.wait_ge(s_se, i + 1)
                times = mixcol("times", T - width).unsqueeze(1).to_broadcast([P, SWA_H, width])
                own.did(V.tensor_tensor(l[:], l[:], times, ALU.mult)); own.settle()
                tot = stat[:, 16 + 8 * i:16 + 8 * i + SWA_H]
                own.did(V.tensor_reduce(tot, l[:], AX.X, ALU.add)); own.settle()
                own.did(V.reciprocal(tot, tot)); own.settle()
                V.tensor_tensor(l[:], l[:], tot.unsqueeze(2).to_broadcast([P, SWA_H, width]), ALU.mult).then_inc(s_sp, 1)

            swa_shift(0, l1, ps_l1, T)
            swa_shift(1, l0, ps_l0, P)
            swa_probs(0, l1, T)
            swa_probs(1, l0, P)
            stretch(dve, M_H2 + 28, M_G2, mod_one)
            dve.wait_ge(s_gelu, 1)
            dve.wait_ge(s_wmm, NZ)
            V.tensor_tensor(hid[:, 0:LRU_N], th[:], z[:, 0:LRU_N], ALU.mult).then_inc(s_ya, 1)
            dve.wait_ge(s_so, 1)
            V.tensor_copy(hid[:, 6:12], ps_so).then_inc(s_yb, 1)
            dve.wait_ge(s_modcol, 5)
            V.tensor_tensor(modv[:, 3:5, :], ps_modcol[:, 0:2, :],
                            pcol("b_mod", 3 * KD, 2 * KD).rearrange("p (a b) -> p a b", a=2), ALU.add).then_inc(s_modread, 1)
            own.settle()
            dve.wait_ge(s_modread, 3)
            V.scalar_tensor_tensor(coef[:, 1, :], modv[:, 4, :], 1.0, pcol("norm_ffn"), ALU.add,
                                   ALU.mult).then_inc(s_coef, 1)
            mean_root([(ps_ssq[0], 768), (ps_ssq[1], 768), (ps_ssq[2], 512)], 4, 2)

            def y_lower(kk):
                dve.wait_ge(s_yhi, kk + 1)
                V.tensor_tensor(h_lo[:, kk, :], hid[:, kk, :], y_hi[:, kk, :].bitcast(F32), ALU.subtract).then_inc(s_ylo, 1)

            for kk in range(KD):
                src = hid[:, kk, :] if kk < 12 else yc[:, kk - 12, :]
                V.scalar_tensor_tensor(hid[:, kk, :], src, pcol("gnorm", kk, 1),
                                       rstd[:, 0 if kk < 6 else 1 if kk < 12 else 2, :], ALU.mult,
                                       ALU.mult).then_inc(s_y, 1)
                if kk >= 2:
                    y_lower(kk - 2)
            y_lower(KD - 2)
            y_lower(KD - 1)

            def x1_tile(j, n, i, k):
                dve.wait_ge(s_wmm, n + 1)
                if k == N_OUT:
                    dve.wait_ge(s_x, 32)
                x_ = tile_of(res, n - N_OUT)
                V.scalar_tensor_tensor(x_, ps_w[k % 2], modv[:, 2, bass.ds(n - N_OUT, 1)], x_, ALU.mult,
                                       ALU.add).then_inc(s_wev, 1)
                m = k - N_OUT + M_G2
                mod_one(m % 4, n - N_OUT + M_G2, i, m)

            for n in range(N_OUT, N_OUT + 4):
                x1_tile(n % 4, n, 0, n)
            stretch(dve, N_OUT + 4, N_WQ, x1_tile)
            mean_root([(banks(7, T), D)], 4 + KD, 3)
            for kk in range(KD):
                V.scalar_tensor_tensor(hid[:, kk, :], res[:, kk, :], coef[:, 1, kk:kk + 1], rstd[:, 0, :], ALU.mult,
                                       ALU.mult).then_inc(s_xn, 1)
            h_lower(h_hi, 3, KD)
            dve.wait_ge(s_modcol, 6)
            V.tensor_tensor(modv[:, 5, :], ps_modcol[:, 2, :], pcol("b_mod", 5 * KD, KD), ALU.add).then_inc(s_modread, 1)

            def top16(rows):
                for vals, idx, src, rest in rows:
                    own.did(V.max(vals[:, 0:8], src))
                own.settle()
                for vals, idx, src, rest in rows:
                    own.did(V.match_replace(rest, vals[:, 0:8], src, TAKEN))
                    own.did(V.max_index(idx[:, 0:8], vals[:, 0:8], src))
                own.settle()
                for vals, idx, src, rest in rows:
                    own.did(V.max(vals[:, 8:16], rest))
                own.settle()
                for vals, idx, src, rest in rows:
                    own.did(V.max_index(idx[:, 8:16], vals[:, 8:16], rest))

            for hc in range(HC):
                dve.wait_ge(s_scr, hc + 1)
                top16([(top_v[:, tt, hc], top_i[:, tt, hc], score[:, tt, hc], left[:, tt, hc]) for tt in range(TT)])
            own.settle()
            own.did(V.tensor_copy(top_f[:], top_i[:]))
            quad = [P, PEER_H, TOPK, TOPK]
            tri = [P, PEER_H, TOPK]
            c4 = cand[:].rearrange("p h (i j) -> p h i j", i=TOPK)
            e4 = eqs[:].rearrange("p h (i j) -> p h i j", i=TOPK)
            iota4 = iota[:, 0:TOPK].unsqueeze(1).unsqueeze(1).to_broadcast(quad)
            for tt in range(TT):
                tv = top_v[:, tt].rearrange("p (h c) k -> p h c k", c=2)
                tf = top_f[:, tt].rearrange("p (h c) k -> p h c k", c=2)
                gate = pick_t[:, tt, 2]
                own.did(V.tensor_tensor(c4, tv[:, :, 0].unsqueeze(3).to_broadcast(quad),
                                        tv[:, :, 1].unsqueeze(2).to_broadcast(quad), ALU.add))
                own.settle()
                top16([(gate[:, h], best_i[:, h].bitcast(U32), cand[:, h], cleft[:, h]) for h in range(PEER_H)])
                own.settle()
                own.did(V.tensor_copy(stat[:, 0:PEER_H], gate[:, :, 0])); own.settle()
                V.tensor_tensor(gate, gate, stat[:, 0:PEER_H].unsqueeze(2).to_broadcast(tri),
                                ALU.subtract).then_inc(s_gx, 1)
                for c in range(2):
                    if c == 0:
                        own.did(V.tensor_scalar(half_i[:], best_i[:], 4, None, ALU.arith_shift_right))
                    else:
                        own.did(V.tensor_scalar(half_i[:], best_i[:], TOPK - 1, None, ALU.bitwise_and))
                    own.settle()
                    own.did(V.tensor_copy(half_f[:], half_i[:])); own.settle()
                    own.did(V.tensor_tensor(e4, iota4, half_f[:].unsqueeze(3).to_broadcast(quad), ALU.is_equal)); own.settle()
                    own.did(V.tensor_tensor(e4, e4, tf[:, :, c].unsqueeze(2).to_broadcast(quad), ALU.mult)); own.settle()
                    own.did(V.tensor_reduce(pick_t[:, tt, c], e4, AX.X, ALU.add)); own.settle()
                dve.wait_ge(s_ge, tt + 1)
                tot = stat[:, 8:8 + PEER_H]
                own.did(V.tensor_reduce(tot, gate, AX.X, ALU.add)); own.settle()
                own.did(V.reciprocal(tot, tot)); own.settle()
                V.tensor_tensor(gate, gate, tot.unsqueeze(2).to_broadcast(tri), ALU.mult).then_inc(s_pk, 1)

            dve.wait_ge(s_pkr, 2)

            def one_hots(r_, n, first=False):
                if not first:
                    dve.wait_ge(s_gmm, n - (HOT_RING - 1))
                V.tensor_tensor(hot_a[:, r_], iota.unsqueeze(1).to_broadcast([P, GT, P]),
                                picks[:, 0, bass.ds(n * GT, GT)].unsqueeze(2).to_broadcast([P, GT, P]), ALU.is_equal)
                for t in range(GT):
                    b, g = (picks[:, i, bass.ds(n * GT + t, 1)] for i in (1, 2))
                    r = V.tensor_scalar(hot_b[:, r_, t, :], iota, b, g, ALU.is_equal, ALU.mult)
                r.then_inc(s_hot, 1)

            for n in range(HOT_RING):
                one_hots(n, n, True)
            with dve.Fori(1, SPREADS // HOT_RING) as i:
                for r_ in range(HOT_RING):
                    one_hots(r_, i * HOT_RING + r_)
            def w_lo(j, n):
                dve.wait_ge(s_whi, n - (N_U + EARLY - 1))
                V.tensor_tensor(wlo[:, j], wraw[:, j], whi[:, j].bitcast(F32), ALU.subtract).then_inc(s_wlo, 1)

            def v_lo(b, n):
                dve.wait_ge(s_vhi, n + 1)
                V.tensor_tensor(vlo[:, b], vraw[:, b], vhi[b].bitcast(F32), ALU.subtract).then_inc(s_vlo, 1)

            def p_mul(half_, n, first=False):
                dve.wait_ge(s_g[half_], (n - half_) * 8 + 16)
                for j in range(GB):
                    b = n * GB + j
                    r = V.tensor_tensor(praw[:, half_, j].rearrange("p (q t) -> p q t", q=TQ),
                                        tile_of(act_u, b % LAG).rearrange("p (q t) -> p q t", q=TQ),
                                        gring[:, half_, :, j, :], ALU.mult)
                r.then_inc(s_pm, 1)

            def p_lo(half_, n):
                dve.wait_ge(s_phi, n + 1)
                V.tensor_tensor(plo[:, half_], praw[:, half_], phi[:, half_].bitcast(F32),
                                ALU.subtract).then_inc(s_plo, 1)

            for n in range(N_U + EARLY, N_U + LAG):
                w_lo(n % 4, n)
            own.did(V.memset(yacc[:], 0.0)); own.settle()
            for n in range(N_U + LAG, N_U + LAG + GB):
                w_lo(n % 4, n)
            v_lo(0, 0)
            v_lo(1, 1)
            dve.wait_ge(s_wev, N_U + GB)
            p_mul(0, 0)
            p_lo(0, 0)

            def add_y(n):
                for u in range(4):
                    dve.wait_ge(s_vmm, n * 4 + (u + 1))
                    y_ = yacc[:, u * 512:(u + 1) * 512]
                    if not isinstance(n, int) or n:
                        dve.wait_ge(s_yadd, n * 4 + (u - 3))
                    V.tensor_tensor(y_, y_, ps_y1[u % 2], ALU.add).then_inc(s_yadd, 1)

            def ahead(g, i, u_next=True, v_next=True):
                n = i * 2 + g
                if u_next:
                    for j in range(GB):
                        k = N_U + LAG + GB + g * GB + j
                        w_lo(k % 4, i * (2 * GB) + k)
                if v_next:
                    p_mul(1 - g, n + 1)
                    for j in range(GB):
                        k = (g + 1) * GB + j
                        v_lo(k % 4, i * (2 * GB) + k)
                    p_lo(1 - g, n + 1)
                add_y(n)

            loops = (NB - LAG) // (2 * GB)
            ahead(0, 0)
            ahead(1, 0)
            with dve.Fori(1, loops - 1) as i:
                for g in range(2):
                    ahead(g, i)
            ahead(0, loops - 1)
            ahead(1, loops - 1, u_next=False)
            def v_next(g, n, m):
                p_mul(g, n)
                for j in range(GB):
                    v_lo(g * GB + j, m * GB + j)
                p_lo(g, n)
                add_y(n - 1)

            def w_next(g, n, m):
                p_mul(g, n)
                for j in range(GB):
                    w_lo((N_U + NB + g * GB + j) % 4, m + j)
                p_lo(g, n)
                add_y(n - 1)

            with dve.Fori(0, TAILS - 1) as i:
                v_next(1, i * 4 + (V_TAIL - 1), i * 2 + (V_TAIL - 1))
                for g in range(2):
                    w_next(g, i * 4 + (V_TAIL + g), i * 4 + (N_U + NB + g * GB))
                v_next(0, i * 4 + (V_TAIL + 2), i * 2 + V_TAIL)
            v_next(1, NV - 3, V_TAIL - 1 + 2 * (TAILS - 1))
            for g in range(2):
                w_next(g, NV - 2 + g, N_U + NB + 4 * (TAILS - 1) + g * GB)
            add_y(NV - 1)
            dve.wait_ge(s_back, 16)
            for kk in range(KD):
                dve.wait_ge(s_yt, kk + 1)
                V.scalar_tensor_tensor(res2[:, kk, :], banks(kk % 4, T), modv[:, 5, kk:kk + 1], res2[:, kk, :], ALU.mult,
                                       ALU.add).then_inc(s_x2, 1)
            mean_root([(banks(7, T), D)], 4 + 2 * KD, 4)
            for kk in range(KD):
                V.scalar_tensor_tensor(res2[:, kk, :], res2[:, kk, :], pcol("final_norm", kk, 1), rstd[:, 0, :],
                                       ALU.mult, ALU.mult).then_inc(s_o, 1)

        @block.gpsimd
        def _(pool):
            def load_mod(j, n, i, k):
                if not (isinstance(n, int) and n < M_G1 + M_RING):
                    pool.wait_ge(s_modacc, n - M_RING + 1)
                pool.dma_start(mod_ring[:, k % 2], wmod[bass.ds(n, 1)].rearrange("o p n -> (o p) n")).then_inc(s_m[k % 2], 16)

            pool.wait_ge(s_relrow, 1)
            pool.dma_start(rel_dram.rearrange("h (p e) -> p h e", p=P), rel_rows[:]).then_inc(s_reld, 16)
            pool.wait_ge(s_reld, 16)
            pool.dma_start(relbias[:], rel_dram[:, P - 1:P - 1 + P * (N_SHIFT - 1)].rearrange(
                "h (p e) -> p h e", p=P)[:, :, 0:T]).then_inc(s_relt, 16)

            def chunk_lo(j, n, i, k):
                for half in range(2):
                    kk = slice(half * (KD // 2), (half + 1) * (KD // 2))
                    pool.wait_ge(s_chi, n * 2 + (half + 1))
                    nc.gpsimd.tensor_tensor(wlo[:, j, kk], wraw[:, j, kk], chi[:, k % 2, kk].bitcast(F32),
                                            ALU.subtract).then_inc(s_clo, 1)

            stretch(pool, 0, (N_U + EARLY) // 4 * 4, chunk_lo)
            stretch(pool, (N_U + EARLY) // 4 * 4, N_U + EARLY, chunk_lo)
            pool.wait_ge(s_spill, 16)
            pool.wait_ge(s_vmm, (NV - 2) * 4)
            pool.dma_start(res2[:], res_dram).then_inc(s_back, 16)
            for q in range(4):
                pool.wait_ge(s_o, 4 * q + 4)
                pool.dma_start(out[:, 4 * q:4 * q + 4], res2[:, 4 * q:4 * q + 4]).then_inc(s_st, 16)
            pool.wait_ge(s_st, 64)


def t5_bucket(dist):
    exact = BUCKETS // 2
    large = exact + (np.log(np.maximum(dist, 1) / exact) / np.log(MAX_DIST / exact) * (BUCKETS - exact)).astype(np.int32)
    return np.where(dist < exact, dist, np.minimum(large, BUCKETS - 1))


def constants():
    p = np.arange(P)[:, None]
    cst = np.zeros((P, N_CST + N_MIX), np.float32)

    def put(name, value):
        a, w = CST[name] if name in CST else (N_CST + MIX[name][0], MIX[name][1])
        cst[:, a:a + w] = value

    put("ident", np.eye(P))
    put("iota", np.arange(P)[None, :])
    put("after", p > np.arange(P)[None, :])
    put("strict", p < np.arange(T)[None, :])
    dist = p + P - np.arange(T)[None, :]
    times = sum(((dist >= 0) & (dist % d == 0) & (dist <= w)).astype(np.float32) for w, d in PATTERNS)
    put("times", times)
    put("bar", np.where(times > 0, 0.0, NEG_INF))
    dist = T - 1 - np.arange(N_SHIFT)
    shifts = ((t5_bucket(np.maximum(dist, 0))[None, :] == np.arange(BUCKETS)[:, None]) & (dist >= 0)[None, :])
    return cst[:, :N_CST], cst[:, N_CST:], shifts.astype(np.float32)


def kernel(x, c, w_mod, b_mod, norm_mix, norm_ffn, w_in, conv_w, conv_b, lru_w_rec, lru_b_rec, lru_w_in, lru_b_in,
           lru_lambda, rel_bias, gnorm_lru, gnorm_swa, gnorm_sb, w_out, peer_wq, peer_subkeys, peer_u, peer_v,
           final_norm):
    import concourse.bacc as bacc
    from concourse.bass_utils import run_bass_kernel_spmd

    A = np.asarray

    def cols(v):
        return A(v).reshape(-1, P).T

    par = np.concatenate([cols(c), cols(norm_mix), cols(norm_ffn), cols(final_norm), cols(b_mod), cols(conv_w),
                          cols(conv_b), cols(lru_b_rec), cols(lru_b_in), cols(lru_lambda), cols(gnorm_lru),
                          cols(gnorm_swa), cols(gnorm_sb)], axis=1)
    cst, mixc, shifts = constants()

    def chunks(w):
        return A(w).reshape(KD, P, -1, P).transpose(2, 1, 0, 3)

    u_blocks = A(peer_u)[0].reshape(P, NB, KD, P).transpose(1, 3, 2, 0)
    order = [*range(0, 6), *range(30, 42), *range(12, 30), *range(6, 12)]
    wst = np.concatenate([chunks(A(w_in)[0])[order], chunks(A(w_out)[0]), chunks(A(peer_wq)[0]), u_blocks], axis=0)
    wm = A(w_mod)[0].reshape(KD, P, 6, D).transpose(0, 2, 1, 3)
    wmod = np.concatenate([wm[:, parts].reshape(-1, P, D) for parts in ([1], [0], [2], [3], [4], [5])], axis=0)
    arrays = {
        "xT": A(x)[0].T.reshape(KD, P, T).transpose(1, 0, 2),
        "par": par,
        "cst": cst,
        "mixc": mixc,
        "shifts": shifts,
        "relb": A(rel_bias),
        "wmod": wmod,
        "wst": wst,
        "lruw": np.stack([A(lru_w_rec)[0], A(lru_w_in)[0]]).transpose(2, 0, 1, 3),
        "subk": A(peer_subkeys)[0].reshape(HC, P, P).transpose(2, 0, 1),
        "vtab": A(peer_v)[0].reshape(P, NB, D).transpose(1, 0, 2),
    }
    arrays = {k: np.ascontiguousarray(v) for k, v in arrays.items()}
    nc = bacc.Bacc("TRN2", target_bir_lowering=False, num_devices=1, dynamic_dma_scratch_size=4096)
    aps = {k: nc.dram_tensor(k, v.shape, mybir.dt.from_np(v.dtype), kind="ExternalInput").ap() for k, v in arrays.items()}
    gates = nc.dram_tensor("gates_dram", (TQ, P, NB, TW), F32, kind="Internal").ap()
    rel = nc.dram_tensor("rel_dram", (SWA_H, P * N_SHIFT), F32, kind="Internal").ap()
    kept = nc.dram_tensor("x1_dram", (P, KD, T), F32, kind="Internal").ap()
    out = nc.dram_tensor("out", (P, KD, T), F32, kind="ExternalOutput").ap()
    hybrid_block(nc, **aps, rel_dram=rel, gates_dram=gates, res_dram=kept, out=out)
    r = run_bass_kernel_spmd(nc, [arrays], core_ids=[0])
    y = r.results[0]["out"]
    return y.transpose(1, 0, 2).reshape(D, T).T.reshape(1, T, D)
```
